# Optimizing a Trainium2 kernel written in Bass

```python
import jax, jax.numpy as jnp
from jax import lax
import numpy as np

D_MODEL = 1024
BATCH = 1
SEQ = 256
DEPTH = 2

N_Q_HEADS = 8
N_KV_HEADS = 2
GQA_GROUP = N_Q_HEADS // N_KV_HEADS
HEAD_DIM = 64
WINDOW = 128
WIN_BLOCK = 128
ROPE_THETA = 10000.0
MASK_VALUE = -1e30
HGRN_HEADS = 4
HGRN_KEY_DIM = 128
HGRN_VAL_DIM = 128
HGRN_CHUNK = 16
LOGF_MIN = -4.0
LB_FLOOR = 1e-30
N_GROUPS = 4
EXPERTS_PER_GROUP = 8
N_EXPERTS = N_GROUPS * EXPERTS_PER_GROUP
TOP_K = 2
D_EXPERT = 512
MOE_BLOCK = 128
NORM_EPS = 1e-6

ATTN_Q_W = N_Q_HEADS * HEAD_DIM
ATTN_KV_W = N_KV_HEADS * HEAD_DIM
HGRN_F_W = HGRN_HEADS * HGRN_KEY_DIM
HGRN_V_W = HGRN_HEADS * HGRN_VAL_DIM
SPLIT_SIZES = (ATTN_Q_W, ATTN_KV_W, ATTN_KV_W,
               HGRN_F_W, HGRN_F_W, HGRN_F_W, HGRN_V_W, HGRN_V_W,
               D_MODEL, D_MODEL)
IN_WIDTH = sum(SPLIT_SIZES)

kernel_name = "hybrid_swa_hgrn2_hmoe_encoder"

def _rmsnorm(x, g):
    x32 = x.astype(jnp.float32)
    y = x32 * lax.rsqrt(jnp.mean(x32 * x32, axis=-1, keepdims=True) + NORM_EPS)
    return (y * g.astype(jnp.float32)).astype(x.dtype)

def _rope(t, pos):
    half = t.shape[-1] // 2
    inv = ROPE_THETA ** (-jnp.arange(half, dtype=jnp.float32) / half)
    ang = pos.astype(jnp.float32)[:, None] * inv[None, :]
    cos = jnp.cos(ang)[None, :, None, :]
    sin = jnp.sin(ang)[None, :, None, :]
    t1, t2 = t[..., :half], t[..., half:]
    return jnp.concatenate([t1 * cos - t2 * sin, t2 * cos + t1 * sin], axis=-1)

def _window_attention(q, k, v, sink):
    B, L = q.shape[0], q.shape[1]
    nb = L // WIN_BLOCK
    q = q.reshape(B, nb, WIN_BLOCK, N_KV_HEADS, GQA_GROUP, HEAD_DIM)

    def band(t):
        tp = jnp.pad(t, ((0, 0), (WIN_BLOCK, WIN_BLOCK), (0, 0), (0, 0)))
        tb = tp.reshape(B, nb + 2, WIN_BLOCK, N_KV_HEADS, HEAD_DIM)
        return jnp.concatenate([tb[:, :-2], tb[:, 1:-1], tb[:, 2:]], axis=2)

    kw, vw = band(k), band(v)
    s = jnp.einsum('bnqkgd,bnskd->bnkgqs', q, kw) * (HEAD_DIM ** -0.5)
    blk = jnp.arange(nb)
    qpos = blk[:, None] * WIN_BLOCK + jnp.arange(WIN_BLOCK)[None, :]
    kpos = (blk[:, None] - 1) * WIN_BLOCK + jnp.arange(3 * WIN_BLOCK)[None, :]
    valid = ((jnp.abs(qpos[:, :, None] - kpos[:, None, :]) <= WINDOW)
             & (kpos >= 0)[:, None, :] & (kpos < L)[:, None, :])
    s = jnp.where(valid[None, :, None, None], s, MASK_VALUE)
    sink_b = sink.reshape(N_KV_HEADS, GQA_GROUP)[None, None, :, :, None, None]
    m = jnp.maximum(jnp.max(s, axis=-1, keepdims=True), sink_b)
    p = jnp.exp(s - m)
    denom = jnp.sum(p, axis=-1, keepdims=True) + jnp.exp(sink_b - m)
    o = jnp.einsum('bnkgqs,bnskd->bnqkgd', p / denom, vw)
    return o.reshape(B, L, ATTN_Q_W)

def _gla_chunkwise(q, k, v, logf):
    B, H, L, DK = q.shape
    DV = v.shape[-1]
    n = L // HGRN_CHUNK
    q, k, logf = [t.reshape(B, H, n, HGRN_CHUNK, DK) for t in (q, k, logf)]
    v = v.reshape(B, H, n, HGRN_CHUNK, DV)
    b = jnp.cumsum(logf, axis=3)
    b_last = b[:, :, :, -1:, :]
    qe = q * jnp.exp(b)
    a = jnp.einsum('bhncd,bhnsd->bhncs', qe, k * jnp.exp(-b))
    tril = jnp.tril(jnp.ones((HGRN_CHUNK, HGRN_CHUNK), dtype=bool))
    a = jnp.where(tril, a, 0.0)
    o = jnp.einsum('bhncs,bhnse->bhnce', a, v)
    kv = jnp.einsum('bhncd,bhnce->bhnde', k * jnp.exp(b_last - b), v)
    decay = jnp.exp(b_last[:, :, :, 0, :])

    def step(S, inp):
        d, u = inp
        return d[..., None] * S + u, S

    _, s_prev = lax.scan(step, jnp.zeros((B, H, DK, DV), jnp.float32),
                         (jnp.moveaxis(decay, 2, 0), jnp.moveaxis(kv, 2, 0)))
    o = o + jnp.einsum('bhncd,nbhde->bhnce', qe, s_prev)
    return o.reshape(B, H, L, DV)

def _hgrn2(qb, zf, zb, ib, ogb, lb, norm_g):
    B, L = qb.shape[0], qb.shape[1]

    def heads(t):
        return t.astype(jnp.float32).reshape(B, L, HGRN_HEADS, -1).transpose(0, 2, 1, 3)

    q = jax.nn.silu(heads(qb))
    v = heads(ib)

    def direction(z, lbd, reverse):
        lbd = lbd.astype(jnp.float32).reshape(1, HGRN_HEADS, 1, HGRN_KEY_DIM)
        logf = jnp.logaddexp(jnp.log(jnp.maximum(lbd, LB_FLOOR)),
                             jnp.log1p(-lbd) + jax.nn.log_sigmoid(heads(z)))
        logf = jnp.maximum(logf, LOGF_MIN)
        k = -jnp.expm1(logf)
        if reverse:
            fl = lambda t: jnp.flip(t, axis=2)
            return fl(_gla_chunkwise(fl(q), fl(k), fl(v), fl(logf)))
        return _gla_chunkwise(q, k, v, logf)

    o = direction(zf, lb[0], False) + direction(zb, lb[1], True)
    o = o.transpose(0, 2, 1, 3).reshape(B, L, HGRN_V_W)
    o = o * lax.rsqrt(jnp.mean(o * o, axis=-1, keepdims=True) + NORM_EPS) * norm_g.astype(jnp.float32)
    return o * jax.nn.silu(ogb.astype(jnp.float32))

def _mixer(h, w_in, sink, lb, hgrn_g, w_up_attn, w_up_hgrn, w_out):
    B, L, _ = h.shape
    proj = h @ w_in
    points = np.cumsum(SPLIT_SIZES)[:-1].tolist()
    qa, ka, va, qb, zf, zb, ib, ogb, ga, gb = jnp.split(proj, points, axis=-1)
    pos = jnp.arange(L)
    qa = _rope(qa.reshape(B, L, N_Q_HEADS, HEAD_DIM).astype(jnp.float32), pos)
    ka = _rope(ka.reshape(B, L, N_KV_HEADS, HEAD_DIM).astype(jnp.float32), pos)
    va = va.reshape(B, L, N_KV_HEADS, HEAD_DIM).astype(jnp.float32)
    y_attn = _window_attention(qa, ka, va, sink.astype(jnp.float32)).astype(h.dtype)
    y_hgrn = _hgrn2(qb, zf, zb, ib, ogb, lb, hgrn_g).astype(h.dtype)
    merged = (jax.nn.sigmoid(ga) * (y_attn @ w_up_attn)
              + jax.nn.sigmoid(gb) * (y_hgrn @ w_up_hgrn))
    return merged @ w_out

def _hier_moe(xf, w_rg, b_rg, w_re, b_re, w_gate, w_up, w_down):
    T, D = xf.shape
    p_g = jax.nn.softmax((xf @ w_rg).astype(jnp.float32) + b_rg.astype(jnp.float32), axis=-1)
    p_top, g_top = lax.top_k(p_g, 1)
    logits_e = jnp.einsum('td,gde->tge', xf, w_re).astype(jnp.float32) + b_re.astype(jnp.float32)
    logits_e = jnp.take_along_axis(logits_e, g_top[:, :, None], axis=1)[:, 0]
    w_top, e_top = lax.top_k(jax.nn.softmax(logits_e, axis=-1), TOP_K)
    w_top = w_top / jnp.sum(w_top, axis=-1, keepdims=True)
    weights = (p_top * w_top).reshape(-1)
    experts = (g_top * EXPERTS_PER_GROUP + e_top).reshape(-1).astype(jnp.int32)
    tokens = jnp.repeat(jnp.arange(T, dtype=jnp.int32), TOP_K)

    n_slots = T * TOP_K
    order = jnp.argsort(experts)
    e_s, t_s, w_s = experts[order], tokens[order], weights[order]
    counts = jnp.bincount(experts, length=N_EXPERTS)
    start = jnp.cumsum(counts) - counts
    padded = (counts + MOE_BLOCK - 1) // MOE_BLOCK * MOE_BLOCK
    pend = jnp.cumsum(padded)
    pstart = pend - padded
    dest = pstart[e_s] + (jnp.arange(n_slots) - start[e_s])
    n_pad = n_slots + N_EXPERTS * MOE_BLOCK
    n_blocks = n_pad // MOE_BLOCK
    slot_token = jnp.full((n_pad,), T, jnp.int32).at[dest].set(t_s)
    slot_weight = jnp.zeros((n_pad,), xf.dtype).at[dest].set(w_s.astype(xf.dtype))
    block_expert = jnp.minimum(
        jnp.searchsorted(pend, jnp.arange(n_blocks) * MOE_BLOCK, side='right'), N_EXPERTS - 1)
    x_pad = jnp.concatenate([xf, jnp.zeros((1, D), xf.dtype)], axis=0)

    def block_fn(args):
        e, idx = args
        hb = x_pad[idx]
        return (jax.nn.silu(hb @ w_gate[e]) * (hb @ w_up[e])) @ w_down[e]

    y = lax.map(block_fn, (block_expert, slot_token.reshape(n_blocks, MOE_BLOCK)))
    y = y.reshape(n_pad, D) * slot_weight[:, None]
    return jax.ops.segment_sum(y, slot_token, num_segments=T + 1)[:T]

def setup_inputs(seed: int = 0) -> dict:
    key = jax.random.key(seed)
    ks = jax.random.split(key, 18)
    f32 = jnp.float32
    nrm = lambda k, shape, scale: jax.random.normal(k, shape, f32) * scale
    return {
        "x": nrm(ks[0], (BATCH, SEQ, D_MODEL), 1.0),
        "attn_norm_g": 1.0 + nrm(ks[1], (DEPTH, D_MODEL), 0.02),
        "w_in": nrm(ks[2], (DEPTH, D_MODEL, IN_WIDTH), D_MODEL ** -0.5),
        "sink_logits": nrm(ks[3], (DEPTH, N_Q_HEADS), 0.5),
        "hgrn_lb_table": nrm(ks[4], (DEPTH, 2, HGRN_F_W), 0.5),
        "hgrn_norm_g": 1.0 + nrm(ks[5], (DEPTH, HGRN_V_W), 0.02),
        "w_up_attn": nrm(ks[6], (DEPTH, ATTN_Q_W, D_MODEL), ATTN_Q_W ** -0.5),
        "w_up_hgrn": nrm(ks[7], (DEPTH, HGRN_V_W, D_MODEL), HGRN_V_W ** -0.5),
        "w_out": nrm(ks[8], (DEPTH, D_MODEL, D_MODEL), D_MODEL ** -0.5),
        "ffn_norm_g": 1.0 + nrm(ks[9], (DEPTH, D_MODEL), 0.02),
        "w_router_group": nrm(ks[10], (DEPTH, D_MODEL, N_GROUPS), D_MODEL ** -0.5),
        "b_router_group": nrm(ks[11], (DEPTH, N_GROUPS), 0.01),
        "w_router_expert": nrm(ks[12], (DEPTH, N_GROUPS, D_MODEL, EXPERTS_PER_GROUP), D_MODEL ** -0.5),
        "b_router_expert": nrm(ks[13], (DEPTH, N_GROUPS, EXPERTS_PER_GROUP), 0.01),
        "w_expert_gate": nrm(ks[14], (DEPTH, N_EXPERTS, D_MODEL, D_EXPERT), D_MODEL ** -0.5),
        "w_expert_up": nrm(ks[15], (DEPTH, N_EXPERTS, D_MODEL, D_EXPERT), D_MODEL ** -0.5),
        "w_expert_down": nrm(ks[16], (DEPTH, N_EXPERTS, D_EXPERT, D_MODEL), D_EXPERT ** -0.5),
        "final_norm_g": 1.0 + nrm(ks[17], (D_MODEL,), 0.02),
    }

def reference(x, attn_norm_g, w_in, sink_logits, hgrn_lb_table, hgrn_norm_g, w_up_attn,
              w_up_hgrn, w_out, ffn_norm_g, w_router_group, b_router_group, w_router_expert,
              b_router_expert, w_expert_gate, w_expert_up, w_expert_down, final_norm_g):
    B, L, D = x.shape
    sm = jax.nn.softmax(hgrn_lb_table.astype(jnp.float32), axis=0)
    lower_bounds = jnp.cumsum(sm, axis=0) - sm[:1]
    for l in range(DEPTH):
        h = _rmsnorm(x, attn_norm_g[l])
        x = x + _mixer(h, w_in[l], sink_logits[l], lower_bounds[l], hgrn_norm_g[l],
                       w_up_attn[l], w_up_hgrn[l], w_out[l])
        h = _rmsnorm(x, ffn_norm_g[l])
        y = _hier_moe(h.reshape(B * L, D), w_router_group[l], b_router_group[l],
                      w_router_expert[l], b_router_expert[l], w_expert_gate[l],
                      w_expert_up[l], w_expert_down[l])
        x = x + y.reshape(B, L, D).astype(x.dtype)
    return _rmsnorm(x, final_norm_g)


_drawn_inputs = setup_inputs


def setup_inputs(seed=0):
    import zlib

    import numpy as np

    out = dict(_drawn_inputs(seed))
    spreads = {}
    factors = {'sink_logits': 8.0,
     'hgrn_norm_g': 3.063,
     'b_router_expert': 4.183,
     'final_norm_g': 8.206,
     'b_router_group': 2.853}
    for name, (base, spread) in spreads.items():
        noise = np.random.default_rng([zlib.crc32(name.encode()), seed]).standard_normal(out[name].shape)
        drawn = base * np.exp(spread * noise) if base else spread * noise
        out[name] = __import__('jax').numpy.asarray(drawn.astype(out[name].dtype))
    for name, factor in factors.items():
        out[name] = (out[name] * factor).astype(out[name].dtype)
    return out
```

```python
from contextlib import ExitStack

import numpy as np

import concourse.bass as bass
from concourse import mybir

F32 = mybir.dt.float32
I32 = mybir.dt.int32
ALU = mybir.AluOpType
ACT = mybir.ActivationFunctionType
AX_X = mybir.AxisListType.X

P = 128
DEPTH, D, S = 2, 1024, 256
IN_W = 5376
NT = S // P
KC = D // P
HEADS, KVH, HD = 8, 2, 64
HH, HK = 4, 128
HW = HH * HK
CHUNK = 16
NCH = P // CHUNK
GROUPS, EPG = 4, 8
NE = GROUPS * EPG
FE = 512
SLOTS = 32
MAX_OVER = (2 * S) // (SLOTS + 1)
EPS = 1e-6
LOGF_MIN = -4.0
NEG = -1e30

SLOT_W = 4096
RING = 6
UNITS = IN_W // 256
W_IN_LOADS = (IN_W + 511) // 512
WUH_PARTS, WO_PARTS = 2, 4
MIX_LOADS = W_IN_LOADS + 1 + WUH_PARTS + WO_PARTS
LOADS = MIX_LOADS + 3 * NE
ROUNDS = LOADS // RING
assert LOADS % RING == 0 and MIX_LOADS % RING == 0 and RING == 6

CONST = {}
_at = 0
for _name, _n in [("ident", P), ("before", P), ("ones", P), ("win0", P), ("win1", P), ("cos", NT * 32),
                  ("sin", NT * 32), ("tri_f", P), ("tri_b", P), ("iota", SLOTS), ("limits", 7), ("falling", 8),
                  ("over_at", MAX_OVER), ("first_row", NE)]:
    CONST[_name] = (_at, _at + _n)
    _at += _n
CONST_W = _at


def constants():
    c = np.zeros((P, CONST_W), np.float32)

    def put(name, v):
        a, b = CONST[name]
        c[:, a:b] = np.asarray(v, np.float32).reshape(-1, b - a)

    i = np.arange(P)
    put("ident", np.eye(P))
    put("before", i[:, None] < i[None, :])
    put("ones", np.ones((P, P)))
    put("win0", np.where(i[None, :] <= i[:, None], 0.0, NEG))
    put("win1", np.where(i[None, :] >= i[:, None], 0.0, NEG))
    half = HD // 2
    inv = np.float32(10000.0) ** (-np.arange(half, dtype=np.float32) / np.float32(half))
    angle = np.arange(S, dtype=np.float32)[:, None] * inv[None, :].astype(np.float32)
    for name, f in (("cos", np.cos), ("sin", np.sin)):
        put(name, f(angle).astype(np.float32).reshape(NT, P, half).transpose(1, 0, 2).reshape(P, -1))
    put("tri_f", i[:, None] <= i[None, :])
    put("tri_b", i[:, None] >= i[None, :])
    put("iota", np.arange(SLOTS)[None])
    put("limits", (SLOTS * np.arange(1, 8))[None])
    put("falling", np.arange(8, 0, -1)[None])
    put("over_at", np.arange(MAX_OVER)[None])
    put("first_row", (SLOTS * np.arange(NE))[None])
    return c


def layers_program(nc, t):
    ctx = ExitStack()
    with ctx:
        def sb(name, shape, dt=F32):
            return ctx.enter_context(nc.sbuf_tensor(name, shape, dt))

        def sem(name):
            return ctx.enter_context(nc.semaphore(name))

        ring = sb("ring", [P, RING, SLOT_W])
        const = sb("const", [P, CONST_W])
        x = sb("x", [P, NT, D])
        xn = sb("xn", [P, NT, D])
        hT = sb("hT", [P, KC, S])
        gate = sb("gate", [P, 16, S])
        qT = sb("qT", [P, NT, 4, P])
        kT = sb("kT", [P, NT, KVH, P])
        vv = sb("vv", [P, NT, P])
        yaT = sb("yaT", [P, 4, S])
        qd = sb("qd", [P, HH, S])
        kd = sb("kd", [P, 2, HH, S])
        bd = sb("bd", [P, 2, HH * NT, P + 1])
        ft = sb("ft", [P, 2, 512])
        hv = sb("hv", [P, NT, HW])
        og = sb("og", [P, NT, HW])
        qc = sb("qc", [P, 2, HH, P])
        ek = sb("ek", [P, 2, NCH, P])
        at_sb = sb("at_sb", [P, 2, 2, P])
        junk = sb("junk", [P, 512])
        small = sb("small", [P, 256])
        gains = sb("gains", [P, 2 * DEPTH, KC])
        rows = sb("rows", [24, P])
        cols = sb("cols", [P, 24])
        lbs = sb("lbs", [P, 2, DEPTH, 8])
        sink = sb("sink", [P, DEPTH, HEADS])
        wr = sb("wr", [P, KC, GROUPS + NE])
        bias = sb("bias", [P, DEPTH, GROUPS + NE])
        ctl = sb("ctl", [1, 1 + MAX_OVER], I32)
        rowi = sb("rowi", [P, 2, NT], I32)

        def C(name):
            a, b = CONST[name]
            return const[:, a:b]

        ident = C("ident")
        cos = C("cos").rearrange("p (t f) -> p t f", t=NT)
        sin = C("sin").rearrange("p (t f) -> p t f", t=NT)

        flat = gate[:, :, :].rearrange("p a b -> p (a b)")
        raw = flat[:, 0:1280].rearrange("p (t n) -> p t n", t=NT)
        rot = flat[:, 1280:2560].rearrange("p (a n) -> p a n", a=2)
        roped = flat[:, 2560:4096].rearrange("p (t n) -> p t n", t=NT)
        prob = flat[:, 0:2048].rearrange("p (g h s) -> p g h s", g=2, h=4)
        probT = flat[:, 2560:3584].rearrange("p (j n) -> p j n", j=NT)
        qe = xn[:, :, :].rearrange("p r (h c u) -> p r h c u", h=HH * NT, u=CHUNK)
        kend = ek[:, 0, :, :]
        kendT = ek[:, 1, :, :]
        logf = ek[:, 1, 0:4, :].rearrange("p a b -> p (a b)")
        state = ft[:, :, :].rearrange("p r (h e) -> p r h e", h=HH)
        yhT = qd
        merged = hT
        kflat = kd[:, :, :, :].rearrange("p r h s -> p (r h s)")
        hs = kflat[:, 0:512].rearrange("p (b c s) -> p b c s", b=2, c=KC)
        sel = kflat[:, 512:640].rearrange("p (b t s) -> p b t s", b=2, t=NT)
        eg = kflat[:, 640:1152].rearrange("p (b s) -> p b s", b=2)
        up = kflat[:, 1152:1664].rearrange("p (b s) -> p b s", b=2)
        hid = ft[:, 0, :].rearrange("p (b s) -> p b s", b=2)
        hidT = ft[:, 1, 0:256].rearrange("p (b j s) -> p b j s", b=2, j=2)
        ysb = junk[:, :].rearrange("p (b s) -> p b s", b=2)
        got = gate[:, :, :].rearrange("p a b -> p (a b)").rearrange("p (k t n) -> p k t n", k=2, t=NT)
        fin_g = kflat[:, 0:D]

        hvf = hv[:, :, :].rearrange("p t n -> p (t n)")
        ogf = og[:, :, :].rearrange("p t n -> p (t n)")

        def cut(flat_ap, at, *shape):
            n = int(np.prod(shape))
            v = flat_ap[:, at:at + n]
            if len(shape) == 2:
                v = v.rearrange("p (a b) -> p a b", a=shape[0])
            return v

        lg = cut(hvf, 0, NT, GROUPS + NE)
        lsel = cut(hvf, 72, NT, EPG)
        m1h = hvf[:, 96:160].rearrange("p (t g e) -> p t g e", t=NT, g=GROUPS)
        m2h = hvf[:, 160:224].rearrange("p (t g e) -> p t g e", t=NT, g=GROUPS)
        mh = cut(hvf, 224, NT, NE)
        tmp = hvf[:, 288:352].rearrange("p (t g e) -> p t g e", t=NT, g=GROUPS)
        pos = cut(hvf, 352, NT, NE)
        posm = cut(hvf, 416, NT, NE)
        count = cut(hvf, 480, NE)
        novb = cut(hvf, 512, NE)
        oend = cut(hvf, 544, NE)
        rbase = cut(hvf, 576, NE)
        ctlf = cut(hvf, 608, 1 + MAX_OVER)
        ooff = cut(hvf, 632, MAX_OVER)
        rowf = cut(hvf, 656, 2, NT)
        ohg = cut(hvf, 664, NT, GROUPS)
        oh1 = cut(hvf, 672, NT, EPG)
        oh2 = cut(hvf, 688, NT, EPG)
        cand = cut(hvf, 704, NT, EPG)
        lsel2 = cut(hvf, 720, NT, EPG)
        eqs = cut(hvf, 736, NT, EPG)
        grid = cut(ogf, 0, MAX_OVER, NE)
        grid2 = cut(ogf, 512, NE, 7)

        def sm(at, n=NT):
            return small[:, at:at + n]

        ss, rs0, rstd, rs1, rs2 = sm(0), sm(2), sm(4), sm(6), sm(28)
        gmax, psum_g, cmax, ptop, m1, m2, w1, w2, e2, den2 = (sm(8 + 2 * i) for i in range(10))
        amax, am, anm, adif, aexp, asum, aden = (small[:, 64 + 8 * i:64 + 8 * i + 8].rearrange("p (g h) -> p g h", g=2)
                                                 for i in range(7))

        def bank(name):
            return ctx.enter_context(nc.psum_tensor(name, [P, 512], F32))

        UB = [bank("unit0"), bank("unit1")]
        SB = [bank("score0"), bank("score1")]
        TB = [bank("turn0"), bank("turn1")]
        OB = [bank("out0"), bank("out1")]

        landed = [sem(f"landed{i}") for i in range(RING)]
        s_const, s_x, s_wr, s_fin, s_out = (sem(n) for n in ("const_in", "x_in", "router_in", "final_in", "out_done"))
        PEV = {}
        for n, per in (("turned", 8), ("unit_mm", UNITS), ("qk_turned", 3), ("score_mm", 4), ("prob_turned", 4),
                       ("pv_mm", 4), ("kend_turned", 2), ("state_mm", 2), ("at_mm", 8), ("o_mm", 8),
                       ("y_turned", 2), ("ua_mm", 4), ("uh_mm", 4), ("wout_mm", WO_PARTS), ("logit_mm", 1), ("pos_mm", 1),
                       ("gather_mm", NE), ("gu_mm", NE), ("hid_turned", NE), ("down_mm", NE),
                       ("unit_seen", UNITS), ("squares", 2), ("prob_exp", 4), ("f_log", 4), ("kend_exp", 1),
                       ("kendT_in", 2), ("state_in", 2), ("ek_exp", 16), ("qe_exp", 2), ("qc_exp", 2), ("osq", 2), ("prob_out", 4),
                       ("gexp", 1), ("e2exp", 1), ("gu_seen", NE), ("hidT_in", NE), ("y_in", NE),
                       ("xn_in", 2), ("h_in", 8), ("roped_in", 1), ("qkT_in", 3), ("sunk", 4), ("prob_in", 4),
                       ("ya_in", 4), ("unit_done", 4), ("f_in", 4), ("b_in", 4), ("kend_in", 1), ("ek_in", 16),
                       ("qe_sub", 2), ("qe_in", 2), ("at_in", 8), ("osum_out", 2), ("y_ready", 2), ("yT_in", 2),
                       ("merged_in", 4), ("x_mixed", 1), ("x_done", 1), ("gsub", 1), ("e2sub", 1), ("mask_in", 1),
                       ("route_in", 1), ("sel_in", NE), ("hs_in", NE), ("hid_in", NE), ("gates_in", 1),
                       ("mean_in", 4), ("root_log", 4), ("root", 4)):
            PEV[n] = (sem(n), per)
        fetched = sem("fetched")
        y_out = [sem(f"y_out{i}") for i in range(2)]
        s_dve, s_pool, s_pre = sem("dve_step"), sem("pool_step"), sem("prepared")
        s_ov = [sem(f"over_dve_step{l}") for l in range(DEPTH)]
        s_lb, s_lbt, s_lbe = sem("lb_rows"), sem("lb_turned"), sem("lb_exp")
        OV = [{n: sem(f"over_{n}{l}") for n in ("landed", "sel", "gather", "hs", "gu", "seen", "hid", "turned",
                                                "hidT", "down", "y", "out", "y_free")} for l in range(DEPTH)]

        def inc(ins, name):
            ins.then_inc(PEV[name][0], 1)

        def wait(eng, name, l, k):
            s, per = PEV[name]
            eng.wait_ge(s, l * per + k)

        ybuf = nc.dram_tensor("ybuf", ((NE + MAX_OVER) * SLOTS, D), F32, kind="Internal").ap()
        w_in, w_ua, w_uh, w_o = t["w_in"], t["w_up_attn"], t["w_up_hgrn"], t["w_out"]

        def slot3(s, k, n):
            return ring[:, s, 0:k * n].rearrange("p (c n) -> p c n", c=k)

        def expert_loads(l, e, s0):
            wg, wu, wd = t["w_expert_gate"], t["w_expert_up"], t["w_expert_down"]
            yield 0, slot3(s0, KC, FE), wg[l, e, :, :].rearrange("(p c) f -> p c f", c=KC)
            yield 1, slot3(s0 + 1, KC, FE), wu[l, e, :, :].rearrange("(p c) f -> p c f", c=KC)
            yield 2, ring[:, s0 + 2, :].rearrange("p (h n) -> p h n", h=2), \
                wd[l, e, :, :].rearrange("(h p j) d -> p h (j d)", h=2, p=P)

        block = ctx.enter_context(nc.Block())

        @block.sync
        def _(sp):
            sp.dma_start(x[:], t["x"].rearrange("b (t p) d -> p (b t) d", p=P)).then_inc(s_x, 16)
            sp.dma_start(const[:], t["consts"]).then_inc(s_const, 16)
            sp.dma_start(gains[:, 0:DEPTH, :], t["attn_norm_g"].rearrange("l (p c) -> p l c", c=KC)).then_inc(s_const, 16)
            sp.dma_start(gains[:, DEPTH:, :], t["ffn_norm_g"].rearrange("l (p c) -> p l c", c=KC)).then_inc(s_const, 16)
            sp.dma_start(rows[0:16, :], t["hgrn_lb_table"].rearrange("l r (h p) -> (l r h) p", p=HK)).then_inc(s_const, 16)
            sp.dma_start(rows[16:24, :], t["hgrn_norm_g"].rearrange("l (h p) -> (l h) p", p=HK)).then_inc(s_const, 16)

            def spread(ap):
                return ap.rearrange("(o l) n -> o l n", o=1).broadcast_to([P, *ap.shape])

            sp.dma_start(sink[:], spread(t["sink_logits"])).then_inc(s_const, 16)
            sp.dma_start(bias[:, :, 0:GROUPS], spread(t["b_router_group"])).then_inc(s_const, 16)
            sp.dma_start(bias[:, :, GROUPS:], spread(t["b_router_expert"].rearrange("l g e -> l (g e)"))).then_inc(s_const, 16)

            def wait_used(l, n):
                if n < 0:
                    l, n = l - 1, n + LOADS
                if l < 0:
                    return
                if n < W_IN_LOADS:
                    wait(sp, "unit_mm", l, min(2 * n + 2, UNITS))
                elif n == W_IN_LOADS:
                    wait(sp, "ua_mm", l, 4)
                elif n <= W_IN_LOADS + WUH_PARTS:
                    wait(sp, "uh_mm", l, 4)
                elif n < MIX_LOADS:
                    wait(sp, "wout_mm", l, n - W_IN_LOADS - WUH_PARTS)
                else:
                    e, k = divmod(n - MIX_LOADS, 3)
                    wait(sp, "down_mm" if k == 2 else "gu_mm", l, e + 1)

            def load(l, n, dst, src):
                wait_used(l, n - RING)
                sp.dma_start(dst, src).then_inc(landed[n % RING], 16)

            for l in range(DEPTH):
                for i in range(W_IN_LOADS):
                    n = min(512, IN_W - 512 * i)
                    load(l, i, slot3(i % RING, KC, n),
                         w_in[l].rearrange("(p c) n -> p c n", c=KC)[:, :, 512 * i:512 * i + n])
                i = W_IN_LOADS
                load(l, i, slot3(i % RING, 4, D), w_ua[l].rearrange("(c p) n -> p c n", p=P))
                for j in range(WUH_PARTS):
                    i += 1
                    load(l, i, slot3(i % RING, 2, D), w_uh[l].rearrange("(c p) n -> p c n", p=P)[:, 2 * j:2 * j + 2, :])
                for j in range(WO_PARTS):
                    i += 1
                    load(l, i, slot3(i % RING, 2, D), w_o[l].rearrange("(c p) n -> p c n", p=P)[:, 2 * j:2 * j + 2, :])

                for e in range(2):
                    for k, d, src in expert_loads(l, e, 3 * e):
                        load(l, MIX_LOADS + 3 * e + k, d, src)
                with sp.Fori(1, NE // 2) as i:
                    for b in range(2):
                        for k, d, src in expert_loads(l, i * 2 + b, 3 * b):
                            wait(sp, "down_mm" if k == 2 else "gu_mm", l, i * 2 + b - 1)
                            sp.dma_start(d, src).then_inc(landed[3 * b + k], 16)

                wait(sp, "route_in", l, 1)
                over = sp.value_load(ctl[0:1, 0:1], min_val=0, max_val=MAX_OVER)
                with sp.Fori(0, MAX_OVER) as j:
                    with sp.If(j < over):
                        sp.wait_ge(OV[l]["down"], j + 1)
                        e = sp.value_load(ctl[0:1, bass.ds(j + 1, 1)], min_val=0, max_val=NE - 1)
                        for k, d, src in expert_loads(l, e, 0):
                            sp.dma_start(d, src).then_inc(OV[l]["landed"], 16)
                    with sp.Else():
                        sp.nop()
                sp.wait_ge(OV[l]["down"], over + 1)
            wait(sp, "xn_in", DEPTH, 1)
            sp.dma_start(t["out"].rearrange("b (t p) d -> p (b t) d", p=P), xn[:]).then_inc(s_out, 16)
            sp.wait_ge(s_out, 16)

        @block.tensor
        def _(pe):
            def arrived(l, n):
                pe.wait_ge(landed[n % RING], 16 * (l * ROUNDS + n // RING + 1))

            def turn(l, half):
                wait(pe, "xn_in", l, half + 1)
                for g in range(4):
                    tt, q = g // 2, g % 2
                    if g >= 2:
                        wait(pe, "h_in", l, 4 * half + g - 1)
                    for c in range(4):
                        m = pe.transpose(TB[g % 2][:, P * c:P * c + P], xn[:, tt, 4 * q + c::KC], ident)
                    inc(m, "turned")

            def unit(l, u):
                if u >= 2:
                    v = u - 2
                    if v in DVE_UNITS:
                        wait(pe, "unit_done", l, DVE_UNITS.index(v) + 1)
                    else:
                        wait(pe, "unit_seen", l, v + 1)
                if u == 0:
                    wait(pe, "h_in", l, 4)
                if u % 2 == 0:
                    arrived(l, u // 2)
                b = UB[u % 2]
                w = slot3((u // 2) % RING, KC, min(512, IN_W - 512 * (u // 2)))
                c0 = 256 * (u % 2)
                for a in range(2):
                    for c in range(KC):
                        if u in TOKEN_UNITS:
                            m = pe.matmul(b[:, 256 * a:256 * a + 256], hT[:, c, P * a:P * a + P], w[:, c, c0:c0 + 256],
                                          start=(c == 0), stop=(c == KC - 1))
                        else:
                            m = pe.matmul(b[:, 256 * a:256 * a + 256], w[:, c, c0 + P * a:c0 + P * a + P], hT[:, c, :],
                                          start=(c == 0), stop=(c == KC - 1))
                inc(m, "unit_mm")

            def qk_turn(l):
                wait(pe, "roped_in", l, 1)
                for tt in range(NT):
                    for c in range(4):
                        m = pe.transpose(TB[tt][:, P * c:P * c + P], roped[:, tt, P * c:P * c + P], ident)
                    inc(m, "qk_turned")
                wait(pe, "qkT_in", l, 1)
                for tt in range(NT):
                    for kv in range(KVH):
                        n = 2 * tt + kv
                        m = pe.transpose(TB[0][:, P * n:P * n + P], roped[:, tt, 512 + P * kv:512 + P * kv + P], ident)
                inc(m, "qk_turned")

            def scores(l, g):
                b, kv = g // 2, g % 2
                if g == 0:
                    wait(pe, "qkT_in", l, 3)
                else:
                    wait(pe, "prob_exp", l, g)
                for hh in range(2):
                    for par in range(2):
                        h0 = 64 * par
                        m = pe.matmul(SB[par][:, 256 * hh:256 * hh + 256], qT[h0:h0 + 64, b, 2 * kv + hh, :],
                                      kT[h0:h0 + 64, :, kv, :], start=True, stop=True)
                inc(m, "score_mm")

            def prob_turn(l, g):
                wait(pe, "prob_in", l, g + 1)
                if g >= 1:
                    wait(pe, "prob_out", l, g)
                for j in range(NT):
                    for n in range(4):
                        m = pe.transpose(TB[j][:, P * n:P * n + P], prob[:, g % 2, n, P * j:P * j + P], ident)
                inc(m, "prob_turned")

            def pv(l, g):
                wait(pe, "prob_out", l, g + 1)
                if g >= 2:
                    wait(pe, "ya_in", l, g - 1)
                kv = g % 2
                for par in range(2):
                    for j in range(NT):
                        m = pe.matmul(OB[g % 2][64 * par:64 * par + 64, 0:256], vv[:, j, 64 * kv:64 * kv + 64],
                                      probT[:, j, 256 * par:256 * par + 256], start=(j == 0), stop=(j == NT - 1))
                inc(m, "pv_mm")

            def kend_turn(l):
                wait(pe, "kend_in", l, 1)
                wait(pe, "prob_out", l, 4)
                for r in range(2):
                    for h in range(HH):
                        m = pe.transpose(TB[r][:, P * h:P * h + P], kend[:, 4 * r + h, :], ident)
                    inc(m, "kend_turned")

            def states(l):
                wait(pe, "unit_seen", l, 11)
                for r in range(2):
                    wait(pe, "kendT_in", l, r + 1)
                    for h in range(HH):
                        m = pe.matmul(TB[r][:, P * h:P * h + P], kendT[:, 4 * r + h, :], hv[:, r, P * h:P * h + P],
                                      start=True, stop=True)
                    inc(m, "state_mm")

            def intra(l, n):
                T, h = n // HH, n % HH
                if n >= 2:
                    wait(pe, "at_in", l, n - 1)
                for r in range(2):
                    wait(pe, "ek_in", l, 2 * n + r + 1)
                    if n == 0:
                        wait(pe, "qe_in", l, r + 1)
                    for i in range(NCH):
                        m = pe.matmul(SB[n % 2][:, P * r + CHUNK * i:P * r + CHUNK * i + CHUNK], ek[:, r, i, :],
                                      qe[:, r, NT * h + T, i, :], start=True, stop=True)
                inc(m, "at_mm")

            def outputs(l, n):
                T, h = n // HH, n % HH
                wait(pe, "at_in", l, n + 1)
                if n == 0:
                    wait(pe, "state_in", l, 2)
                    wait(pe, "ya_in", l, 4)
                o = OB[T][:, P * h:P * h + P]
                v = hv[:, T, P * h:P * h + P]
                pe.matmul(o, at_sb[:, n % 2, 0, :], v, start=True, stop=False)
                pe.matmul(o, at_sb[:, n % 2, 1, :], v, start=False, stop=False)
                r = 0 if T == 1 else 1
                inc(pe.matmul(o, qc[:, r, h, :], state[:, r, h, :], start=False, stop=True), "o_mm")

            def y_turn(l, T):
                wait(pe, "y_ready", l, T + 1)
                wait(pe, "state_in", l, T + 1)
                for c in range(4):
                    m = pe.transpose(TB[T][:, P * c:P * c + P], og[:, T, P * c:P * c + P], ident)
                inc(m, "y_turned")

            def up_attn(l, i):
                if i == 0:
                    arrived(l, W_IN_LOADS)
                wait(pe, "unit_seen", l, UNITS)
                if i >= 2:
                    wait(pe, "merged_in", l, i - 1)
                w = slot3(W_IN_LOADS % RING, 4, D)
                for a in range(2):
                    f = P * (2 * i + a)
                    for c in range(4):
                        m = pe.matmul(UB[i % 2][:, 256 * a:256 * a + 256], w[:, c, f:f + P], yaT[:, c, :],
                                      start=(c == 0), stop=(c == 3))
                inc(m, "ua_mm")

            def up_hgrn(l, i):
                if i == 0:
                    for j in range(WUH_PARTS):
                        arrived(l, W_IN_LOADS + 1 + j)
                    wait(pe, "yT_in", l, 2)
                if i >= 2:
                    wait(pe, "merged_in", l, i - 1)
                for a in range(2):
                    f = P * (2 * i + a)
                    for c in range(4):
                        w = slot3((W_IN_LOADS + 1 + c // 2) % RING, 2, D)
                        m = pe.matmul(SB[i % 2][:, 256 * a:256 * a + 256], w[:, c % 2, f:f + P], yhT[:, c, :],
                                      start=(c == 0), stop=(c == 3))
                inc(m, "uh_mm")

            def mix_out(l):
                wait(pe, "merged_in", l, 4)
                for c in range(KC):
                    n = W_IN_LOADS + 1 + WUH_PARTS + c // 2
                    if c % 2 == 0:
                        arrived(l, n)
                    w = slot3(n % RING, 2, D)
                    for tt in range(NT):
                        for half in range(2):
                            o = (TB if tt == 0 else OB)[half]
                            m = pe.matmul(o[:, :], merged[:, c, P * tt:P * tt + P], w[:, c % 2, 512 * half:512 * half + 512],
                                          start=(c == 0), stop=(c == KC - 1))
                    if c % 2 == 1:
                        inc(m, "wout_mm")

            def route(l):
                wait(pe, "h_in", l, 8)
                if l == 0:
                    pe.wait_ge(s_wr, 16 * 5)
                else:
                    pe.wait_ge(s_wr, 2 * 16 * 5)
                for tt in range(NT):
                    for c in range(KC):
                        m = pe.matmul(UB[0][:, 64 * tt:64 * tt + 36], hT[:, c, P * tt:P * tt + P], wr[:, c, :],
                                      start=(c == 0), stop=(c == KC - 1))
                inc(m, "logit_mm")
                wait(pe, "mask_in", l, 1)
                one, bef = C("ones"), C("before")
                pe.matmul(UB[1][:, 0:NE], bef, mh[:, 0, :], start=True, stop=True)
                pe.matmul(UB[1][:, NE:2 * NE], bef, mh[:, 1, :], start=True, stop=False)
                pe.matmul(UB[1][:, NE:2 * NE], one, mh[:, 0, :], start=False, stop=True)
                pe.matmul(UB[1][:, 2 * NE:3 * NE], one, mh[:, 0, :], start=True, stop=False)
                inc(pe.matmul(UB[1][:, 2 * NE:3 * NE], one, mh[:, 1, :], start=False, stop=True), "pos_mm")

            def gather(b):
                for c in range(KC):
                    for tt in range(NT):
                        m = pe.matmul(UB[b][:, SLOTS * c:SLOTS * c + SLOTS], xn[:, tt, c::KC], sel[:, b, tt, :],
                                      start=(tt == 0), stop=(tt == NT - 1))
                return m

            def gate_up(b, s0):
                wg, wu = slot3(s0, KC, FE), slot3(s0 + 1, KC, FE)
                for c in range(KC):
                    for q in range(4):
                        m = pe.matmul(SB[b][32 * q:32 * q + 32, 0:256], hs[:, b, c, :],
                                      (wg, wu)[q // 2][:, c, 256 * (q % 2):256 * (q % 2) + 256],
                                      start=(c == 0), stop=(c == KC - 1))
                return m

            def hid_turn(b):
                for j in range(2):
                    m = pe.transpose(TB[b][:, P * j:P * j + P], hid[:, b, j::2], ident)
                return m

            def down(b, s0):
                wd = ring[:, s0 + 2, :].rearrange("p (h j d) -> p h j d", h=2, j=2)
                for k in range(4):
                    half, j = k // 2, k % 2
                    for q in range(4):
                        m = pe.matmul(OB[b][32 * q:32 * q + 32, 0:256], hidT[:, b, j, 32 * half:32 * half + 32],
                                      wd[:, half, j, 256 * q:256 * q + 256], start=(k == 0), stop=(k == 3))
                return m

            def expert(l, e, i, b, first, last):
                for k in range(2):
                    pe.wait_ge(landed[3 * b + k], (i + l * ROUNDS + MIX_LOADS // RING + 1) * 16)
                wait(pe, "hs_in", l, e + 1)
                if not first:
                    wait(pe, "hid_in", l, e - 1)
                inc(gate_up(b, 3 * b), "gu_mm")
                if not last or b == 0:
                    wait(pe, "sel_in", l, e + 2)
                    if not (first and b == 0):
                        wait(pe, "hs_in", l, e)
                    inc(gather(1 - b), "gather_mm")
                wait(pe, "hid_in", l, e + 1)
                if not first:
                    wait(pe, "hidT_in", l, e - 1)
                inc(hid_turn(b), "hid_turned")
                wait(pe, "hidT_in", l, e + 1)
                if not first:
                    wait(pe, "y_in", l, e - 1)
                pe.wait_ge(landed[3 * b + 2], (i + l * ROUNDS + MIX_LOADS // RING + 1) * 16)
                inc(down(b, 3 * b), "down_mm")

            pe.wait_ge(s_const, 16 * 8)
            pe.transpose(TB[0][:, 0:24], rows[:, :], ident[0:24, 0:24]).then_inc(s_lbt, 1)
            pe.wait_ge(s_lb, 1)
            for l in range(DEPTH):
                turn(l, 0)
                for u in range(4):
                    unit(l, u)
                qk_turn(l)
                unit(l, 4)
                scores(l, 0)
                unit(l, 5)
                for g in range(4):
                    prob_turn(l, g)
                    if g < 3:
                        scores(l, g + 1)
                    pv(l, g)
                    unit(l, 6 + g)
                unit(l, 10)
                kend_turn(l)
                unit(l, 11)
                states(l)
                unit(l, 12)
                for n in range(8):
                    intra(l, n)
                    unit(l, 13 + n)
                    outputs(l, n)
                    if n == 5:
                        y_turn(l, 0)
                up_attn(l, 0)
                up_attn(l, 1)
                y_turn(l, 1)
                for i in range(4):
                    up_hgrn(l, i)
                    if i < 2:
                        up_attn(l, i + 2)
                mix_out(l)
                turn(l, 1)
                route(l)
                wait(pe, "sel_in", l, 1)
                wait(pe, "route_in", l, 1)
                inc(gather(0), "gather_mm")
                for b in range(2):
                    expert(l, b, 0, b, True, False)
                with pe.Fori(1, NE // 2 - 1) as i:
                    for b in range(2):
                        expert(l, i * 2 + b, i, b, False, False)
                for b in range(2):
                    expert(l, NE - 2 + b, NE // 2 - 1, b, False, True)

                ov = OV[l]
                over = pe.value_load(ctl[0:1, 0:1], min_val=0, max_val=MAX_OVER)
                wait(pe, "y_in", l, NE)
                pe.sem_inc(ov["down"], 1)
                with pe.Fori(0, MAX_OVER) as j:
                    with pe.If(j < over):
                        pe.wait_ge(ov["sel"], j + 1)
                        gather(0).then_inc(ov["gather"], 1)
                        pe.wait_ge(ov["hs"], j + 1)
                        pe.wait_ge(ov["landed"], (j + 1) * 48)
                        gate_up(0, 0).then_inc(ov["gu"], 1)
                        pe.wait_ge(ov["hid"], j + 1)
                        hid_turn(0).then_inc(ov["turned"], 1)
                        pe.wait_ge(ov["hidT"], j + 1)
                        down(0, 0).then_inc(ov["down"], 1)
                    with pe.Else():
                        pe.nop()

        @block.scalar
        def _(act):
            A = nc.scalar.activation

            def squares(l, half):
                if half == 0 and l > 0:
                    wait(act, "x_done", l - 1, 1)
                if half == 0 and l == 0:
                    act.wait_ge(s_x, 16)
                if half == 1:
                    wait(act, "x_mixed", l, 1)
                for tt in range(NT):
                    m = A(xn[:, tt, :], x[:, tt, :], ACT.Square, accum_out=ss[:, tt:tt + 1])
                inc(m, "squares")

            def root(l, k, a, b):
                wait(act, "mean_in", l, k)
                inc(A(rs1[:, a:b], rs0[:, a:b], ACT.Ln), "root_log")
                wait(act, "root_log", l, k)
                inc(A(rs1[:, a:b], rs1[:, a:b], ACT.Exp, scale=-0.5), "root")

            def unit(l, u):
                wait(act, "unit_mm", l, u + 1)
                b = UB[u % 2][:, :]
                b2 = b.rearrange("p (a n) -> p a n", a=2)
                if u < 2:
                    if l > 0:
                        wait(act, "x_done", l - 1, 1)
                    m = A(raw[:, :, 256 * u:256 * u + 256], b2, ACT.Copy)
                elif u == 2:
                    A(raw[:, :, 512:640], b2[:, :, 0:P], ACT.Copy)
                    m = A(vv[:, :, :], b2[:, :, P:2 * P], ACT.Copy)
                elif u in (3, 4):
                    m = A(qd[:, 2 * (u - 3):2 * (u - 3) + 2, :], b2, ACT.Exp, scale=-1.0)
                elif u in Z_UNITS:
                    z = u - 5
                    if z >= 2:
                        wait(act, "b_in", l, z - 1)
                    m = A(ft[:, z % 2, :], b, ACT.Exp, scale=-1.0)
                elif u in (9, 10):
                    m = A(hv[:, :, 256 * (u - 9):256 * (u - 9) + 256], b2, ACT.Copy)
                elif u in (11, 12):
                    m = A(og[:, :, 256 * (u - 11):256 * (u - 11) + 256], b2, ACT.Exp, scale=-1.0)
                else:
                    if u == 13:
                        wait(act, "pv_mm", l, 4)
                    m = A(gate[:, 2 * (u - 13):2 * (u - 13) + 2, :], b2, ACT.Exp, scale=-1.0)
                inc(m, "unit_seen")

            def log_f(l, z):
                wait(act, "f_in", l, z + 1)
                if z >= 1:
                    wait(act, "b_in", l, z)
                inc(A(logf, ft[:, z % 2, :], ACT.Ln), "f_log")

            def probs(l, g):
                wait(act, "sunk", l, g + 1)
                if g >= 2:
                    wait(act, "prob_turned", l, g - 1)
                for n in range(4):
                    par, hh = n // 2, n % 2
                    A(prob[:, g % 2, n, :], SB[par][:, 256 * hh:256 * hh + 256], ACT.Exp, scale=1.0,
                      bias=anm[:, g % 2, n:n + 1], accum_out=asum[:, g % 2, n:n + 1])
                inc(A(aexp[:, g % 2, :], adif[:, g % 2, :], ACT.Exp), "prob_exp")

            def prob_out(l, g):
                wait(act, "prob_turned", l, g + 1)
                if g >= 1:
                    wait(act, "pv_mm", l, g)
                for j in range(NT):
                    m = A(probT[:, j, :], TB[j][:, :], ACT.Copy)
                inc(m, "prob_out")

            def kend_exp(l):
                wait(act, "b_in", l, 4)
                for r in range(2):
                    for h in range(HH):
                        hT_ = NT * h + r
                        b, edge = ((bd[:, 0, hT_, 1:P + 1], bd[:, 0, hT_, P:P + 1]) if r == 0 else
                                   (bd[:, 1, hT_, 0:P], bd[:, 1, hT_, 0:1]))
                        m = A(kend[:, 4 * r + h, :], b, ACT.Exp, scale=-1.0, bias=edge)
                inc(m, "kend_exp")

            def q_exp(l):
                for r in range(2):
                    wait(act, "qe_sub", l, r + 1)
                    inc(A(xn[:, r, :], xn[:, r, :], ACT.Exp), "qe_exp")
                    b = bd[:, r, 1 - r::NT, :]
                    inc(A(qc[:, r, :, :], b[:, :, 1 - r:P + 1 - r], ACT.Exp), "qc_exp")

            def kendT(l):
                for r in range(2):
                    wait(act, "kend_turned", l, r + 1)
                    inc(A(ek[:, 1, 4 * r:4 * r + 4, :], TB[r][:, :].rearrange("p (h s) -> p h s", h=HH), ACT.Copy), "kendT_in")

            def state_in(l):
                for r in range(2):
                    wait(act, "state_mm", l, r + 1)
                    inc(A(ft[:, r, :], TB[r][:, :], ACT.Copy), "state_in")

            def ek_exp(l, n):
                T, h = n // HH, n % HH
                for r in range(2):
                    if n == 0:
                        wait(act, "state_mm", l, 2)
                    else:
                        wait(act, "at_mm", l, n)
                    b = bd[:, r, NT * h + T, :]
                    for i in range(NCH):
                        if r == 0:
                            m = A(ek[:, 0, i, 0:CHUNK * (i + 1)], b[:, 1:CHUNK * (i + 1) + 1], ACT.Exp, scale=-1.0,
                                  bias=b[:, CHUNK * i:CHUNK * i + 1])
                        else:
                            m = A(ek[:, 1, i, CHUNK * i:P], b[:, CHUNK * i:P], ACT.Exp, scale=-1.0,
                                  bias=b[:, CHUNK * (i + 1):CHUNK * (i + 1) + 1])
                    inc(m, "ek_exp")

            def o_square(l, T):
                wait(act, "o_mm", l, 4 * T + 4)
                inc(A(junk[:, :], OB[T][:, :], ACT.Square, accum_out=ss[:, T:T + 1]), "osq")
                root(l, 2 + T, T, T + 1)

            def expert(l, e, i, b, first):
                wait(act, "gu_mm", l, e + 1)
                if not first:
                    wait(act, "hid_in", l, e - 1)
                A(eg[0:64, b, :], SB[b][0:64, 0:256], ACT.Exp, scale=-1.0)
                inc(A(up[0:64, b, :], SB[b][64:128, 0:256], ACT.Copy), "gu_seen")
                wait(act, "hid_turned", l, e + 1)
                if not first:
                    wait(act, "down_mm", l, e - 1)
                inc(A(hidT[:, b, :, :], TB[b][:, 0:2 * P].rearrange("p (j s) -> p j s", j=2)[:, :, 0:64], ACT.Copy), "hidT_in")
                wait(act, "down_mm", l, e + 1)
                if not (first and isinstance(l, int) and l == 0):
                    act.wait_ge(y_out[b], (i + l * (NE // 2)) * 16)
                inc(A(ysb[:, b, :], OB[b][:, 0:256], ACT.Copy), "y_in")

            act.wait_ge(s_lb, 2)
            A(cols[:, 0:16], cols[:, 0:16], ACT.Exp).then_inc(s_lbe, 1)
            for l in range(DEPTH):
                squares(l, 0)
                root(l, 1, 0, NT)
                for u in range(5):
                    unit(l, u)
                probs(l, 0)
                unit(l, 5)
                for g in range(4):
                    prob_out(l, g)
                    if g == 0:
                        log_f(l, 0)
                    if g < 3:
                        probs(l, g + 1)
                    unit(l, 6 + g)
                    if g < 3:
                        log_f(l, g + 1)
                kend_exp(l)
                q_exp(l)
                unit(l, 10)
                kendT(l)
                unit(l, 11)
                state_in(l)
                ek_exp(l, 0)
                unit(l, 12)
                for n in range(8):
                    if n < 7:
                        ek_exp(l, n + 1)
                    unit(l, 13 + n)
                    if n == 4:
                        o_square(l, 0)
                o_square(l, 1)
                squares(l, 1)
                root(l, 4, 0, NT)
                wait(act, "gsub", l, 1)
                inc(A(cand[:, :, 0:GROUPS], cand[:, :, 0:GROUPS], ACT.Exp), "gexp")
                wait(act, "e2sub", l, 1)
                inc(A(e2, e2, ACT.Exp), "e2exp")
                for b in range(2):
                    expert(l, b, 0, b, True)
                with act.Fori(1, NE // 2) as i:
                    for b in range(2):
                        expert(l, i * 2 + b, i, b, False)
                ov = OV[l]
                wait(act, "route_in", l, 1)
                over = act.value_load(ctl[0:1, 0:1], min_val=0, max_val=MAX_OVER)
                with act.Fori(0, MAX_OVER) as j:
                    with act.If(j < over):
                        act.wait_ge(ov["gu"], j + 1)
                        A(eg[0:64, 0, :], SB[0][0:64, 0:256], ACT.Exp, scale=-1.0)
                        A(up[0:64, 0, :], SB[0][64:128, 0:256], ACT.Copy).then_inc(ov["seen"], 1)
                        act.wait_ge(ov["turned"], j + 1)
                        A(hidT[:, 0, :, :], TB[0][:, 0:2 * P].rearrange("p (j s) -> p j s", j=2)[:, :, 0:64],
                          ACT.Copy).then_inc(ov["hidT"], 1)
                        act.wait_ge(ov["down"], j + 2)
                        act.wait_ge(ov["y_free"], j + 1)
                        A(ysb[:, 0, :], OB[0][:, 0:256], ACT.Copy).then_inc(ov["y"], 1)
                    with act.Else():
                        act.nop()
            squares(DEPTH, 0)
            root(DEPTH, 1, 0, NT)

        @block.vector
        def _(dve):
            V = nc.vector
            step = [0]

            def link(ins):
                step[0] += 1
                ins.then_inc(s_dve, 1)
                dve.wait_ge(s_dve, step[0])

            def bc(ap, n):
                return ap.unsqueeze(len(ap.shape)).broadcast_to([*ap.shape, n])

            def inverse_root(l, k, a, b, n):
                if k in (1, 4):
                    wait(dve, "squares", l, (k + 2) // 3)
                else:
                    wait(dve, "osq", l, k - 1)
                v, y, u = rs0[:, a:b], rs1[:, a:b], rs2[:, a:b]
                inc(V.tensor_scalar(v, ss[:, a:b], 1.0 / n, EPS, ALU.mult, ALU.add), "mean_in")
                wait(dve, "root", l, k)
                link(V.tensor_tensor(u, y, y, ALU.mult))
                link(V.tensor_tensor(u, u, v, ALU.mult))
                link(V.tensor_scalar(u, u, -0.5, 1.5, ALU.mult, ALU.add))
                link(V.tensor_tensor(rstd[:, a:b], y, u, ALU.mult))

            def normalise(l, half):
                inverse_root(l, 3 * half + 1, 0, NT, D)
                for tt in range(NT):
                    m = V.tensor_scalar(xn[:, tt, :], x[:, tt, :], rstd[:, tt:tt + 1], None, ALU.mult)
                inc(m, "xn_in")

            def turned(l, half):
                for g in range(4):
                    tt, q = g // 2, g % 2
                    wait(dve, "turned", l, 4 * half + g + 1)
                    inc(V.tensor_tensor(hT[:, 4 * q:4 * q + 4, P * tt:P * tt + P],
                                        TB[g % 2][:, :].rearrange("p (c s) -> p c s", c=4),
                                        bc(gains[:, DEPTH * half + l, 4 * q:4 * q + 4], P), ALU.mult), "h_in")

            def sigmoid_tail(ap):
                link(V.tensor_scalar(ap, ap, 1.0, None, ALU.add))
                link(V.reciprocal(ap, ap))

            def rope(l):
                wait(dve, "unit_seen", l, 3)
                for tt in range(NT):
                    src = raw[:, tt, :].rearrange("p (h a f) -> p h a f", a=2, f=32)
                    t1, t2 = src[:, :, 0, :], src[:, :, 1, :]
                    c = cos[:, tt, :].unsqueeze(1).broadcast_to([P, 10, 32])
                    s = sin[:, tt, :].unsqueeze(1).broadcast_to([P, 10, 32])
                    r0 = rot[:, 0, 320 * tt:320 * tt + 320].rearrange("p (h f) -> p h f", f=32)
                    r1 = rot[:, 1, 320 * tt:320 * tt + 320].rearrange("p (h f) -> p h f", f=32)
                    dq = roped[:, tt, 0:512].rearrange("p (h a f) -> p h a f", a=2, f=32)
                    dk = roped[:, tt, 512:768].rearrange("p (v d a f) -> p v d a f", v=2, d=2, f=32)
                    for a, (u, w, op) in enumerate(((t1, t2, ALU.subtract), (t2, t1, ALU.add))):
                        V.tensor_tensor(r0, u, c, ALU.mult)
                        link(V.tensor_tensor(r1, w, s, ALU.mult))
                        V.tensor_tensor(dq[:, :, a, :], r0[:, 0:8, :], r1[:, 0:8, :], op)
                        V.tensor_tensor(dk[:, :, 0, a, :], r0[:, 8:10, :], r1[:, 8:10, :], op)
                        m = V.tensor_tensor(dk[:, :, 1, a, :], r0[:, 8:10, :], r1[:, 8:10, :], op)
                        if tt == NT - 1 and a == 1:
                            inc(m, "roped_in")
                        else:
                            link(m)

            def qk_in(l):
                for tt in range(NT):
                    wait(dve, "qk_turned", l, tt + 1)
                    inc(V.tensor_scalar(qT[:, tt, :, :], TB[tt][:, :].rearrange("p (c s) -> p c s", c=4), HD ** -0.5, None,
                                        ALU.mult), "qkT_in")
                wait(dve, "qk_turned", l, 3)
                inc(V.tensor_copy(kT[:, :, :, :], TB[0][:, :].rearrange("p (t k s) -> p t k s", t=NT, k=KVH)), "qkT_in")

            def sink_max(l, g):
                b, kv = g // 2, g % 2
                wait(dve, "score_mm", l, g + 1)
                for par in range(2):
                    sc = SB[par][:, :].rearrange("p (h s) -> p h s", h=2)
                    part = sc[:, :, P:2 * P] if b == 0 else sc[:, :, 0:P]
                    mask = C("win0" if b == 0 else "win1").unsqueeze(1).broadcast_to([P, 2, P])
                    link(V.tensor_tensor(part, part, mask, ALU.add))
                for par in range(2):
                    sc = SB[par][:, :].rearrange("p (h s) -> p h s", h=2)
                    link(V.tensor_reduce(amax[:, g % 2, 2 * par:2 * par + 2], sc, AX_X, ALU.max))
                sk = sink[:, l, 4 * kv:4 * kv + 4].rearrange("p (h a) -> p a h", a=2)
                mx, m4 = amax[:, g % 2, :], am[:, g % 2, :]
                link(V.tensor_tensor(m4.rearrange("p (a h) -> p a h", a=2), mx.rearrange("p (a h) -> p a h", a=2), sk, ALU.max))
                link(V.tensor_scalar(anm[:, g % 2, :], m4, -1.0, None, ALU.mult))
                inc(V.tensor_tensor(adif[:, g % 2, :].rearrange("p (a h) -> p a h", a=2), sk,
                                    m4.rearrange("p (a h) -> p a h", a=2), ALU.subtract), "sunk")

            def prob_in(l, g):
                wait(dve, "prob_exp", l, g + 1)
                ad = aden[:, g % 2, :]
                link(V.tensor_tensor(ad, asum[:, g % 2, :], aexp[:, g % 2, :], ALU.add))
                link(V.reciprocal(ad, ad))
                for n in range(4):
                    m = V.tensor_scalar(prob[:, g % 2, n, :], prob[:, g % 2, n, :], ad[:, n:n + 1], None, ALU.mult)
                inc(m, "prob_in")

            def ya_in(l, g):
                b, kv = g // 2, g % 2
                wait(dve, "pv_mm", l, g + 1)
                inc(V.tensor_copy(yaT[:, 2 * kv:2 * kv + 2, P * b:P * b + P],
                                  OB[g % 2][:, 0:256].rearrange("p (c s) -> p c s", c=2)), "ya_in")

            def silu_unit(l, u):
                wait(dve, "unit_seen", l, u + 1)
                b2 = UB[u % 2][:, :].rearrange("p (a n) -> p a n", a=2)
                dst = qd[:, 2 * (u - 3):2 * (u - 3) + 2, :] if u < 5 else og[:, :, 256 * (u - 11):256 * (u - 11) + 256]
                sigmoid_tail(dst)
                inc(V.tensor_tensor(dst, dst, b2, ALU.mult), "unit_done")

            def forget(l, z):
                r, hh = z // 2, z % 2
                wait(dve, "unit_seen", l, 5 + z + 1)
                f = ft[:, z % 2, :]
                sigmoid_tail(f)
                for a in range(2):
                    h = 4 * r + 2 * hh + a
                    link(V.tensor_scalar(f[:, 256 * a:256 * a + 256], f[:, 256 * a:256 * a + 256], lbs[:, 0, l, h:h + 1],
                                         lbs[:, 1, l, h:h + 1], ALU.mult, ALU.add))
                V.tensor_scalar(f, f, float(np.exp(LOGF_MIN)), None, ALU.max).then_inc(PEV["f_in"][0], 1)
                wait(dve, "f_in", l, z + 1)
                link(V.tensor_scalar(kd[:, r, 2 * hh:2 * hh + 2, :].rearrange("p a s -> p (a s)"), f, -1.0, 1.0,
                                     ALU.mult, ALU.add))

            def cumulate(l, z):
                r, hh = z // 2, z % 2
                wait(dve, "f_log", l, z + 1)
                for a in range(2):
                    for T in range(NT):
                        lf = logf[:, 256 * a + P * T:256 * a + P * T + P]
                        b = bd[:, r, NT * (2 * hh + a) + T, :]
                        if r == 0:
                            m = V.tensor_tensor_scan(b[:, 1:P + 1], C("ones"), lf, 0.0, ALU.mult, ALU.add)
                        else:
                            m = V.tensor_tensor_scan(b[:, 0:P][:, ::-1], C("ones"), lf[:, ::-1], 0.0, ALU.mult, ALU.add)
                inc(m, "b_in")

            def q_sub(l):
                wait(dve, "b_in", l, 4)
                for r in range(2):
                    b = bd[:, r, :, 1 - r:P + 1 - r].rearrange("p h (c u) -> p h c u", u=CHUNK)
                    edge = bd[:, r, :, CHUNK * r:P + CHUNK * r - (CHUNK - 1):CHUNK] if r == 0 else \
                        bd[:, r, :, CHUNK:P + 1:CHUNK]
                    inc(V.tensor_tensor(qe[:, r, :, :, :], b, bc(edge, CHUNK), ALU.subtract), "qe_sub")

            def q_in(l):
                for r in range(2):
                    wait(dve, "qc_exp", l, r + 1)
                    V.tensor_tensor(qc[:, r, :, :], qc[:, r, :, :], qd[:, :, P * (1 - r):P * (1 - r) + P], ALU.mult)
                    e = xn[:, r, :]
                    inc(V.tensor_tensor(e, e, qd[:, :, :].rearrange("p h s -> p (h s)"), ALU.mult), "qe_in")

            def kend_in(l):
                wait(dve, "kend_exp", l, 1)
                for r in range(2):
                    e = kend[:, 4 * r:4 * r + 4, :]
                    m = V.tensor_tensor(e, e, kd[:, r, :, P * r:P * r + P], ALU.mult)
                inc(m, "kend_in")

            def ek_in(l, n):
                T, h = n // HH, n % HH
                for r in range(2):
                    wait(dve, "ek_exp", l, 2 * n + r + 1)
                    k = kd[:, r, h, P * T:P * T + P].unsqueeze(1).broadcast_to([P, NCH, P])
                    inc(V.tensor_tensor(ek[:, r, :, :], ek[:, r, :, :], k, ALU.mult), "ek_in")

            def at_in(l, n):
                wait(dve, "at_mm", l, n + 1)
                if n >= 2:
                    wait(dve, "o_mm", l, n - 1)
                for r, name in ((0, "tri_f"), (1, "tri_b")):
                    m = V.tensor_tensor(at_sb[:, n % 2, r, :], SB[n % 2][:, P * r:P * r + P], C(name), ALU.mult)
                inc(m, "at_in")

            def y_ready(l, T):
                inverse_root(l, 2 + T, T, T + 1, HW)
                inc(V.scalar_tensor_tensor(out=og[:, T, :], in0=OB[T][:, :], scalar=rstd[:, T:T + 1], in1=og[:, T, :],
                                           op0=ALU.mult, op1=ALU.mult), "y_ready")

            def yT_in(l, T):
                wait(dve, "y_turned", l, T + 1)
                inc(V.tensor_tensor(yhT[:, :, P * T:P * T + P], TB[T][:, :].rearrange("p (c s) -> p c s", c=4),
                                    bc(cols[:, 16 + 4 * l:20 + 4 * l], P), ALU.mult), "yT_in")

            def merge(l, i):
                wait(dve, "ua_mm", l, i + 1)
                wait(dve, "uh_mm", l, i + 1)
                ga, gb = gate[:, 2 * i:2 * i + 2, :], gate[:, 8 + 2 * i:8 + 2 * i + 2, :]
                V.tensor_tensor(ga, ga, UB[i % 2][:, :].rearrange("p (a s) -> p a s", a=2), ALU.mult)
                link(V.tensor_tensor(gb, gb, SB[i % 2][:, :].rearrange("p (a s) -> p a s", a=2), ALU.mult))
                inc(V.tensor_tensor(merged[:, 2 * i:2 * i + 2, :], ga, gb, ALU.add), "merged_in")

            def first_of(out, values, best, n):
                link(V.tensor_tensor(eqs[:, :, 0:n], values, bc(best, n), ALU.is_equal))
                fall = C("falling")[:, 8 - n:8].unsqueeze(1).broadcast_to([P, NT, n])
                link(V.tensor_tensor(eqs[:, :, 0:n], eqs[:, :, 0:n], fall, ALU.mult))
                link(V.tensor_reduce(cmax, eqs[:, :, 0:n], AX_X, ALU.max))
                link(V.tensor_tensor(out, eqs[:, :, 0:n], bc(cmax, n), ALU.is_equal))

            def route(l):
                wait(dve, "logit_mm", l, 1)
                b2 = UB[0][:, 0:128].rearrange("p (t n) -> p t n", t=NT)[:, :, 0:GROUPS + NE]
                link(V.tensor_tensor(lg, b2, bias[:, l, :].unsqueeze(1).broadcast_to([P, NT, GROUPS + NE]), ALU.add))
                g4 = lg[:, :, 0:GROUPS]
                link(V.tensor_reduce(gmax, g4, AX_X, ALU.max))
                inc(V.tensor_tensor(cand[:, :, 0:GROUPS], g4, bc(gmax, GROUPS), ALU.subtract), "gsub")
                first_of(ohg, g4, gmax, GROUPS)
                e4 = lg[:, :, GROUPS:].rearrange("p t (g e) -> p t g e", g=GROUPS)
                for tt in range(NT):
                    link(V.tensor_tensor(tmp[:, tt, :, :], e4[:, tt, :, :], bc(ohg[:, tt, :], EPG), ALU.mult))
                link(V.tensor_reduce(lsel, tmp.rearrange("p t g e -> p t e g"), AX_X, ALU.add))
                link(V.tensor_reduce(m1, lsel, AX_X, ALU.max))
                first_of(oh1, lsel, m1, EPG)
                link(V.scalar_tensor_tensor(out=lsel2, in0=oh1, scalar=NEG, in1=lsel, op0=ALU.mult, op1=ALU.add))
                link(V.tensor_reduce(m2, lsel2, AX_X, ALU.max))
                inc(V.tensor_tensor(e2, m2, m1, ALU.subtract), "e2sub")
                first_of(oh2, lsel2, m2, EPG)
                for tt in range(NT):
                    for dst, oh in ((m1h, oh1), (m2h, oh2)):
                        link(V.tensor_tensor(dst[:, tt, :, :], bc(ohg[:, tt, :], EPG),
                                             oh[:, tt, :].unsqueeze(1).broadcast_to([P, GROUPS, EPG]), ALU.mult))
                m1f, m2f = (a.rearrange("p t g e -> p (t g e)") for a in (m1h, m2h))
                mf = mh.rearrange("p t e -> p (t e)")
                inc(V.tensor_tensor(mf, m1f, m2f, ALU.add), "mask_in")
                wait(dve, "gexp", l, 1)
                link(V.tensor_reduce(psum_g, cand[:, :, 0:GROUPS], AX_X, ALU.add))
                link(V.reciprocal(ptop, psum_g))
                wait(dve, "e2exp", l, 1)
                link(V.tensor_scalar(den2, e2, 1.0, None, ALU.add))
                link(V.reciprocal(den2, den2))
                link(V.tensor_tensor(w1, den2, ptop, ALU.mult))
                link(V.tensor_tensor(w2, w1, e2, ALU.mult))
                wait(dve, "pos_mm", l, 1)
                posf, posmf = (a.rearrange("p t e -> p (t e)") for a in (pos, posm))
                link(V.tensor_copy(posf, UB[1][:, 0:2 * NE]))
                link(V.scalar_tensor_tensor(out=posmf, in0=posf, scalar=1.0, in1=mf, op0=ALU.add, op1=ALU.mult))
                link(V.tensor_scalar(posmf, posmf, -1.0, None, ALU.add))
                link(V.tensor_copy(count, UB[1][:, 2 * NE:3 * NE]))
                link(V.tensor_tensor(grid2, bc(count, 7), C("limits").unsqueeze(1).broadcast_to([P, NE, 7]), ALU.is_gt))
                link(V.tensor_reduce(novb, grid2, AX_X, ALU.add))
                link(V.tensor_tensor_scan(oend, C("ones")[:, 0:NE], novb, 0.0, ALU.mult, ALU.add))
                link(V.tensor_copy(ctlf[:, 0:1], oend[:, NE - 1:NE]))
                link(V.tensor_tensor(grid, oend.unsqueeze(1).broadcast_to([P, MAX_OVER, NE]), bc(C("over_at"), NE), ALU.is_le))
                link(V.tensor_reduce(ctlf[:, 1:], grid, AX_X, ALU.add))
                link(V.tensor_scalar(ctlf[:, 1:], ctlf[:, 1:], float(NE - 1), None, ALU.min))
                link(V.tensor_tensor(grid, grid, novb.unsqueeze(1).broadcast_to([P, MAX_OVER, NE]), ALU.mult))
                link(V.tensor_reduce(ooff, grid, AX_X, ALU.add))
                link(V.tensor_tensor(ooff, C("over_at"), ooff, ALU.subtract))
                link(V.tensor_scalar(ooff, ooff, 1.0, float(SLOTS), ALU.add, ALU.mult))
                link(V.tensor_copy(ctl[0:1, :], ctlf[0:1, :]))
                link(V.tensor_tensor(rbase, oend, novb, ALU.subtract))
                link(V.tensor_scalar(rbase, rbase, float(NE - 1), float(SLOTS), ALU.add, ALU.mult))
                link(V.tensor_tensor(rbase, rbase, C("first_row"), ALU.subtract))
                t2 = tmp.rearrange("p t g e -> p t (g e)")
                link(V.tensor_scalar(t2, pos, float(SLOTS), None, ALU.is_ge))
                rb = rbase.unsqueeze(1).broadcast_to([P, NT, NE])
                fr = C("first_row").unsqueeze(1).broadcast_to([P, NT, NE])
                link(V.tensor_tensor(t2, t2, rb, ALU.mult))
                link(V.tensor_tensor(t2, t2, fr, ALU.add))
                link(V.tensor_tensor(t2, t2, pos, ALU.add))
                for k, m in enumerate((m1h, m2h)):
                    m3 = m.rearrange("p t g e -> p t (g e)")
                    link(V.tensor_tensor(m3, m3, t2, ALU.mult))
                    link(V.tensor_reduce(rowf[:, k, :], m3, AX_X, ALU.add))
                inc(V.tensor_copy(rowi[:, :, :], rowf), "route_in")

            def select(b, column, offset=None):
                for tt in range(NT):
                    if offset is None:
                        m = V.tensor_scalar(sel[:, b, tt, :], C("iota"), posm[:, tt, bass.ds(column, 1)], None, ALU.is_equal)
                    else:
                        m = V.tensor_scalar(sel[:, b, tt, :], C("iota"), offset, posm[:, tt, bass.ds(column, 1)],
                                            ALU.add, ALU.is_equal)
                return m

            def tokens_in(l, b):
                return V.tensor_tensor(hs[:, b, :, :], UB[b][:, 0:SLOTS * KC].rearrange("p (c s) -> p c s", c=KC),
                                       bc(gains[:, DEPTH + l, :], SLOTS), ALU.mult)

            def hidden(b, own):
                g = eg[0:64, b, :]
                own(V.tensor_scalar(g, g, 1.0, None, ALU.add))
                own(V.reciprocal(g, g))
                own(V.tensor_tensor(g, g, SB[b][0:64, 0:256], ALU.mult))
                return V.tensor_tensor(hid[0:64, b, :], g, up[0:64, b, :], ALU.mult)

            def expert(l, e, b, first, last, own):
                if not (last and b == 1):
                    if not (first and b == 0):
                        wait(dve, "gather_mm", l, e)
                    inc(select(1 - b, e + 1), "sel_in")
                wait(dve, "gu_seen", l, e + 1)
                if not first:
                    wait(dve, "hid_turned", l, e - 1)
                inc(hidden(b, own), "hid_in")
                if not (last and b == 1):
                    wait(dve, "gather_mm", l, e + 2)
                    if not (first and b == 0):
                        wait(dve, "gu_mm", l, e)
                    inc(tokens_in(l, 1 - b), "hs_in")

            V.memset(bd[:, 0, :, 0:1], 0.0)
            V.memset(bd[:, 1, :, P:P + 1], 0.0)
            link(V.memset(ek[:, :, :, :], 0.0))
            dve.wait_ge(s_lbt, 1)
            V.tensor_copy(cols[:, :], TB[0][:, 0:24]).then_inc(s_lb, 1)
            dve.wait_ge(s_lb, 1)
            link(V.tensor_tensor(small[:, 128:136], cols[:, 0:8], cols[:, 8:16], ALU.max))
            V.tensor_tensor(cols[:, 0:8], cols[:, 0:8], small[:, 128:136], ALU.subtract)
            V.tensor_tensor(cols[:, 8:16], cols[:, 8:16], small[:, 128:136], ALU.subtract).then_inc(s_lb, 1)
            dve.wait_ge(s_lbe, 1)
            link(V.tensor_tensor(small[:, 128:136], cols[:, 0:8], cols[:, 8:16], ALU.add))
            link(V.reciprocal(small[:, 128:136], small[:, 128:136]))
            link(V.tensor_tensor(cols[:, 0:8], cols[:, 0:8], small[:, 128:136], ALU.mult))
            link(V.tensor_tensor(cols[:, 8:16], cols[:, 8:16], small[:, 128:136], ALU.mult))
            link(V.tensor_tensor(small[:, 136:144], cols[:, 0:8], cols[:, 8:16], ALU.add))
            link(V.tensor_tensor(small[:, 144:152], cols[:, 0:8], cols[:, 0:8], ALU.subtract))
            link(V.tensor_tensor(small[:, 152:160], small[:, 136:144], cols[:, 0:8], ALU.subtract))
            for l in range(DEPTH):
                lb = small[:, 144 + 8 * l:152 + 8 * l]
                link(V.tensor_scalar(lbs[:, 0, l, :], lb, -1.0, 1.0, ALU.mult, ALU.add))
                link(V.tensor_scalar(lbs[:, 1, l, :], lb, 1e-30, None, ALU.max))

            for l in range(DEPTH):
                normalise(l, 0)
                turned(l, 0)
                rope(l)
                silu_unit(l, 3)
                qk_in(l)
                silu_unit(l, 4)
                sink_max(l, 0)
                prob_in(l, 0)
                forget(l, 0)
                for g in range(4):
                    if g < 3:
                        sink_max(l, g + 1)
                    cumulate(l, g)
                    if g < 3:
                        prob_in(l, g + 1)
                    ya_in(l, g)
                    if g < 3:
                        forget(l, g + 1)
                q_sub(l)
                kend_in(l)
                q_in(l)
                silu_unit(l, 11)
                ek_in(l, 0)
                silu_unit(l, 12)
                for n in range(8):
                    at_in(l, n)
                    if n < 7:
                        ek_in(l, n + 1)
                    wait(dve, "unit_seen", l, 13 + n + 1)
                    sigmoid_tail(gate[:, 2 * n:2 * n + 2, :])
                    if n == 4:
                        y_ready(l, 0)
                    if n == 5:
                        yT_in(l, 0)
                y_ready(l, 1)
                yT_in(l, 1)
                for i in range(4):
                    merge(l, i)
                wait(dve, "wout_mm", l, WO_PARTS)
                dve.wait_ge(s_pre, 32)
                for tt in range(NT):
                    for half in range(2):
                        o = (TB if tt == 0 else OB)[half]
                        xs = x[:, tt, 512 * half:512 * half + 512]
                        m = V.tensor_tensor(xs, xs, o[:, :], ALU.add)
                inc(m, "x_mixed")
                normalise(l, 1)
                turned(l, 1)
                route(l)
                wait(dve, "route_in", l, 1)
                inc(select(0, 0), "sel_in")
                wait(dve, "gather_mm", l, 1)
                inc(tokens_in(l, 0), "hs_in")
                for b in range(2):
                    expert(l, b, b, True, False, link)
                per = 6
                base = step[0]
                with dve.Fori(1, NE // 2 - 1) as i:
                    done = [0]

                    def own(ins):
                        done[0] += 1
                        ins.then_inc(s_dve, 1)
                        dve.wait_ge(s_dve, i * per + (base - per + done[0]))

                    for b in range(2):
                        expert(l, i * 2 + b, b, False, False, own)
                    assert done[0] == per
                step[0] += per * (NE // 2 - 2)
                for b in range(2):
                    expert(l, NE - 2 + b, b, False, True, link)

                ov = OV[l]
                wait(dve, "route_in", l, 1)
                over = dve.value_load(ctl[0:1, 0:1], min_val=0, max_val=MAX_OVER)
                wait(dve, "down_mm", l, NE)
                s_own = s_ov[l]
                with dve.Fori(0, MAX_OVER) as j:
                    with dve.If(j < over):
                        e = dve.value_load(ctl[0:1, bass.ds(j + 1, 1)], min_val=0, max_val=NE - 1)
                        select(0, e, ooff[:, bass.ds(j, 1)]).then_inc(ov["sel"], 1)
                        dve.wait_ge(ov["gather"], j + 1)
                        tokens_in(l, 0).then_inc(ov["hs"], 1)
                        dve.wait_ge(ov["seen"], j + 1)
                        done = [0]

                        def own(ins):
                            done[0] += 1
                            ins.then_inc(s_own, 1)
                            dve.wait_ge(s_own, j * 3 + done[0])

                        hidden(0, own).then_inc(ov["hid"], 1)
                    with dve.Else():
                        dve.nop()

                dve.wait_ge(fetched, 64 * (l + 1))
                for k, w in enumerate((w1, w2)):
                    for tt in range(NT):
                        m = V.scalar_tensor_tensor(out=x[:, tt, :], in0=got[:, k, tt, :], scalar=w[:, tt:tt + 1],
                                                   in1=x[:, tt, :], op0=ALU.mult, op1=ALU.add)
                        if k == 0:
                            link(m)
                inc(m, "x_done")
            inverse_root(DEPTH, 1, 0, NT, D)
            dve.wait_ge(s_fin, 16)
            for tt in range(NT):
                m = V.scalar_tensor_tensor(out=xn[:, tt, :], in0=x[:, tt, :], scalar=rstd[:, tt:tt + 1], in1=fin_g,
                                           op0=ALU.mult, op1=ALU.mult)
            inc(m, "xn_in")

        @block.gpsimd
        def _(pool):
            pool.wait_ge(s_x, 16)
            over_rows = ybuf[NE * SLOTS:, :]
            pool.dma_start(over_rows[0:2 * P, :].rearrange("(t p) n -> p t n", p=P), x[:, :, :]).then_inc(s_pre, 16)
            pool.dma_start(over_rows[2 * P:, :].rearrange("(t p) n -> p t n", t=2), x[0:MAX_OVER * SLOTS // 2 - P, :, :]
                           ).then_inc(s_pre, 16)
            for l in range(DEPTH):
                for i, src in enumerate([t["w_router_group"][l].rearrange("(p c) g -> p c g", c=KC)] +
                                        [t["w_router_expert"][l, g].rearrange("(p c) e -> p c e", c=KC)
                                         for g in range(GROUPS)]):
                    a = 0 if i == 0 else GROUPS + EPG * (i - 1)
                    n = GROUPS if i == 0 else EPG
                    if l > 0 and i == 0:
                        wait(pool, "logit_mm", l - 1, 1)
                    pool.dma_start(wr[:, :, a:a + n], src).then_inc(s_wr, 16)
                def put(b, row):
                    return pool.dma_start(ybuf[bass.ds(row, SLOTS), :].rearrange("s (q n) -> q s n", q=4),
                                          ysb[:, b, :])

                with pool.Fori(0, NE // 2) as i:
                    for b in range(2):
                        wait(pool, "y_in", l, i * 2 + b + 1)
                        put(b, i * (2 * SLOTS) + b * SLOTS).then_inc(y_out[b], 16)
                wait(pool, "route_in", l, 1)
                over = pool.value_load(ctl[0:1, 0:1], min_val=0, max_val=MAX_OVER)
                for b in range(2):
                    pool.wait_ge(y_out[b], (l + 1) * (NE // 2) * 16)
                pool.sem_inc(OV[l]["y_free"], 1)
                with pool.Fori(0, MAX_OVER) as j:
                    with pool.If(j < over):
                        pool.wait_ge(OV[l]["y"], j + 1)
                        put(0, j * SLOTS + NE * SLOTS).then_inc(OV[l]["out"], 16)
                        pool.wait_ge(OV[l]["out"], (j + 1) * 16)
                        pool.sem_inc(OV[l]["y_free"], 1)
                    with pool.Else():
                        pool.nop()
                pool.wait_ge(s_pre, 32)
                for k in range(2):
                    for tt in range(NT):
                        pool.indirect_dma_start(got[:, k, tt, :], None, ybuf[:, :],
                                                bass.IndirectOffsetOnAxis(ap=rowi[:, k, tt:tt + 1], axis=0)
                                                ).then_inc(fetched, 16)
            wait(pool, "hs_in", DEPTH - 1, NE)
            wait(pool, "hid_in", DEPTH - 1, NE)
            pool.wait_ge(fetched, 64 * DEPTH)
            wait(pool, "x_done", DEPTH - 1, 1)
            pool.dma_start(fin_g, t["final_norm_g"].rearrange("(o n) -> o n", o=1).broadcast_to([P, D])).then_inc(s_fin, 16)


TOKEN_UNITS = (0, 1, 2, 9, 10, 11, 12)
Z_UNITS = (5, 6, 7, 8)
DVE_UNITS = (3, 4, 11, 12)

_INS = ["x", "attn_norm_g", "w_in", "sink_logits", "hgrn_lb_table", "hgrn_norm_g", "w_up_attn", "w_up_hgrn",
        "w_out", "ffn_norm_g", "w_router_group", "b_router_group", "w_router_expert", "b_router_expert",
        "w_expert_gate", "w_expert_up", "w_expert_down", "final_norm_g"]


def kernel(**inputs):
    import concourse.bacc as _bacc
    from concourse.bass_utils import run_bass_kernel_spmd as _run

    nc = _bacc.Bacc("TRN2", target_bir_lowering=False, num_devices=1)
    arrays = {f"in_{n}": np.ascontiguousarray(inputs[n]) for n in _INS}
    arrays["in_consts"] = constants()
    t = {}
    for n, a in arrays.items():
        t[n[3:]] = nc.dram_tensor(n, a.shape, mybir.dt.from_np(a.dtype), kind="ExternalInput").ap()
    t["out"] = nc.dram_tensor("result", (1, S, D), F32, kind="ExternalOutput").ap()
    layers_program(nc, t)
    r = _run(nc, [arrays], core_ids=[0])
    return r.results[0]["result"]
```

```python
from contextlib import ExitStack

import numpy as np

import concourse.bass as bass
from concourse import mybir

F32 = mybir.dt.float32
I32 = mybir.dt.int32
ALU = mybir.AluOpType
ACT = mybir.ActivationFunctionType
AX_X = mybir.AxisListType.X

P = 128
DEPTH, D, S = 2, 1024, 256
IN_W = 5376
NT = S // P
KC = D // P
HEADS, KVH, HD = 8, 2, 64
HH, HK = 4, 128
HW = HH * HK
CHUNK = 16
NCH = P // CHUNK
GROUPS, EPG = 4, 8
NE = GROUPS * EPG
FE = 512
SLOTS = 32
MAX_OVER = (2 * S) // (SLOTS + 1)
EPS = 1e-6
LOGF_MIN = -4.0
NEG = -1e30

SLOT_W = 4096
RING = 6
UNITS = IN_W // 256
W_IN_LOADS = (IN_W + 511) // 512
WUH_PARTS, WO_PARTS = 2, 4
MIX_LOADS = W_IN_LOADS + 1 + WUH_PARTS + WO_PARTS
DEPTH_E = 3
MIX_ROUNDS = MIX_LOADS // RING
FIRST_E, LAST_E, STEP_E = 2, 6, 6
LOOPS_E = (NE - FIRST_E - LAST_E) // STEP_E
assert MIX_LOADS % RING == 0 and RING == 2 * 3 and FIRST_E + LAST_E + STEP_E * LOOPS_E == NE

CONST = {}
_at = 0
for _name, _n in [("ident", P), ("before", P), ("ones", P), ("win0", P), ("win1", P), ("cos", NT * 32),
                  ("sin", NT * 32), ("tri_f", P), ("tri_b", P), ("iota", SLOTS), ("limits", 7), ("falling", NE),
                  ("over_at", MAX_OVER)]:
    CONST[_name] = (_at, _at + _n)
    _at += _n
CONST_W = _at


def constants():
    c = np.zeros((P, CONST_W), np.float32)

    def put(name, v):
        a, b = CONST[name]
        c[:, a:b] = np.asarray(v, np.float32).reshape(-1, b - a)

    i = np.arange(P)
    put("ident", np.eye(P))
    put("before", i[:, None] < i[None, :])
    put("ones", np.ones((P, P)))
    put("win0", np.where(i[None, :] <= i[:, None], 0.0, NEG))
    put("win1", np.where(i[None, :] >= i[:, None], 0.0, NEG))
    half = HD // 2
    inv = np.float32(10000.0) ** (-np.arange(half, dtype=np.float32) / np.float32(half))
    angle = np.arange(S, dtype=np.float32)[:, None] * inv[None, :].astype(np.float32)
    for name, f in (("cos", np.cos), ("sin", np.sin)):
        put(name, f(angle).astype(np.float32).reshape(NT, P, half).transpose(1, 0, 2).reshape(P, -1))
    put("tri_f", i[:, None] <= i[None, :])
    put("tri_b", i[:, None] >= i[None, :])
    put("iota", 1 + np.arange(SLOTS)[None])
    put("limits", (SLOTS * np.arange(1, 8))[None])
    put("falling", np.arange(NE, 0, -1)[None])
    put("over_at", np.arange(MAX_OVER)[None])
    return c


def layers_program(nc, t):
    ctx = ExitStack()
    with ctx:
        def sb(name, shape, dt=F32):
            return ctx.enter_context(nc.sbuf_tensor(name, shape, dt))

        def sem(name):
            return ctx.enter_context(nc.semaphore(name))

        ring = sb("ring", [P, RING, SLOT_W])
        const = sb("const", [P, CONST_W])
        x = sb("x", [P, NT, D])
        xn = sb("xn", [P, NT, D])
        hT = sb("hT", [P, KC, S])
        gate = sb("gate", [P, 16, S])
        qT = sb("qT", [P, NT, 4, P])
        late0 = sb("late0", [P, SLOT_W])
        late1 = sb("late1", [P, SLOT_W])
        yaT = sb("yaT", [P, 4, S])
        qd = sb("qd", [P, HH, S])
        ft = sb("ft", [P, 2, 512])
        hv = sb("hv", [P, NT, HW])
        og = sb("og", [P, NT, HW])
        at_sb = sb("at_sb", [P, 2, 2, P])
        junk = sb("junk", [P, 512])
        small = sb("small", [P, 256])
        gains = sb("gains", [P, 2 * DEPTH, KC])
        gains2 = sb("gains2", [P, DEPTH, KC])
        rows = sb("rows", [24, P])
        cols = sb("cols", [P, 24])
        lbs = sb("lbs", [P, 2, DEPTH, 8])
        sink = sb("sink", [P, DEPTH, HEADS])
        wr = sb("wr", [P, KC, GROUPS + NE])
        bias = sb("bias", [P, DEPTH, GROUPS + NE])
        ctl = sb("ctl", [1, 1 + MAX_OVER], I32)

        kd = late0[:, 0:2048].rearrange("p (r h s) -> p r h s", r=2, h=HH)
        ek = late0[:, 2048:4096].rearrange("p (r c s) -> p r c s", r=2, c=NCH)
        n_b = 2 * HH * NT * (P + 1)
        bd = late1[:, 0:n_b].rearrange("p (r h s) -> p r h s", r=2, s=P + 1)
        qc = late1[:, n_b:n_b + 1024].rearrange("p (r h s) -> p r h s", r=2, h=HH)
        kT = late1[:, n_b + 1024:n_b + 1536].rearrange("p (t k s) -> p t k s", t=NT, k=KVH)
        vv = late1[:, n_b + 1536:n_b + 1792].rearrange("p (t s) -> p t s", t=NT)

        def C(name):
            a, b = CONST[name]
            return const[:, a:b]

        ident = C("ident")
        cos = C("cos").rearrange("p (t f) -> p t f", t=NT)
        sin = C("sin").rearrange("p (t f) -> p t f", t=NT)

        flat = gate[:, :, :].rearrange("p a b -> p (a b)")
        raw = flat[:, 0:1280].rearrange("p (t n) -> p t n", t=NT)
        rot = flat[:, 1280:2560].rearrange("p (a n) -> p a n", a=2)
        roped = flat[:, 2560:4096].rearrange("p (t n) -> p t n", t=NT)
        prob = flat[:, 0:2048].rearrange("p (g h s) -> p g h s", g=2, h=4)
        probT = flat[:, 2560:3584].rearrange("p (j n) -> p j n", j=NT)
        qe = xn[:, :, :].rearrange("p r (h c u) -> p r h c u", h=HH * NT, u=CHUNK)
        kend = ek[:, 0, :, :]
        kendT = ek[:, 1, :, :]
        logf = ek[:, 1, 0:4, :].rearrange("p a b -> p (a b)")
        state = ft[:, :, :].rearrange("p r (h e) -> p r h e", h=HH)
        yhT = qd
        merged = hT
        qf, ftf = qT[:, :, :, :].rearrange("p t c s -> p (t c s)"), ft[:, :, :].rearrange("p r s -> p (r s)")
        yf = yaT[:, :, :].rearrange("p c s -> p (c s)")
        hs = qf[:, 0:512].rearrange("p (b h q s) -> p b h q s", b=2, h=2, q=4)
        hrow = qd[:, :, :].rearrange("p h s -> p (h s)")[:, 0:256]
        up = qf[:, 512:1024].rearrange("p (b s) -> p b s", b=2)
        hid = ftf[:, 0:512].rearrange("p (b s) -> p b s", b=2)
        hidT = ftf[:, 512:768].rearrange("p (b j s) -> p b j s", b=2, j=2)
        sel = ftf[:, 768:896].rearrange("p (b t s) -> p b t s", b=2, t=NT)
        eg = yf[:, 0:512].rearrange("p (b s) -> p b s", b=2)
        selw = yf[:, 512:1024].rearrange("p (b t q s) -> p b t q s", b=2, t=NT, q=4)
        selT = at_sb[:, :, :, :].rearrange("p b t s -> p b (t s)").rearrange("p b (t s) -> p b t s", t=NT)
        ysb = junk[:, :].rearrange("p (b s) -> p b s", b=2)
        fin_g = yf

        hvf = hv[:, :, :].rearrange("p t n -> p (t n)")
        ogf = og[:, :, :].rearrange("p t n -> p (t n)")

        def cut(flat_ap, at, *shape):
            n = int(np.prod(shape))
            v = flat_ap[:, at:at + n]
            if len(shape) == 2:
                v = v.rearrange("p (a b) -> p a b", a=shape[0])
            return v

        lg = cut(hvf, 0, NT, GROUPS + NE)
        m1h = cut(hvf, 96, NT, NE)
        m2h = cut(hvf, 160, NT, NE)
        mh = cut(hvf, 224, NT, NE)
        masked = cut(hvf, 288, NT, NE)
        tie = cut(hvf, 352, NT, NE)
        posm = cut(hvf, 416, NT, NE)
        count = cut(hvf, 480, NE)
        novb = cut(hvf, 512, NE)
        oend = cut(hvf, 544, NE)
        wsel = cut(hvf, 576, NT, NE)
        ctlf = cut(hvf, 640, 1 + MAX_OVER)
        ooff = cut(hvf, 656, MAX_OVER)
        ohg = cut(hvf, 672, NT, GROUPS)
        gexp = cut(hvf, 680, NT, GROUPS)
        grid = cut(ogf, 0, MAX_OVER, NE)
        grid2 = cut(ogf, 512, NE, 7)

        def sm(at, n=NT):
            return small[:, at:at + n]

        ss, rs0, rstd, rs1, rs2 = sm(0), sm(2), sm(4), sm(6), sm(28)
        gmax, psum_g, cmax, ptop, m1, m2, w1, w2, e2, den2 = (sm(8 + 2 * i) for i in range(10))
        amax, am, anm, adif, aexp, asum, aden = (small[:, 64 + 8 * i:64 + 8 * i + 8].rearrange("p (g h) -> p g h", g=2)
                                                 for i in range(7))

        def bank(name):
            return ctx.enter_context(nc.psum_tensor(name, [P, 512], F32))

        UB = [bank("unit0"), bank("unit1")]
        SB = [bank("score0"), bank("score1")]
        TB = [bank("turn0"), bank("turn1")]
        OB = [bank("out0"), bank("out1")]
        ACC = [UB, OB]
        SUMS = UB + OB
        GB, HB, YB = SB[0], SB[1], TB[1]
        HT_B, ST_B = TB[0][:, 0:256], TB[0][:, 256:512]

        def part(b, par):
            return b[:, 256 * par:256 * par + 256]

        landed = [sem(f"landed{i}") for i in range(3 * DEPTH_E)]
        s_const, s_x, s_wr, s_fin, s_out = (sem(n) for n in ("const_in", "x_in", "router_in", "final_in", "out_done"))
        s_head = sem("head_in")
        PEV = {}
        for n, per in (("turned", 8), ("unit_mm", UNITS), ("qk_turned", 3), ("score_mm", 4), ("prob_turned", 4),
                       ("pv_mm", 4), ("kend_turned", 2), ("state_mm", 2), ("at_mm", 8), ("o_mm", 8),
                       ("y_turned", 2), ("ua_mm", 4), ("uh_mm", 4), ("wout0_mm", 1), ("wout_mm", WO_PARTS), ("logit_mm", 1), ("pos_mm", 1),
                       ("gather_mm", NE), ("rows_turned", NE), ("rows_in", NE), ("gu_mm", NE), ("hid_turned", NE), ("down_mm", NE), ("sel_turned", NE), ("sum_mm", NE),
                       ("unit_seen", UNITS), ("sigmoid", 16), ("squares", 3), ("prob_exp", 4), ("f_log", 4), ("kend_exp", 1),
                       ("kendT_in", 2), ("state_in", 2), ("ek_exp", 16), ("qe_exp", 2), ("qc_exp", 2), ("osq", 2), ("prob_out", 4),
                       ("gexp", 1), ("e2exp", 1), ("gu_seen", NE), ("hidT_in", NE), ("y_in", NE), ("selT_in", NE),
                       ("xn_in", 3), ("h_in", 8), ("roped_in", 1), ("qkT_in", 3), ("sunk", 4), ("prob_in", 4),
                       ("ya_in", 4), ("unit_done", 4), ("f_in", 4), ("b_in", 4), ("kend_in", 1), ("ek_in", 16),
                       ("qe_sub", 2), ("qe_in", 2), ("at_in", 8), ("osum_out", 2), ("y_ready", 2), ("yT_in", 2),
                       ("merged_in", 4), ("x_mixed", 2), ("x_done", 1), ("gsub", 1), ("e2sub", 1), ("mask_in", 1),
                       ("route_in", 1), ("sel_in", NE), ("hs_in", NE), ("hid_in", NE), ("selw_in", NE),
                       ("mean_in", 5), ("root_log", 5), ("root", 5),
                       ("cleared", 1)):
            PEV[n] = (sem(n), per)
        s_dve, s_act = sem("dve_step"), sem("act_step")
        s_summed = sem("all_summed")
        s_ov = [sem(f"over_dve_step{l}") for l in range(DEPTH)]
        s_lb, s_lbt, s_lbe = sem("lb_rows"), sem("lb_turned"), sem("lb_exp")
        OV = [{n: sem(f"over_{n}{l}") for n in ("landed", "sel", "gather", "hs", "gu", "seen", "hid", "turned",
                                                "hidT", "rows", "rows_turned", "selw", "sel_turned", "selT", "down", "y", "sum")}
              for l in range(DEPTH)]

        def inc(ins, name):
            ins.then_inc(PEV[name][0], 1)

        def wait(eng, name, l, k):
            s, per = PEV[name]
            eng.wait_ge(s, l * per + k)

        w_in, w_ua, w_uh, w_o = t["w_in"], t["w_up_attn"], t["w_up_hgrn"], t["w_out"]

        def slot(s):
            return ring[:, s, :] if s < RING else (late0[:, :], late1[:, :],
                                                   gate[:, :, :].rearrange("p a b -> p (a b)"))[s - RING]

        def slot3(s, k, n):
            return slot(s)[:, 0:k * n].rearrange("p (c n) -> p c n", c=k)

        def expert_loads(l, e, s0):
            wg, wu, wd = t["w_expert_gate"], t["w_expert_up"], t["w_expert_down"]
            yield 0, slot3(s0, KC, FE), wg[l, e, :, :].rearrange("(p c) f -> p c f", c=KC)
            yield 1, slot3(s0 + 1, KC, FE), wu[l, e, :, :].rearrange("(p c) f -> p c f", c=KC)
            yield 2, slot(s0 + 2).rearrange("p (h n) -> p h n", h=2), \
                wd[l, e, :, :].rearrange("(h p j) d -> p h (j d)", h=2, p=P)

        def spread(ap):
            return ap.rearrange("(o l) n -> o l n", o=1).broadcast_to([P, *ap.shape])

        block = ctx.enter_context(nc.Block())

        @block.sync
        def _(sp):
            sp.dma_start(x[:], t["x"].rearrange("b (t p) d -> p (b t) d", p=P)).then_inc(s_x, 16)
            sp.dma_start(const[:], t["consts"]).then_inc(s_head, 16)

            def wait_used(l, n):
                if n < 0:
                    if l > 0:
                        e, k = NE - 2 + (n + 6) // 3, (n + 6) % 3
                        wait(sp, "down_mm" if k == 2 else "gu_mm", l - 1, e + 1)
                elif n < W_IN_LOADS:
                    wait(sp, "unit_mm", l, min(2 * n + 2, UNITS))
                elif n == W_IN_LOADS:
                    wait(sp, "ua_mm", l, 4)
                elif n <= W_IN_LOADS + WUH_PARTS:
                    wait(sp, "uh_mm", l, 4)
                else:
                    wait(sp, "wout_mm", l, n - W_IN_LOADS - WUH_PARTS)

            def load(l, n, dst, src):
                wait_used(l, n - RING)
                sp.dma_start(dst, src).then_inc(landed[n % RING], 16)

            for l in range(DEPTH):
                for i in range(W_IN_LOADS):
                    n = min(512, IN_W - 512 * i)
                    load(l, i, slot3(i % RING, KC, n),
                         w_in[l].rearrange("(p c) n -> p c n", c=KC)[:, :, 512 * i:512 * i + n])
                i = W_IN_LOADS
                load(l, i, slot3(i % RING, 4, D), w_ua[l].rearrange("(c p) n -> p c n", p=P))
                for j in range(WUH_PARTS):
                    i += 1
                    load(l, i, slot3(i % RING, 2, D), w_uh[l].rearrange("(c p) n -> p c n", p=P)[:, 2 * j:2 * j + 2, :])
                for j in range(WO_PARTS):
                    i += 1
                    load(l, i, slot3(i % RING, 2, D), w_o[l].rearrange("(c p) n -> p c n", p=P)[:, 2 * j:2 * j + 2, :])

                for e in range(2):
                    for k, d, src in expert_loads(l, e, 3 * e):
                        load(l, MIX_LOADS + 3 * e + k, d, src)

                def expert_in(e, g):
                    for k, d, src in expert_loads(l, e, 3 * g):
                        wait(sp, "down_mm" if k == 2 else "gu_mm", l, e - 2)
                        sp.dma_start(d, src).then_inc(landed[3 * g + k], 16)

                for k, d, src in expert_loads(l, 2, 6):
                    wait(sp, *(("ek_in", l, 16), ("o_mm", l, 8), ("merged_in", l, 4))[k])
                    if k == 0:
                        wait(sp, "at_mm", l, 8)
                    sp.dma_start(d, src).then_inc(landed[6 + k], 16)
                with sp.Fori(0, (NE - 5) // 3) as i:
                    for g in range(3):
                        expert_in(i * 3 + 3 + g, g)
                for e in range(NE - 2, NE):
                    expert_in(e, e % 3)

                wait(sp, "route_in", l, 1)
                over = sp.value_load(ctl[0:1, 0:1], min_val=0, max_val=MAX_OVER)
                with sp.If(over > 0):
                    with sp.Fori(0, MAX_OVER) as j:
                        with sp.If(j < over):
                            sp.wait_ge(OV[l]["down"], j + 1)
                            e = sp.value_load(ctl[0:1, bass.ds(j + 1, 1)], min_val=0, max_val=NE - 1)
                            for k, d, src in expert_loads(l, e, 0):
                                sp.dma_start(d, src).then_inc(OV[l]["landed"], 16)
                        with sp.Else():
                            sp.nop()
                    sp.wait_ge(s_summed, l + 1)
                    sp.nop()
                with sp.Else():
                    sp.nop()
            wait(sp, "xn_in", DEPTH, 1)
            sp.dma_start(t["out"].rearrange("b (t p) d -> p (b t) d", p=P), xn[:]).then_inc(s_out, 16)
            sp.wait_ge(s_out, 16)

        @block.tensor
        def _(pe):
            def arrived(l, n):
                pe.wait_ge(landed[n % RING], 16 * (l * (MIX_ROUNDS + (NE + 2) // 3) + n // RING + 1))

            def turn(l, half):
                for g in range(4):
                    tt, q = g // 2, g % 2
                    if q == 0:
                        wait(pe, "xn_in", l, 1 if half == 0 else 2 + tt)
                    if g >= 2:
                        wait(pe, "h_in", l, 4 * half + g - 1)
                    for c in range(4):
                        m = pe.transpose(TB[g % 2][:, P * c:P * c + P], xn[:, tt, 4 * q + c::KC], ident)
                    inc(m, "turned")

            def unit(l, u):
                if u >= 2:
                    v = u - 2
                    if v in DVE_UNITS:
                        wait(pe, "unit_done", l, DVE_UNITS.index(v) + 1)
                    else:
                        wait(pe, "unit_seen", l, v + 1)
                if u == 0:
                    wait(pe, "h_in", l, 4)
                if u % 2 == 0:
                    arrived(l, u // 2)
                b = UB[u % 2]
                w = slot3((u // 2) % RING, KC, min(512, IN_W - 512 * (u // 2)))
                c0 = 256 * (u % 2)
                for a in range(2):
                    for c in range(KC):
                        if u in TOKEN_UNITS:
                            m = pe.matmul(b[:, 256 * a:256 * a + 256], hT[:, c, P * a:P * a + P], w[:, c, c0:c0 + 256],
                                          start=(c == 0), stop=(c == KC - 1))
                        else:
                            m = pe.matmul(b[:, 256 * a:256 * a + 256], w[:, c, c0 + P * a:c0 + P * a + P], hT[:, c, :],
                                          start=(c == 0), stop=(c == KC - 1))
                inc(m, "unit_mm")

            def qk_turn(l):
                wait(pe, "roped_in", l, 1)
                for tt in range(NT):
                    for c in range(4):
                        m = pe.transpose(TB[tt][:, P * c:P * c + P], roped[:, tt, P * c:P * c + P], ident)
                    inc(m, "qk_turned")
                wait(pe, "qkT_in", l, 1)
                for tt in range(NT):
                    for kv in range(KVH):
                        n = 2 * tt + kv
                        m = pe.transpose(TB[0][:, P * n:P * n + P], roped[:, tt, 512 + P * kv:512 + P * kv + P], ident)
                inc(m, "qk_turned")

            def scores(l, g):
                b, kv = g // 2, g % 2
                if g == 0:
                    wait(pe, "qkT_in", l, 3)
                else:
                    wait(pe, "prob_exp", l, g)
                for hh in range(2):
                    for par in range(2):
                        h0 = 64 * par
                        m = pe.matmul(SB[par][:, 256 * hh:256 * hh + 256], qT[h0:h0 + 64, b, 2 * kv + hh, :],
                                      kT[h0:h0 + 64, :, kv, :], start=True, stop=True)
                inc(m, "score_mm")

            def prob_turn(l, g):
                wait(pe, "prob_in", l, g + 1)
                if g >= 1:
                    wait(pe, "prob_out", l, g)
                for j in range(NT):
                    for n in range(4):
                        m = pe.transpose(TB[j][:, P * n:P * n + P], prob[:, g % 2, n, P * j:P * j + P], ident)
                inc(m, "prob_turned")

            def pv(l, g):
                wait(pe, "prob_out", l, g + 1)
                if g >= 2:
                    wait(pe, "ya_in", l, g - 1)
                kv = g % 2
                for par in range(2):
                    for j in range(NT):
                        m = pe.matmul(OB[g % 2][64 * par:64 * par + 64, 0:256], vv[:, j, 64 * kv:64 * kv + 64],
                                      probT[:, j, 256 * par:256 * par + 256], start=(j == 0), stop=(j == NT - 1))
                inc(m, "pv_mm")

            def kend_turn(l):
                wait(pe, "kend_in", l, 1)
                wait(pe, "prob_out", l, 4)
                for r in range(2):
                    for h in range(HH):
                        m = pe.transpose(TB[r][:, P * h:P * h + P], kend[:, 4 * r + h, :], ident)
                    inc(m, "kend_turned")

            def states(l):
                wait(pe, "unit_seen", l, 11)
                for r in range(2):
                    wait(pe, "kendT_in", l, r + 1)
                    for h in range(HH):
                        m = pe.matmul(TB[r][:, P * h:P * h + P], kendT[:, 4 * r + h, :], hv[:, r, P * h:P * h + P],
                                      start=True, stop=True)
                    inc(m, "state_mm")

            def intra(l, n):
                T, h = n // HH, n % HH
                if n >= 2:
                    wait(pe, "at_in", l, n - 1)
                for r in range(2):
                    wait(pe, "ek_in", l, 2 * n + r + 1)
                    if n == 0:
                        wait(pe, "qe_in", l, r + 1)
                    for i in range(NCH):
                        m = pe.matmul(SB[n % 2][:, P * r + CHUNK * i:P * r + CHUNK * i + CHUNK], ek[:, r, i, :],
                                      qe[:, r, NT * h + T, i, :], start=True, stop=True)
                inc(m, "at_mm")

            def outputs(l, n):
                T, h = n // HH, n % HH
                wait(pe, "at_in", l, n + 1)
                if n == 0:
                    wait(pe, "state_in", l, 2)
                    wait(pe, "ya_in", l, 4)
                o = OB[T][:, P * h:P * h + P]
                v = hv[:, T, P * h:P * h + P]
                pe.matmul(o, at_sb[:, n % 2, 0, :], v, start=True, stop=False)
                pe.matmul(o, at_sb[:, n % 2, 1, :], v, start=False, stop=False)
                r = 0 if T == 1 else 1
                inc(pe.matmul(o, qc[:, r, h, :], state[:, r, h, :], start=False, stop=True), "o_mm")

            def y_turn(l, T):
                wait(pe, "y_ready", l, T + 1)
                wait(pe, "state_in", l, T + 1)
                for c in range(4):
                    m = pe.transpose(TB[T][:, P * c:P * c + P], og[:, T, P * c:P * c + P], ident)
                inc(m, "y_turned")

            def up_attn(l, i):
                if i == 0:
                    arrived(l, W_IN_LOADS)
                wait(pe, "unit_seen", l, UNITS)
                if i >= 2:
                    wait(pe, "merged_in", l, i - 1)
                w = slot3(W_IN_LOADS % RING, 4, D)
                for a in range(2):
                    f = P * (2 * i + a)
                    for c in range(4):
                        m = pe.matmul(UB[i % 2][:, 256 * a:256 * a + 256], w[:, c, f:f + P], yaT[:, c, :],
                                      start=(c == 0), stop=(c == 3))
                inc(m, "ua_mm")

            def up_hgrn(l, i):
                if i == 0:
                    for j in range(WUH_PARTS):
                        arrived(l, W_IN_LOADS + 1 + j)
                    wait(pe, "yT_in", l, 2)
                if i >= 2:
                    wait(pe, "merged_in", l, i - 1)
                for a in range(2):
                    f = P * (2 * i + a)
                    for c in range(4):
                        w = slot3((W_IN_LOADS + 1 + c // 2) % RING, 2, D)
                        m = pe.matmul(SB[i % 2][:, 256 * a:256 * a + 256], w[:, c % 2, f:f + P], yhT[:, c, :],
                                      start=(c == 0), stop=(c == 3))
                inc(m, "uh_mm")

            def mix_out(l):
                wait(pe, "merged_in", l, 4)
                for tt in range(NT):
                    for c in range(KC):
                        n = W_IN_LOADS + 1 + WUH_PARTS + c // 2
                        if tt == 0 and c % 2 == 0:
                            arrived(l, n)
                        w = slot3(n % RING, 2, D)
                        for half in range(2):
                            m = pe.matmul(ACC[tt][half][:, :], merged[:, c, P * tt:P * tt + P],
                                          w[:, c % 2, 512 * half:512 * half + 512], start=(c == 0), stop=(c == KC - 1))
                        if tt == NT - 1 and c % 2 == 1:
                            inc(m, "wout_mm")
                    if tt == 0:
                        inc(m, "wout0_mm")

            def route(l):
                wait(pe, "h_in", l, 8)
                if l == 0:
                    pe.wait_ge(s_wr, 16 * 5)
                else:
                    pe.wait_ge(s_wr, 2 * 16 * 5)
                for tt in range(NT):
                    for c in range(KC):
                        m = pe.matmul(SB[0][:, 64 * tt:64 * tt + 36], hT[:, c, P * tt:P * tt + P], wr[:, c, :],
                                      start=(c == 0), stop=(c == KC - 1))
                inc(m, "logit_mm")
                wait(pe, "mask_in", l, 1)
                one, bef = C("ones"), C("before")
                pe.matmul(SB[1][:, 0:NE], bef, mh[:, 0, :], start=True, stop=True)
                pe.matmul(SB[1][:, NE:2 * NE], bef, mh[:, 1, :], start=True, stop=False)
                pe.matmul(SB[1][:, NE:2 * NE], one, mh[:, 0, :], start=False, stop=True)
                pe.matmul(SB[1][:, 2 * NE:3 * NE], one, mh[:, 0, :], start=True, stop=False)
                inc(pe.matmul(SB[1][:, 2 * NE:3 * NE], one, mh[:, 1, :], start=False, stop=True), "pos_mm")

            def gather(b):
                for tt in range(NT):
                    for q in range(4):
                        m = pe.matmul(part(GB, 0)[32 * q:32 * q + 32, :], sel[:, b, tt, :],
                                      xn[:, tt, :].rearrange("p (f c) -> p c f", c=KC)[:, 2 * q:2 * q + 2, :],
                                      start=(tt == 0), stop=(tt == NT - 1))
                return m

            def rows_turn():
                for half in range(2):
                    m = pe.transpose(part(GB, 1)[:, P * half:P * half + P], hrow[:, P * half:P * half + P], ident)
                return m

            def gate_up(b, s0):
                wg, wu = slot3(s0, KC, FE), slot3(s0 + 1, KC, FE)
                for c in range(KC):
                    for q in range(4):
                        m = pe.matmul(part(HB, b)[32 * q:32 * q + 32, :], hs[:, b, c % 2, c // 2, :],
                                      (wg, wu)[q // 2][:, c, 256 * (q % 2):256 * (q % 2) + 256],
                                      start=(c == 0), stop=(c == KC - 1))
                return m

            def sel_turn(b):
                for tt in range(NT):
                    m = pe.transpose(ST_B[:, P * tt:P * tt + P], selw[:, b, tt, :, :].rearrange("p q s -> p (q s)"), ident)
                return m

            def hid_turn(b):
                for j in range(2):
                    m = pe.transpose(HT_B[:, P * j:P * j + P], hid[:, b, j::2], ident)
                return m

            def down(b, s0):
                wd = slot(s0 + 2).rearrange("p (h j d) -> p h j d", h=2, j=2)
                for k in range(4):
                    half, j = k // 2, k % 2
                    for q in range(4):
                        m = pe.matmul(part(YB, b)[32 * q:32 * q + 32, :], hidT[:, b, j, 32 * half:32 * half + 32],
                                      wd[:, half, j, 256 * q:256 * q + 256], start=(k == 0), stop=(k == 3))
                return m

            def add_up(b, first):
                for tt in range(NT):
                    for q in range(4):
                        m = pe.matmul(part(SUMS[q], tt), selT[32 * q:32 * q + 32, b, tt, :],
                                      ysb[32 * q:32 * q + 32, b, :], start=(first and tt == 0), stop=True,
                                      skip_group_check=True)
                return m

            def expert(l, e, third, g, b, first=False, second=False, last=False):
                rounds, before = ((MIX_ROUNDS + (NE + 2) // 3, MIX_ROUNDS) if g < 2 else ((NE - 2) // 3, 0))
                count = (third + l * rounds + before + 1) * 16
                for k in range(2):
                    pe.wait_ge(landed[3 * g + k], count)
                wait(pe, "hs_in", l, e + 1)
                if not (first or second):
                    wait(pe, "hid_in", l, e - 1)
                inc(gate_up(b, 3 * g), "gu_mm")
                wait(pe, "selw_in", l, e + 1)
                inc(sel_turn(b), "sel_turned")
                if not first:
                    wait(pe, "y_in", l, e)
                    inc(add_up(1 - b, second), "sum_mm")
                if not last:
                    wait(pe, "sel_in", l, e + 2)
                    if not first:
                        wait(pe, "hs_in", l, e)
                    inc(gather(1 - b), "gather_mm")
                wait(pe, "selT_in", l, e + 1)
                wait(pe, "hid_in", l, e + 1)
                inc(hid_turn(b), "hid_turned")
                if not last:
                    wait(pe, "rows_in", l, e + 2)
                    inc(rows_turn(), "rows_turned")
                wait(pe, "hidT_in", l, e + 1)
                if not (first or second):
                    wait(pe, "y_in", l, e - 1)
                pe.wait_ge(landed[3 * g + 2], count)
                inc(down(b, 3 * g), "down_mm")

            pe.wait_ge(s_head, 16)
            for l in range(DEPTH):
                turn(l, 0)
                for u in range(4):
                    unit(l, u)
                    if l == 0 and u == 0:
                        pe.wait_ge(s_const, 16 * 7)
                        pe.transpose(TB[0][:, 0:24], rows[:, :], ident[0:24, 0:24]).then_inc(s_lbt, 1)
                        pe.wait_ge(s_lb, 1)
                qk_turn(l)
                unit(l, 4)
                scores(l, 0)
                unit(l, 5)
                for g in range(4):
                    prob_turn(l, g)
                    if g < 3:
                        scores(l, g + 1)
                    pv(l, g)
                    unit(l, 6 + g)
                unit(l, 10)
                kend_turn(l)
                unit(l, 11)
                states(l)
                unit(l, 12)
                for n in range(8):
                    intra(l, n)
                    unit(l, 13 + n)
                    outputs(l, n)
                    if n == 5:
                        y_turn(l, 0)
                up_attn(l, 0)
                up_attn(l, 1)
                y_turn(l, 1)
                for i in range(4):
                    up_hgrn(l, i)
                    if i < 2:
                        up_attn(l, i + 2)
                mix_out(l)
                turn(l, 1)
                route(l)
                wait(pe, "sel_in", l, 1)
                inc(gather(0), "gather_mm")
                wait(pe, "rows_in", l, 1)
                inc(rows_turn(), "rows_turned")
                for e in range(FIRST_E):
                    expert(l, e, 0, e, e, first=(e == 0), second=(e == 1))
                with pe.Fori(0, LOOPS_E) as i:
                    for k in range(FIRST_E, FIRST_E + STEP_E):
                        expert(l, i * STEP_E + k, i * 2 + k // 3, k % 3, k % 2)
                for e in range(NE - LAST_E, NE):
                    expert(l, e, e // 3, e % 3, e % 2, last=(e == NE - 1))
                wait(pe, "y_in", l, NE)
                inc(add_up(1, False), "sum_mm")

                ov = OV[l]
                wait(pe, "route_in", l, 1)
                over = pe.value_load(ctl[0:1, 0:1], min_val=0, max_val=MAX_OVER)
                pe.sem_inc(ov["down"], 1)
                with pe.If(over > 0):
                    with pe.Fori(0, MAX_OVER) as j:
                        with pe.If(j < over):
                            pe.wait_ge(ov["sel"], j + 1)
                            gather(0).then_inc(ov["gather"], 1)
                            pe.wait_ge(ov["rows"], j + 1)
                            rows_turn().then_inc(ov["rows_turned"], 1)
                            pe.wait_ge(ov["hs"], j + 1)
                            pe.wait_ge(ov["landed"], (j + 1) * 48)
                            gate_up(0, 0).then_inc(ov["gu"], 1)
                            pe.wait_ge(ov["selw"], j + 1)
                            sel_turn(0).then_inc(ov["sel_turned"], 1)
                            pe.wait_ge(ov["selT"], j + 1)
                            pe.wait_ge(ov["hid"], j + 1)
                            hid_turn(0).then_inc(ov["turned"], 1)
                            pe.wait_ge(ov["hidT"], j + 1)
                            down(0, 0).then_inc(ov["down"], 1)
                            pe.wait_ge(ov["y"], j + 1)
                            add_up(0, False).then_inc(ov["sum"], 1)
                        with pe.Else():
                            pe.nop()
                    pe.wait_ge(ov["sum"], over)
                with pe.Else():
                    pe.nop()
                pe.sem_inc(s_summed, 1)

        @block.scalar
        def _(act):
            A = nc.scalar.activation
            steps = [0]
            one = C("ones")[:, 0:1]

            def link(ins):
                steps[0] += 1
                ins.then_inc(s_act, 1)
                act.wait_ge(s_act, steps[0])

            def sigmoid(ap):
                link(A(ap, ap, ACT.Ln, bias=one))
                inc(A(ap, ap, ACT.Exp, scale=-1.0), "sigmoid")

            def squares(l, half):
                if half == 0 and l > 0:
                    wait(act, "x_done", l - 1, 1)
                if half == 0 and l == 0:
                    act.wait_ge(s_x, 16)
                for tt in range(NT):
                    if half == 1:
                        wait(act, "x_mixed", l, tt + 1)
                    m = A(xn[:, tt, :], x[:, tt, :], ACT.Square, accum_out=ss[:, tt:tt + 1])
                    if half == 1:
                        inc(m, "squares")
                        root(l, 4 + tt, tt, tt + 1)
                if half == 0:
                    inc(m, "squares")

            def root(l, k, a, b):
                wait(act, "mean_in", l, k)
                inc(A(rs1[:, a:b], rs0[:, a:b], ACT.Ln), "root_log")
                wait(act, "root_log", l, k)
                inc(A(rs1[:, a:b], rs1[:, a:b], ACT.Exp, scale=-0.5), "root")

            def unit(l, u):
                wait(act, "unit_mm", l, u + 1)
                b = UB[u % 2][:, :]
                b2 = b.rearrange("p (a n) -> p a n", a=2)
                if u < 2:
                    if l > 0:
                        wait(act, "x_done", l - 1, 1)
                    m = A(raw[:, :, 256 * u:256 * u + 256], b2, ACT.Copy)
                elif u == 2:
                    A(raw[:, :, 512:640], b2[:, :, 0:P], ACT.Copy)
                    m = A(vv[:, :, :], b2[:, :, P:2 * P], ACT.Copy)
                elif u in (3, 4):
                    dst = qd[:, 2 * (u - 3):2 * (u - 3) + 2, :]
                elif u in Z_UNITS:
                    z = u - 5
                    if z >= 2:
                        wait(act, "b_in", l, z - 1)
                    dst, b2 = ft[:, z % 2, :], b
                elif u in (9, 10):
                    m = A(hv[:, :, 256 * (u - 9):256 * (u - 9) + 256], b2, ACT.Copy)
                elif u in (11, 12):
                    dst = og[:, :, 256 * (u - 11):256 * (u - 11) + 256]
                else:
                    if u == 13:
                        wait(act, "pv_mm", l, 4)
                    dst = gate[:, 2 * (u - 13):2 * (u - 13) + 2, :]
                if u not in SIGMOID_UNITS:
                    inc(m, "unit_seen")
                else:
                    inc(A(dst, b2, ACT.Exp, scale=-1.0), "unit_seen")
                    wait(act, "unit_seen", l, u + 1)
                    sigmoid(dst)

            def log_f(l, z):
                wait(act, "f_in", l, z + 1)
                if z >= 1:
                    wait(act, "b_in", l, z)
                wait(act, "cleared", l, 1)
                inc(A(logf, ft[:, z % 2, :], ACT.Ln), "f_log")

            def probs(l, g):
                wait(act, "sunk", l, g + 1)
                if g >= 2:
                    wait(act, "prob_turned", l, g - 1)
                for n in range(4):
                    par, hh = n // 2, n % 2
                    A(prob[:, g % 2, n, :], SB[par][:, 256 * hh:256 * hh + 256], ACT.Exp, scale=1.0,
                      bias=anm[:, g % 2, n:n + 1], accum_out=asum[:, g % 2, n:n + 1])
                inc(A(aexp[:, g % 2, :], adif[:, g % 2, :], ACT.Exp), "prob_exp")

            def prob_out(l, g):
                wait(act, "prob_turned", l, g + 1)
                if g >= 1:
                    wait(act, "pv_mm", l, g)
                for j in range(NT):
                    m = A(probT[:, j, :], TB[j][:, :], ACT.Copy)
                inc(m, "prob_out")

            def kend_exp(l):
                wait(act, "b_in", l, 4)
                for r in range(2):
                    for h in range(HH):
                        hT_ = NT * h + r
                        b, edge = ((bd[:, 0, hT_, 1:P + 1], bd[:, 0, hT_, P:P + 1]) if r == 0 else
                                   (bd[:, 1, hT_, 0:P], bd[:, 1, hT_, 0:1]))
                        m = A(kend[:, 4 * r + h, :], b, ACT.Exp, scale=-1.0, bias=edge)
                inc(m, "kend_exp")

            def q_exp(l):
                for r in range(2):
                    wait(act, "qe_sub", l, r + 1)
                    inc(A(xn[:, r, :], xn[:, r, :], ACT.Exp), "qe_exp")
                    b = bd[:, r, 1 - r::NT, :]
                    inc(A(qc[:, r, :, :], b[:, :, 1 - r:P + 1 - r], ACT.Exp), "qc_exp")

            def kendT(l):
                for r in range(2):
                    wait(act, "kend_turned", l, r + 1)
                    inc(A(ek[:, 1, 4 * r:4 * r + 4, :], TB[r][:, :].rearrange("p (h s) -> p h s", h=HH), ACT.Copy), "kendT_in")

            def state_in(l):
                for r in range(2):
                    wait(act, "state_mm", l, r + 1)
                    inc(A(ft[:, r, :], TB[r][:, :], ACT.Copy), "state_in")

            def ek_exp(l, n):
                T, h = n // HH, n % HH
                for r in range(2):
                    if n == 0:
                        wait(act, "state_mm", l, 2)
                    else:
                        wait(act, "at_mm", l, n)
                    b = bd[:, r, NT * h + T, :]
                    for i in range(NCH):
                        if r == 0:
                            m = A(ek[:, 0, i, 0:CHUNK * (i + 1)], b[:, 1:CHUNK * (i + 1) + 1], ACT.Exp, scale=-1.0,
                                  bias=b[:, CHUNK * i:CHUNK * i + 1])
                        else:
                            m = A(ek[:, 1, i, CHUNK * i:P], b[:, CHUNK * i:P], ACT.Exp, scale=-1.0,
                                  bias=b[:, CHUNK * (i + 1):CHUNK * (i + 1) + 1])
                    inc(m, "ek_exp")

            def o_square(l, T):
                wait(act, "o_mm", l, 4 * T + 4)
                inc(A(junk[:, :], OB[T][:, :], ACT.Square, accum_out=ss[:, T:T + 1]), "osq")
                root(l, 2 + T, T, T + 1)

            def gate_out(b):
                A(eg[0:64, b, :], part(HB, b)[0:64, :], ACT.Exp, scale=-1.0)
                return A(up[0:64, b, :], part(HB, b)[64:128, :], ACT.Copy)

            def selT_out(b):
                return A(selT[:, b, :, :], ST_B.rearrange("p (t s) -> p t s", t=NT), ACT.Copy)

            def rows_out():
                return A(hrow, part(GB, 0), ACT.Copy)

            def hidT_out(b):
                return A(hidT[:, b, :, :], HT_B.rearrange("p (j s) -> p j s", j=2)[:, :, 0:64], ACT.Copy)

            def expert(l, e, b, early=False, last=False):
                wait(act, "gu_mm", l, e + 1)
                if not early:
                    wait(act, "hid_in", l, e - 1)
                inc(gate_out(b), "gu_seen")
                wait(act, "sel_turned", l, e + 1)
                if not early:
                    wait(act, "sum_mm", l, e - 1)
                inc(selT_out(b), "selT_in")
                if not last:
                    wait(act, "gather_mm", l, e + 2)
                    inc(rows_out(), "rows_in")
                wait(act, "hid_turned", l, e + 1)
                inc(hidT_out(b), "hidT_in")
                wait(act, "down_mm", l, e + 1)
                inc(A(ysb[:, b, :], part(YB, b), ACT.Copy), "y_in")

            nc.scalar.preload_act_table_set("natural_log_exp_and_others")
            for ap, src in ((gains[:, 0:DEPTH, :], t["attn_norm_g"].rearrange("l (p c) -> p l c", c=KC)),
                            (gains[:, DEPTH:, :], t["ffn_norm_g"].rearrange("l (p c) -> p l c", c=KC)),
                            (rows[0:16, :], t["hgrn_lb_table"].rearrange("l r (h p) -> (l r h) p", p=HK)),
                            (rows[16:24, :], t["hgrn_norm_g"].rearrange("l (h p) -> (l h) p", p=HK)),
                            (sink[:], spread(t["sink_logits"])),
                            (bias[:, :, 0:GROUPS], spread(t["b_router_group"])),
                            (bias[:, :, GROUPS:], spread(t["b_router_expert"].rearrange("l g e -> l (g e)")))):
                act.dma_start(ap, src).then_inc(s_const, 16)
            for l in range(DEPTH):
                squares(l, 0)
                root(l, 1, 0, NT)
                if l == 0:
                    act.wait_ge(s_head, 16)
                for u in range(5):
                    unit(l, u)
                    if l == 0 and u == 0:
                        act.wait_ge(s_lb, 2)
                        A(cols[:, 0:16], cols[:, 0:16], ACT.Exp).then_inc(s_lbe, 1)
                probs(l, 0)
                unit(l, 5)
                for g in range(4):
                    prob_out(l, g)
                    if g == 0:
                        log_f(l, 0)
                    if g < 3:
                        probs(l, g + 1)
                    unit(l, 6 + g)
                    if g < 3:
                        log_f(l, g + 1)
                kend_exp(l)
                q_exp(l)
                unit(l, 10)
                kendT(l)
                unit(l, 11)
                state_in(l)
                ek_exp(l, 0)
                unit(l, 12)
                for n in range(8):
                    if n < 7:
                        ek_exp(l, n + 1)
                    unit(l, 13 + n)
                    if n == 4:
                        o_square(l, 0)
                o_square(l, 1)
                squares(l, 1)
                wait(act, "gsub", l, 1)
                inc(A(gexp, gexp, ACT.Exp), "gexp")
                wait(act, "e2sub", l, 1)
                inc(A(e2, e2, ACT.Exp), "e2exp")
                wait(act, "gather_mm", l, 1)
                inc(rows_out(), "rows_in")
                for e in range(2):
                    expert(l, e, e, early=True)
                with act.Fori(1, NE // 2 - 1) as i:
                    for b in range(2):
                        expert(l, i * 2 + b, b)
                for e in range(NE - 2, NE):
                    expert(l, e, e % 2, last=(e == NE - 1))
                ov = OV[l]
                wait(act, "route_in", l, 1)
                over = act.value_load(ctl[0:1, 0:1], min_val=0, max_val=MAX_OVER)
                wait(act, "sum_mm", l, NE)
                with act.If(over > 0):
                    with act.Fori(0, MAX_OVER) as j:
                        with act.If(j < over):
                            act.wait_ge(ov["gather"], j + 1)
                            rows_out().then_inc(ov["rows"], 1)
                            act.wait_ge(ov["gu"], j + 1)
                            gate_out(0).then_inc(ov["seen"], 1)
                            act.wait_ge(ov["sel_turned"], j + 1)
                            selT_out(0).then_inc(ov["selT"], 1)
                            act.wait_ge(ov["turned"], j + 1)
                            hidT_out(0).then_inc(ov["hidT"], 1)
                            act.wait_ge(ov["down"], j + 2)
                            A(ysb[:, 0, :], part(YB, 0), ACT.Copy).then_inc(ov["y"], 1)
                        with act.Else():
                            act.nop()
                with act.Else():
                    act.nop()
            squares(DEPTH, 0)
            root(DEPTH, 1, 0, NT)

        @block.vector
        def _(dve):
            V = nc.vector
            step = [0]

            def link(ins):
                step[0] += 1
                ins.then_inc(s_dve, 1)
                dve.wait_ge(s_dve, step[0])

            def bc(ap, n):
                return ap.unsqueeze(len(ap.shape)).broadcast_to([*ap.shape, n])

            def inverse_root(l, k, a, b, n):
                if k in (1, 4, 5):
                    wait(dve, "squares", l, max(1, k - 2))
                else:
                    wait(dve, "osq", l, k - 1)
                v, y, u = rs0[:, a:b], rs1[:, a:b], rs2[:, a:b]
                inc(V.tensor_scalar(v, ss[:, a:b], 1.0 / n, EPS, ALU.mult, ALU.add), "mean_in")
                wait(dve, "root", l, k)
                link(V.tensor_tensor(u, y, y, ALU.mult))
                link(V.tensor_tensor(u, u, v, ALU.mult))
                link(V.tensor_scalar(u, u, -0.5, 1.5, ALU.mult, ALU.add))
                link(V.tensor_tensor(rstd[:, a:b], y, u, ALU.mult))

            def normalise(l, half):
                if half == 0:
                    inverse_root(l, 1, 0, NT, D)
                for tt in range(NT):
                    if half == 1:
                        mixed(l, tt)
                        inverse_root(l, 4 + tt, tt, tt + 1, D)
                    m = V.tensor_scalar(xn[:, tt, :], x[:, tt, :], rstd[:, tt:tt + 1], None, ALU.mult)
                    if half == 1:
                        inc(m, "xn_in")
                if half == 0:
                    inc(m, "xn_in")

            def mixed(l, tt):
                wait(dve, "wout0_mm" if tt == 0 else "wout_mm", l, 1 if tt == 0 else WO_PARTS)
                for half in range(2):
                    xs = x[:, tt, 512 * half:512 * half + 512]
                    m = V.tensor_tensor(xs, xs, ACC[tt][half][:, :], ALU.add)
                inc(m, "x_mixed")
                wait(dve, "x_mixed", l, tt + 1)

            def turned(l, half):
                for g in range(4):
                    tt, q = g // 2, g % 2
                    wait(dve, "turned", l, 4 * half + g + 1)
                    inc(V.tensor_tensor(hT[:, 4 * q:4 * q + 4, P * tt:P * tt + P],
                                        TB[g % 2][:, :].rearrange("p (c s) -> p c s", c=4),
                                        bc(gains[:, DEPTH * half + l, 4 * q:4 * q + 4], P), ALU.mult), "h_in")

            def rope(l):
                wait(dve, "unit_seen", l, 3)
                for tt in range(NT):
                    src = raw[:, tt, :].rearrange("p (h a f) -> p h a f", a=2, f=32)
                    t1, t2 = src[:, :, 0, :], src[:, :, 1, :]
                    c = cos[:, tt, :].unsqueeze(1).broadcast_to([P, 10, 32])
                    s = sin[:, tt, :].unsqueeze(1).broadcast_to([P, 10, 32])
                    r0 = rot[:, 0, 320 * tt:320 * tt + 320].rearrange("p (h f) -> p h f", f=32)
                    r1 = rot[:, 1, 320 * tt:320 * tt + 320].rearrange("p (h f) -> p h f", f=32)
                    dq = roped[:, tt, 0:512].rearrange("p (h a f) -> p h a f", a=2, f=32)
                    dk = roped[:, tt, 512:768].rearrange("p (v d a f) -> p v d a f", v=2, d=2, f=32)
                    for a, (u, w, op) in enumerate(((t1, t2, ALU.subtract), (t2, t1, ALU.add))):
                        V.tensor_tensor(r0, u, c, ALU.mult)
                        link(V.tensor_tensor(r1, w, s, ALU.mult))
                        V.tensor_tensor(dq[:, :, a, :], r0[:, 0:8, :], r1[:, 0:8, :], op)
                        V.tensor_tensor(dk[:, :, 0, a, :], r0[:, 8:10, :], r1[:, 8:10, :], op)
                        m = V.tensor_tensor(dk[:, :, 1, a, :], r0[:, 8:10, :], r1[:, 8:10, :], op)
                        if tt == NT - 1 and a == 1:
                            inc(m, "roped_in")
                        else:
                            link(m)

            def qk_in(l):
                for tt in range(NT):
                    wait(dve, "qk_turned", l, tt + 1)
                    inc(V.tensor_scalar(qT[:, tt, :, :], TB[tt][:, :].rearrange("p (c s) -> p c s", c=4), HD ** -0.5, None,
                                        ALU.mult), "qkT_in")
                wait(dve, "qk_turned", l, 3)
                inc(V.tensor_copy(kT[:, :, :, :], TB[0][:, :].rearrange("p (t k s) -> p t k s", t=NT, k=KVH)), "qkT_in")

            def sink_max(l, g):
                b, kv = g // 2, g % 2
                wait(dve, "score_mm", l, g + 1)
                for par in range(2):
                    sc = SB[par][:, :].rearrange("p (h s) -> p h s", h=2)
                    part = sc[:, :, P:2 * P] if b == 0 else sc[:, :, 0:P]
                    mask = C("win0" if b == 0 else "win1").unsqueeze(1).broadcast_to([P, 2, P])
                    link(V.tensor_tensor(part, part, mask, ALU.add))
                for par in range(2):
                    sc = SB[par][:, :].rearrange("p (h s) -> p h s", h=2)
                    link(V.tensor_reduce(amax[:, g % 2, 2 * par:2 * par + 2], sc, AX_X, ALU.max))
                sk = sink[:, l, 4 * kv:4 * kv + 4].rearrange("p (h a) -> p a h", a=2)
                mx, m4 = amax[:, g % 2, :], am[:, g % 2, :]
                link(V.tensor_tensor(m4.rearrange("p (a h) -> p a h", a=2), mx.rearrange("p (a h) -> p a h", a=2), sk, ALU.max))
                link(V.tensor_scalar(anm[:, g % 2, :], m4, -1.0, None, ALU.mult))
                inc(V.tensor_tensor(adif[:, g % 2, :].rearrange("p (a h) -> p a h", a=2), sk,
                                    m4.rearrange("p (a h) -> p a h", a=2), ALU.subtract), "sunk")

            def prob_in(l, g):
                wait(dve, "prob_exp", l, g + 1)
                ad = aden[:, g % 2, :]
                link(V.tensor_tensor(ad, asum[:, g % 2, :], aexp[:, g % 2, :], ALU.add))
                link(V.reciprocal(ad, ad))
                for n in range(4):
                    m = V.tensor_scalar(prob[:, g % 2, n, :], prob[:, g % 2, n, :], ad[:, n:n + 1], None, ALU.mult)
                inc(m, "prob_in")

            def ya_in(l, g):
                b, kv = g // 2, g % 2
                wait(dve, "pv_mm", l, g + 1)
                inc(V.tensor_copy(yaT[:, 2 * kv:2 * kv + 2, P * b:P * b + P],
                                  OB[g % 2][:, 0:256].rearrange("p (c s) -> p c s", c=2)), "ya_in")

            def silu_unit(l, u):
                wait(dve, "sigmoid", l, SIGMOID_UNITS.index(u) + 1)
                b2 = UB[u % 2][:, :].rearrange("p (a n) -> p a n", a=2)
                dst = qd[:, 2 * (u - 3):2 * (u - 3) + 2, :] if u < 5 else og[:, :, 256 * (u - 11):256 * (u - 11) + 256]
                inc(V.tensor_tensor(dst, dst, b2, ALU.mult), "unit_done")

            def forget(l, z):
                r, hh = z // 2, z % 2
                wait(dve, "sigmoid", l, SIGMOID_UNITS.index(5 + z) + 1)
                f = ft[:, z % 2, :]
                for a in range(2):
                    h = 4 * r + 2 * hh + a
                    link(V.tensor_scalar(f[:, 256 * a:256 * a + 256], f[:, 256 * a:256 * a + 256], lbs[:, 0, l, h:h + 1],
                                         lbs[:, 1, l, h:h + 1], ALU.mult, ALU.add))
                V.tensor_scalar(f, f, float(np.exp(LOGF_MIN)), None, ALU.max).then_inc(PEV["f_in"][0], 1)
                wait(dve, "f_in", l, z + 1)
                link(V.tensor_scalar(kd[:, r, 2 * hh:2 * hh + 2, :].rearrange("p a s -> p (a s)"), f, -1.0, 1.0,
                                     ALU.mult, ALU.add))

            def cumulate(l, z):
                r, hh = z // 2, z % 2
                wait(dve, "f_log", l, z + 1)
                wait(dve, "cleared", l, 1)
                for a in range(2):
                    for T in range(NT):
                        lf = logf[:, 256 * a + P * T:256 * a + P * T + P]
                        b = bd[:, r, NT * (2 * hh + a) + T, :]
                        if r == 0:
                            m = V.tensor_tensor_scan(b[:, 1:P + 1], C("ones"), lf, 0.0, ALU.mult, ALU.add)
                        else:
                            m = V.tensor_tensor_scan(b[:, 0:P][:, ::-1], C("ones"), lf[:, ::-1], 0.0, ALU.mult, ALU.add)
                inc(m, "b_in")

            def q_sub(l):
                wait(dve, "b_in", l, 4)
                for r in range(2):
                    b = bd[:, r, :, 1 - r:P + 1 - r].rearrange("p h (c u) -> p h c u", u=CHUNK)
                    edge = bd[:, r, :, CHUNK * r:P + CHUNK * r - (CHUNK - 1):CHUNK] if r == 0 else \
                        bd[:, r, :, CHUNK:P + 1:CHUNK]
                    inc(V.tensor_tensor(qe[:, r, :, :, :], b, bc(edge, CHUNK), ALU.subtract), "qe_sub")

            def q_in(l):
                for r in range(2):
                    wait(dve, "qc_exp", l, r + 1)
                    V.tensor_tensor(qc[:, r, :, :], qc[:, r, :, :], qd[:, :, P * (1 - r):P * (1 - r) + P], ALU.mult)
                    e = xn[:, r, :]
                    inc(V.tensor_tensor(e, e, qd[:, :, :].rearrange("p h s -> p (h s)"), ALU.mult), "qe_in")

            def kend_in(l):
                wait(dve, "kend_exp", l, 1)
                for r in range(2):
                    e = kend[:, 4 * r:4 * r + 4, :]
                    m = V.tensor_tensor(e, e, kd[:, r, :, P * r:P * r + P], ALU.mult)
                inc(m, "kend_in")

            def ek_in(l, n):
                T, h = n // HH, n % HH
                for r in range(2):
                    wait(dve, "ek_exp", l, 2 * n + r + 1)
                    k = kd[:, r, h, P * T:P * T + P].unsqueeze(1).broadcast_to([P, NCH, P])
                    inc(V.tensor_tensor(ek[:, r, :, :], ek[:, r, :, :], k, ALU.mult), "ek_in")

            def at_in(l, n):
                wait(dve, "at_mm", l, n + 1)
                if n >= 2:
                    wait(dve, "o_mm", l, n - 1)
                for r, name in ((0, "tri_f"), (1, "tri_b")):
                    m = V.tensor_tensor(at_sb[:, n % 2, r, :], SB[n % 2][:, P * r:P * r + P], C(name), ALU.mult)
                inc(m, "at_in")

            def y_ready(l, T):
                inverse_root(l, 2 + T, T, T + 1, HW)
                inc(V.scalar_tensor_tensor(out=og[:, T, :], in0=OB[T][:, :], scalar=rstd[:, T:T + 1], in1=og[:, T, :],
                                           op0=ALU.mult, op1=ALU.mult), "y_ready")

            def yT_in(l, T):
                wait(dve, "y_turned", l, T + 1)
                inc(V.tensor_tensor(yhT[:, :, P * T:P * T + P], TB[T][:, :].rearrange("p (c s) -> p c s", c=4),
                                    bc(cols[:, 16 + 4 * l:20 + 4 * l], P), ALU.mult), "yT_in")

            def merge(l, i):
                wait(dve, "sigmoid", l, 16)
                wait(dve, "ua_mm", l, i + 1)
                wait(dve, "uh_mm", l, i + 1)
                ga, gb = gate[:, 2 * i:2 * i + 2, :], gate[:, 8 + 2 * i:8 + 2 * i + 2, :]
                V.tensor_tensor(ga, ga, UB[i % 2][:, :].rearrange("p (a s) -> p a s", a=2), ALU.mult)
                link(V.tensor_tensor(gb, gb, SB[i % 2][:, :].rearrange("p (a s) -> p a s", a=2), ALU.mult))
                inc(V.tensor_tensor(merged[:, 2 * i:2 * i + 2, :], ga, gb, ALU.add), "merged_in")

            def first_of(out, values, best, n):
                tv = tie[:, :, 0:n]
                for tt in range(NT):
                    m = V.scalar_tensor_tensor(out=tv[:, tt, :], in0=values[:, tt, :], scalar=best[:, tt:tt + 1],
                                               in1=C("falling")[:, NE - n:NE], op0=ALU.is_equal, op1=ALU.mult)
                link(m)
                link(V.tensor_reduce(cmax, tv, AX_X, ALU.max))
                link(V.tensor_tensor(out, tv, bc(cmax, n), ALU.is_equal))

            def route(l):
                wait(dve, "logit_mm", l, 1)
                b2 = SB[0][:, 0:128].rearrange("p (t n) -> p t n", t=NT)[:, :, 0:GROUPS + NE]
                link(V.tensor_tensor(lg, b2, bias[:, l, :].unsqueeze(1).broadcast_to([P, NT, GROUPS + NE]), ALU.add))
                g4 = lg[:, :, 0:GROUPS]
                link(V.tensor_reduce(gmax, g4, AX_X, ALU.max))
                inc(V.tensor_tensor(gexp, g4, bc(gmax, GROUPS), ALU.subtract), "gsub")
                first_of(ohg, g4, gmax, GROUPS)
                link(V.tensor_scalar(ohg, ohg, -1.0, -NEG, ALU.add, ALU.mult))
                link(V.tensor_tensor(masked.rearrange("p t (g e) -> p t g e", g=GROUPS),
                                     lg[:, :, GROUPS:].rearrange("p t (g e) -> p t g e", g=GROUPS), bc(ohg, EPG), ALU.add))
                link(V.tensor_reduce(m1, masked, AX_X, ALU.max))
                first_of(m1h, masked, m1, NE)
                link(V.scalar_tensor_tensor(out=masked, in0=m1h, scalar=NEG, in1=masked, op0=ALU.mult, op1=ALU.add))
                link(V.tensor_reduce(m2, masked, AX_X, ALU.max))
                inc(V.tensor_tensor(e2, m2, m1, ALU.subtract), "e2sub")
                first_of(m2h, masked, m2, NE)
                inc(V.tensor_tensor(mh, m1h, m2h, ALU.add), "mask_in")
                wait(dve, "gexp", l, 1)
                link(V.tensor_reduce(psum_g, gexp, AX_X, ALU.add))
                link(V.reciprocal(ptop, psum_g))
                wait(dve, "e2exp", l, 1)
                link(V.tensor_scalar(den2, e2, 1.0, None, ALU.add))
                link(V.reciprocal(den2, den2))
                link(V.tensor_tensor(w1, den2, ptop, ALU.mult))
                link(V.tensor_tensor(w2, w1, e2, ALU.mult))
                wait(dve, "pos_mm", l, 1)
                link(V.scalar_tensor_tensor(out=posm.rearrange("p t e -> p (t e)"), in0=SB[1][:, 0:2 * NE], scalar=1.0,
                                            in1=mh.rearrange("p t e -> p (t e)"), op0=ALU.add, op1=ALU.mult))

            def weights(l):
                for tt in range(NT):
                    V.tensor_scalar(wsel[:, tt, :], m1h[:, tt, :], w1[:, tt:tt + 1], None, ALU.mult)
                link(V.tensor_copy(count, SB[1][:, 2 * NE:3 * NE]))
                for tt in range(NT):
                    m = V.scalar_tensor_tensor(out=wsel[:, tt, :], in0=m2h[:, tt, :], scalar=w2[:, tt:tt + 1],
                                               in1=wsel[:, tt, :], op0=ALU.mult, op1=ALU.add)
                link(m)

            def over_table(l):
                link(V.tensor_tensor(grid2, bc(count, 7), C("limits").unsqueeze(1).broadcast_to([P, NE, 7]), ALU.is_gt))
                link(V.tensor_reduce(novb, grid2, AX_X, ALU.add))
                link(V.tensor_tensor_scan(oend, C("ones")[:, 0:NE], novb, 0.0, ALU.mult, ALU.add))
                link(V.tensor_copy(ctlf[:, 0:1], oend[:, NE - 1:NE]))
                link(V.tensor_tensor(grid, oend.unsqueeze(1).broadcast_to([P, MAX_OVER, NE]), bc(C("over_at"), NE), ALU.is_le))
                link(V.tensor_reduce(ctlf[:, 1:], grid, AX_X, ALU.add))
                link(V.tensor_scalar(ctlf[:, 1:], ctlf[:, 1:], float(NE - 1), None, ALU.min))
                link(V.tensor_tensor(grid, grid, novb.unsqueeze(1).broadcast_to([P, MAX_OVER, NE]), ALU.mult))
                link(V.tensor_reduce(ooff, grid, AX_X, ALU.add))
                link(V.tensor_tensor(ooff, C("over_at"), ooff, ALU.subtract))
                link(V.tensor_scalar(ooff, ooff, 1.0, float(SLOTS), ALU.add, ALU.mult))
                inc(V.tensor_copy(ctl[0:1, :], ctlf[0:1, :]), "route_in")

            def select(b, column, offset=None):
                for tt in range(NT):
                    if offset is None:
                        m = V.tensor_scalar(sel[:, b, tt, :], C("iota"), posm[:, tt, bass.ds(column, 1)], None, ALU.is_equal)
                    else:
                        m = V.tensor_scalar(sel[:, b, tt, :], C("iota"), offset, posm[:, tt, bass.ds(column, 1)],
                                            ALU.add, ALU.is_equal)
                return m

            def weigh(b, column):
                for tt in range(NT):
                    m = V.tensor_scalar(selw[:, b, tt, :, :], sel[:, b, tt, :].unsqueeze(1).broadcast_to([P, 4, SLOTS]),
                                        wsel[:, tt, bass.ds(column, 1)], None, ALU.mult)
                return m

            def tokens_in(l, b):
                return V.tensor_tensor(hs[:, b, :, :, :].rearrange("p h q s -> p (h q) s"),
                                       part(GB, 1).rearrange("p (c s) -> p c s", c=KC),
                                       bc(gains2[:, l, :], SLOTS), ALU.mult)

            def hidden(b, own):
                g = eg[0:64, b, :]
                own(V.tensor_scalar(g, g, 1.0, None, ALU.add))
                own(V.reciprocal(g, g))
                own(V.tensor_tensor(g, g, part(HB, b)[0:64, :], ALU.mult))
                return V.tensor_tensor(hid[0:64, b, :], g, up[0:64, b, :], ALU.mult)

            def expert(l, e, b, own, first=False, second=False, last=False):
                early = first or second
                if not early:
                    wait(dve, "sel_turned", l, e - 1)
                inc(weigh(b, e), "selw_in")
                if not last:
                    if not first:
                        wait(dve, "gather_mm", l, e)
                    inc(select(1 - b, e + 1), "sel_in")
                wait(dve, "gu_seen", l, e + 1)
                if not early:
                    wait(dve, "hid_turned", l, e - 1)
                inc(hidden(b, own), "hid_in")
                if not last:
                    wait(dve, "rows_turned", l, e + 2)
                    if not first:
                        wait(dve, "gu_mm", l, e)
                    inc(tokens_in(l, 1 - b), "hs_in")

            def lower_bounds():
                dve.wait_ge(s_lbt, 1)
                V.tensor_copy(cols[:, :], TB[0][:, 0:24]).then_inc(s_lb, 1)
                dve.wait_ge(s_lb, 1)
                link(V.tensor_tensor(small[:, 128:136], cols[:, 0:8], cols[:, 8:16], ALU.max))
                V.tensor_tensor(cols[:, 0:8], cols[:, 0:8], small[:, 128:136], ALU.subtract)
                V.tensor_tensor(cols[:, 8:16], cols[:, 8:16], small[:, 128:136], ALU.subtract).then_inc(s_lb, 1)
                dve.wait_ge(s_lbe, 1)
                link(V.tensor_tensor(small[:, 128:136], cols[:, 0:8], cols[:, 8:16], ALU.add))
                link(V.reciprocal(small[:, 128:136], small[:, 128:136]))
                link(V.tensor_tensor(cols[:, 0:8], cols[:, 0:8], small[:, 128:136], ALU.mult))
                link(V.tensor_tensor(cols[:, 8:16], cols[:, 8:16], small[:, 128:136], ALU.mult))
                link(V.tensor_tensor(small[:, 136:144], cols[:, 0:8], cols[:, 8:16], ALU.add))
                link(V.tensor_tensor(small[:, 144:152], cols[:, 0:8], cols[:, 0:8], ALU.subtract))
                link(V.tensor_tensor(small[:, 152:160], small[:, 136:144], cols[:, 0:8], ALU.subtract))
                for l in range(DEPTH):
                    lb = small[:, 144 + 8 * l:152 + 8 * l]
                    link(V.tensor_scalar(lbs[:, 0, l, :], lb, -1.0, 1.0, ALU.mult, ALU.add))
                    link(V.tensor_scalar(lbs[:, 1, l, :], lb, 1e-30, None, ALU.max))

            for l in range(DEPTH):
                normalise(l, 0)
                if l == 0:
                    dve.wait_ge(s_const, 16 * 7)
                turned(l, 0)
                if l == 0:
                    for half in range(2):
                        m = V.tensor_copy(gains2[:, :, 4 * half:4 * half + 4], gains[:, DEPTH:, half::2])
                    link(m)
                    lower_bounds()
                rope(l)
                silu_unit(l, 3)
                qk_in(l)
                silu_unit(l, 4)
                sink_max(l, 0)
                prob_in(l, 0)
                forget(l, 0)
                for g in range(4):
                    if g < 3:
                        sink_max(l, g + 1)
                    cumulate(l, g)
                    if g < 3:
                        prob_in(l, g + 1)
                    ya_in(l, g)
                    if g < 3:
                        forget(l, g + 1)
                q_sub(l)
                kend_in(l)
                q_in(l)
                silu_unit(l, 11)
                ek_in(l, 0)
                silu_unit(l, 12)
                for n in range(8):
                    at_in(l, n)
                    if n < 7:
                        ek_in(l, n + 1)
                    if n == 4:
                        y_ready(l, 0)
                    if n == 5:
                        yT_in(l, 0)
                y_ready(l, 1)
                yT_in(l, 1)
                for i in range(4):
                    merge(l, i)
                normalise(l, 1)
                turned(l, 1)
                route(l)
                inc(select(0, 0), "sel_in")
                weights(l)
                wait(dve, "rows_turned", l, 1)
                inc(tokens_in(l, 0), "hs_in")
                over_table(l)
                for e in range(2):
                    expert(l, e, e, link, first=(e == 0), second=(e == 1))
                per = 6
                base = step[0]
                with dve.Fori(1, NE // 2 - 1) as i:
                    done = [0]

                    def own(ins):
                        done[0] += 1
                        ins.then_inc(s_dve, 1)
                        dve.wait_ge(s_dve, i * per + (base - per + done[0]))

                    for b in range(2):
                        expert(l, i * 2 + b, b, own)
                    assert done[0] == per
                step[0] += per * (NE // 2 - 2)
                for e in range(NE - 2, NE):
                    expert(l, e, e % 2, link, last=(e == NE - 1))

                ov = OV[l]
                over = dve.value_load(ctl[0:1, 0:1], min_val=0, max_val=MAX_OVER)
                wait(dve, "sum_mm", l, NE)
                s_own = s_ov[l]
                with dve.If(over > 0):
                    with dve.Fori(0, MAX_OVER) as j:
                        with dve.If(j < over):
                            e = dve.value_load(ctl[0:1, bass.ds(j + 1, 1)], min_val=0, max_val=NE - 1)
                            done = [0]

                            def own(ins):
                                done[0] += 1
                                ins.then_inc(s_own, 1)
                                dve.wait_ge(s_own, j * 4 + done[0])

                            own(select(0, e, ooff[:, bass.ds(j, 1)]))
                            weigh(0, e).then_inc(ov["selw"], 1)
                            dve.sem_inc(ov["sel"], 1)
                            dve.wait_ge(ov["rows_turned"], j + 1)
                            tokens_in(l, 0).then_inc(ov["hs"], 1)
                            dve.wait_ge(ov["seen"], j + 1)
                            dve.wait_ge(ov["sel_turned"], j + 1)
                            hidden(0, own).then_inc(ov["hid"], 1)
                        with dve.Else():
                            dve.nop()
                with dve.Else():
                    dve.nop()

                dve.wait_ge(s_summed, l + 1)
                for q in range(4):
                    xs = x[:, :, 256 * q:256 * q + 256]
                    m = V.tensor_tensor(xs, xs, SUMS[q][:, :].rearrange("p (t n) -> p t n", t=NT), ALU.add)
                inc(m, "x_done")
            inverse_root(DEPTH, 1, 0, NT, D)
            dve.wait_ge(s_fin, 16)
            for tt in range(NT):
                m = V.scalar_tensor_tensor(out=xn[:, tt, :], in0=x[:, tt, :], scalar=rstd[:, tt:tt + 1], in1=fin_g,
                                           op0=ALU.mult, op1=ALU.mult)
            inc(m, "xn_in")

        @block.gpsimd
        def _(pool):
            for l in range(DEPTH):
                if l > 0:
                    wait(pool, "x_done", l - 1, 1)
                for ap in (bd[:, 0, :, 0:1], bd[:, 1, :, P:P + 1], ek[:, :, :, :]):
                    m = pool.memset(ap, 0.0)
                inc(m, "cleared")
                for i, src in enumerate([t["w_router_group"][l].rearrange("(p c) g -> p c g", c=KC)] +
                                        [t["w_router_expert"][l, g].rearrange("(p c) e -> p c e", c=KC)
                                         for g in range(GROUPS)]):
                    a = 0 if i == 0 else GROUPS + EPG * (i - 1)
                    n = GROUPS if i == 0 else EPG
                    pool.dma_start(wr[:, :, a:a + n], src).then_inc(s_wr, 16)
            wait(pool, "sum_mm", DEPTH - 1, NE)
            wait(pool, "x_done", DEPTH - 1, 1)
            pool.dma_start(fin_g, t["final_norm_g"].rearrange("(o n) -> o n", o=1).broadcast_to([P, D])).then_inc(s_fin, 16)


TOKEN_UNITS = (0, 1, 2, 9, 10, 11, 12)
SIGMOID_UNITS = (3, 4, 5, 6, 7, 8, 11, 12, 13, 14, 15, 16, 17, 18, 19, 20)
Z_UNITS = (5, 6, 7, 8)
DVE_UNITS = (3, 4, 11, 12)

_INS = ["x", "attn_norm_g", "w_in", "sink_logits", "hgrn_lb_table", "hgrn_norm_g", "w_up_attn", "w_up_hgrn",
        "w_out", "ffn_norm_g", "w_router_group", "b_router_group", "w_router_expert", "b_router_expert",
        "w_expert_gate", "w_expert_up", "w_expert_down", "final_norm_g"]


def kernel(**inputs):
    import concourse.bacc as _bacc
    from concourse.bass_utils import run_bass_kernel_spmd as _run

    nc = _bacc.Bacc("TRN2", target_bir_lowering=False, num_devices=1)
    arrays = {f"in_{n}": np.ascontiguousarray(inputs[n]) for n in _INS}
    arrays["in_consts"] = constants()
    t = {}
    for n, a in arrays.items():
        t[n[3:]] = nc.dram_tensor(n, a.shape, mybir.dt.from_np(a.dtype), kind="ExternalInput").ap()
    t["out"] = nc.dram_tensor("result", (1, S, D), F32, kind="ExternalOutput").ap()
    layers_program(nc, t)
    r = _run(nc, [arrays], core_ids=[0])
    return r.results[0]["result"]
```

```python
from contextlib import ExitStack

import numpy as np

import concourse.bass as bass
from concourse import mybir

F32 = mybir.dt.float32
I32 = mybir.dt.int32
ALU = mybir.AluOpType
ACT = mybir.ActivationFunctionType
AX_X = mybir.AxisListType.X

P = 128
DEPTH, D, S = 2, 1024, 256
IN_W = 5376
NT = S // P
KC = D // P
HEADS, KVH, HD = 8, 2, 64
HH, HK = 4, 128
HW = HH * HK
CHUNK = 16
NCH = P // CHUNK
GROUPS, EPG = 4, 8
NE = GROUPS * EPG
FE = 512
SLOTS = 32
MAX_OVER = (2 * S) // (SLOTS + 1)
EPS = 1e-6
LOGF_MIN = -4.0
NEG = -1e30

SLOT_W = 4096
RING = 6
UNITS = IN_W // 256
W_IN_LOADS = (IN_W + 511) // 512
WO_PARTS = 2
MIX_LOADS = W_IN_LOADS + 2 + WO_PARTS
DEPTH_E = 3
FIRST_E, LAST_E, STEP_E = 2, 6, 6
LOOPS_E = (NE - FIRST_E - LAST_E) // STEP_E
assert MIX_LOADS % RING == 3 and RING == 2 * 3 and NE % 3 == 2 and FIRST_E + LAST_E + STEP_E * LOOPS_E == NE

CONST = {}
_at = 0
for _name, _n in [("ident", P), ("before", P), ("ones", P), ("win0", P), ("win1", P), ("cos", NT * 32),
                  ("sin", NT * 32), ("tri_f", P), ("tri_b", P), ("iota", SLOTS), ("limits", 7), ("falling", NE),
                  ("over_at", MAX_OVER)]:
    CONST[_name] = (_at, _at + _n)
    _at += _n
CONST_W = _at




def slot_of(l, n):
    return (n + 3 * l) % RING


def third_of(l, g):
    return 2 if g == 2 else slot_of(l, MIX_LOADS + 3 * g) // 3


def mixer_loads(l, s):
    return sum(slot_of(l, n) == s for n in range(MIX_LOADS)) if s < RING else 0


def loads_before(l, s):
    return sum(mixer_loads(k, s) + sum(third_of(k, e % 3) == s // 3 for e in range(NE)) for k in range(l))


def constants():
    c = np.zeros((P, CONST_W), np.float32)

    def put(name, v):
        a, b = CONST[name]
        c[:, a:b] = np.asarray(v, np.float32).reshape(-1, b - a)

    i = np.arange(P)
    put("ident", np.eye(P))
    put("before", i[:, None] < i[None, :])
    put("ones", np.ones((P, P)))
    put("win0", np.where(i[None, :] <= i[:, None], 0.0, NEG))
    put("win1", np.where(i[None, :] >= i[:, None], 0.0, NEG))
    half = HD // 2
    inv = np.float32(10000.0) ** (-np.arange(half, dtype=np.float32) / np.float32(half))
    angle = np.arange(S, dtype=np.float32)[:, None] * inv[None, :].astype(np.float32)
    for name, f in (("cos", np.cos), ("sin", np.sin)):
        put(name, f(angle).astype(np.float32).reshape(NT, P, half).transpose(1, 0, 2).reshape(P, -1))
    put("tri_f", i[:, None] <= i[None, :])
    put("tri_b", i[:, None] >= i[None, :])
    put("iota", 1 + np.arange(SLOTS)[None])
    put("limits", (SLOTS * np.arange(1, 8))[None])
    put("falling", np.arange(NE, 0, -1)[None])
    put("over_at", np.arange(MAX_OVER)[None])
    return c


def layers_program(nc, t):
    ctx = ExitStack()
    with ctx:
        def sb(name, shape, dt=F32):
            return ctx.enter_context(nc.sbuf_tensor(name, shape, dt))

        def sem(name):
            return ctx.enter_context(nc.semaphore(name))

        ring = sb("ring", [P, RING, SLOT_W])
        const = sb("const", [P, CONST_W])
        x = sb("x", [P, NT, D])
        xn = sb("xn", [P, NT, D])
        hT = sb("hT", [P, KC, S])
        gate = sb("gate", [P, 16, S])
        qT = sb("qT", [P, NT, 4, P])
        late0 = sb("late0", [P, SLOT_W])
        late1 = sb("late1", [P, SLOT_W])
        yaT = sb("yaT", [P, 4, S])
        qd = sb("qd", [P, HH, S])
        ft = sb("ft", [P, 2, 512])
        hv = sb("hv", [P, NT, HW])
        og = sb("og", [P, NT, HW])
        at_sb = sb("at_sb", [P, 2, 2, P])
        junk = sb("junk", [P, 512])
        small = sb("small", [P, 256])
        gains = sb("gains", [P, 2 * DEPTH, KC])
        gains2 = sb("gains2", [P, DEPTH, KC])
        rows = sb("rows", [24, P])
        cols = sb("cols", [P, 24])
        lbs = sb("lbs", [P, 2, DEPTH, 8])
        sink = sb("sink", [P, DEPTH, HEADS])
        wr = sb("wr", [P, KC, GROUPS + NE])
        bias = sb("bias", [P, DEPTH, GROUPS + NE])
        ctl = sb("ctl", [1, 1 + MAX_OVER], I32)

        kd = late0[:, 0:2048].rearrange("p (r h s) -> p r h s", r=2, h=HH)
        ek = late0[:, 2048:4096].rearrange("p (r c s) -> p r c s", r=2, c=NCH)
        n_b = 2 * HH * NT * (P + 1)
        bd = late1[:, 0:n_b].rearrange("p (r h s) -> p r h s", r=2, s=P + 1)
        qc = late1[:, n_b:n_b + 1024].rearrange("p (r h s) -> p r h s", r=2, h=HH)
        kT = late1[:, n_b + 1024:n_b + 1536].rearrange("p (t k s) -> p t k s", t=NT, k=KVH)
        vv = late1[:, n_b + 1536:n_b + 1792].rearrange("p (t s) -> p t s", t=NT)

        def C(name):
            a, b = CONST[name]
            return const[:, a:b]

        ident = C("ident")
        cos = C("cos").rearrange("p (t f) -> p t f", t=NT)
        sin = C("sin").rearrange("p (t f) -> p t f", t=NT)

        flat = gate[:, :, :].rearrange("p a b -> p (a b)")
        raw = flat[:, 0:1280].rearrange("p (t n) -> p t n", t=NT)
        rot = flat[:, 1280:2560].rearrange("p (a n) -> p a n", a=2)
        roped = flat[:, 2560:4096].rearrange("p (t n) -> p t n", t=NT)
        prob = flat[:, 0:2048].rearrange("p (g h s) -> p g h s", g=2, h=4)
        probT = flat[:, 2560:3584].rearrange("p (j n) -> p j n", j=NT)
        qe = xn[:, :, :].rearrange("p r (h c u) -> p r h c u", h=HH * NT, u=CHUNK)
        kend = ek[:, 0, :, :]
        kendT = ek[:, 1, :, :]
        logf = ek[:, 1, 0:4, :].rearrange("p a b -> p (a b)")
        state = ft[:, :, :].rearrange("p r (h e) -> p r h e", h=HH)
        yhT = qd
        merged = hT
        qf, ftf = qT[:, :, :, :].rearrange("p t c s -> p (t c s)"), ft[:, :, :].rearrange("p r s -> p (r s)")
        yf = yaT[:, :, :].rearrange("p c s -> p (c s)")
        hs = qf[:, 0:512].rearrange("p (b h q s) -> p b h q s", b=2, h=2, q=4)
        hrow = qd[:, :, :].rearrange("p h s -> p (h s)")[:, 0:256]
        up = qf[:, 512:1024].rearrange("p (b s) -> p b s", b=2)
        hid = ftf[:, 0:512].rearrange("p (b s) -> p b s", b=2)
        hidT = ftf[:, 512:768].rearrange("p (b j s) -> p b j s", b=2, j=2)
        sel = ftf[:, 768:896].rearrange("p (b t s) -> p b t s", b=2, t=NT)
        eg = yf[:, 0:512].rearrange("p (b s) -> p b s", b=2)
        selw = yf[:, 512:1024].rearrange("p (b t q s) -> p b t q s", b=2, t=NT, q=4)
        selT = at_sb[:, :, :, :].rearrange("p b t s -> p b (t s)").rearrange("p b (t s) -> p b t s", t=NT)
        ysb = junk[:, :].rearrange("p (b s) -> p b s", b=2)
        fin_g = hT[:, :, :].rearrange("p c s -> p (c s)")[:, 0:D]

        hvf = hv[:, :, :].rearrange("p t n -> p (t n)")
        ogf = og[:, :, :].rearrange("p t n -> p (t n)")

        def cut(flat_ap, at, *shape):
            n = int(np.prod(shape))
            v = flat_ap[:, at:at + n]
            if len(shape) == 2:
                v = v.rearrange("p (a b) -> p a b", a=shape[0])
            return v

        lg = cut(hvf, 0, NT, GROUPS + NE)
        m1h = cut(hvf, 96, NT, NE)
        m2h = cut(hvf, 160, NT, NE)
        mh = cut(hvf, 224, NT, NE)
        masked = cut(hvf, 288, NT, NE)
        tie = cut(hvf, 352, NT, NE)
        posm = cut(hvf, 416, NT, NE)
        count = cut(hvf, 480, NE)
        novb = cut(hvf, 512, NE)
        oend = cut(hvf, 544, NE)
        wsel = cut(hvf, 576, NT, NE)
        ctlf = cut(hvf, 640, 1 + MAX_OVER)
        ooff = cut(hvf, 656, MAX_OVER)
        ohg = cut(hvf, 672, NT, GROUPS)
        gexp = cut(hvf, 680, NT, GROUPS)
        grid = cut(ogf, 0, MAX_OVER, NE)
        grid2 = cut(ogf, 512, NE, 7)

        def sm(at, n=NT):
            return small[:, at:at + n]

        ss, rs0, rstd, rs1, rs2, ssh = sm(0), sm(2), sm(4), sm(6), sm(28), sm(30)
        ssq = small[:, 32:40].rearrange("p (t q) -> p t q", t=NT)
        gmax, psum_g, cmax, ptop, m1, m2, w1, w2, e2, den2 = (sm(8 + 2 * i) for i in range(10))
        amax, am, anm, adif, aexp, asum, aden = (small[:, 64 + 8 * i:64 + 8 * i + 8].rearrange("p (g h) -> p g h", g=2)
                                                 for i in range(7))

        def bank(name):
            return ctx.enter_context(nc.psum_tensor(name, [P, 512], F32))

        UB = [bank("unit0"), bank("unit1")]
        SB = [bank("score0"), bank("score1")]
        TB = [bank("turn0"), bank("turn1")]
        OB = [bank("out0"), bank("out1")]
        ACC = [UB, OB]
        UA, UH = [TB[0], UB[1], UB[0], TB[1]], SB + OB
        SUMS = UB + OB
        GB, HB, YB = SB[0], SB[1], TB[1]
        COUNT_B = TB[1][:, 0:NE]
        HT_B, ST_B = TB[0][:, 0:256], TB[0][:, 256:512]

        def part(b, par):
            return b[:, 256 * par:256 * par + 256]

        landed = [sem(f"landed{i}") for i in range(3 * DEPTH_E)]
        s_const, s_x, s_wr, s_fin, s_out = (sem(n) for n in ("const_in", "x_in", "router_in", "final_in", "out_done"))
        s_head = sem("head_in")
        PEV = {}
        for n, per in (("turned", 8), ("unit_mm", UNITS), ("qk_turned", 3), ("score_mm", 4), ("prob_turned", 4),
                       ("pv_mm", 4), ("kend_turned", 2), ("state_mm", 2), ("at_mm", 8), ("o_mm", 8),
                       ("y_turned", 2), ("ua_mm", 4), ("uh_mm", 4), ("wout0_mm", 2), ("wout_mm", WO_PARTS), ("logit_mm", 1), ("pos_mm", 1), ("count_mm", 1),
                       ("gather_mm", NE), ("rows_turned", NE), ("gu_mm", NE), ("hid_turned", NE), ("down_mm", NE),
                       ("sel_turned", NE), ("sum_mm", NE - 1),
                       ("sum_last", 4),
                       ("unit_seen", UNITS), ("sigmoid", 16), ("squares", 4), ("prob_exp", 4), ("f_log", 4), ("kend_exp", 1),
                       ("kendT_in", 2), ("state_in", 2), ("ek_exp", 16), ("qe_exp", 2), ("qc_exp", 2), ("osq", 2), ("prob_out", 4),
                       ("gexp", 1), ("e2exp", 1), ("rows_in", NE), ("gu_seen", NE), ("hidT_in", NE), ("y_in", NE), ("selT_in", NE),
                       ("xn_in", 4), ("h_in", 8), ("roped_in", 1), ("qkT_in", 3), ("sunk", 4), ("prob_in", 4),
                       ("ya_in", 4), ("unit_done", 4), ("f_in", 4), ("b_in", 4), ("kend_in", 1), ("ek_in", 16),
                       ("qe_sub", 2), ("qe_in", 2), ("at_in", 8), ("osum_out", 2), ("y_ready", 2), ("yT_in", 2),
                       ("merged_in", 4), ("x_mixed", 3), ("x_done", 4), ("gsub", 1), ("e2sub", 1), ("mask_in", 1),
                       ("route_in", 1), ("sel_in", NE), ("hs_in", NE), ("hid_in", NE), ("selw_in", NE),
                       ("mean_in", 5), ("root_log", 5), ("root", 5),
                       ("cleared", 1)):
            PEV[n] = (sem(n), per)
        s_dve, s_act = sem("dve_step"), sem("act_step")
        s_ov = [sem(f"over_dve_step{l}") for l in range(DEPTH)]
        s_lb, s_lbt, s_lbe = sem("lb_rows"), sem("lb_turned"), sem("lb_exp")
        OV = [{n: sem(f"over_{n}{l}") for n in ("landed", "sel", "gather", "hs", "gu", "seen", "hid", "turned",
                                                "hidT", "rows", "rows_turned", "selw", "sel_turned", "selT", "down", "y", "sum")}
              for l in range(DEPTH)]

        def inc(ins, name):
            ins.then_inc(PEV[name][0], 1)

        def wait(eng, name, l, k):
            s, per = PEV[name]
            eng.wait_ge(s, l * per + k)

        w_in, w_ua, w_uh, w_o = t["w_in"], t["w_up_attn"], t["w_up_hgrn"], t["w_out"]

        def slot(s):
            return ring[:, s, :] if s < RING else (late0[:, :], late1[:, :],
                                                   gate[:, :, :].rearrange("p a b -> p (a b)"))[s - RING]

        def slot3(s, k, n):
            return slot(s)[:, 0:k * n].rearrange("p (c n) -> p c n", c=k)

        def expert_loads(l, e, s0):
            wg, wu, wd = t["w_expert_gate"], t["w_expert_up"], t["w_expert_down"]
            yield 0, slot3(s0, KC, FE), wg[l, e, :, :].rearrange("(p c) f -> p c f", c=KC)
            yield 1, slot3(s0 + 1, KC, FE), wu[l, e, :, :].rearrange("(p c) f -> p c f", c=KC)
            yield 2, slot(s0 + 2).rearrange("p (h n) -> p h n", h=2), \
                wd[l, e, :, :].rearrange("(h p j) d -> p h (j d)", h=2, p=P)

        def spread(ap):
            return ap.rearrange("(o l) n -> o l n", o=1).broadcast_to([P, *ap.shape])

        block = ctx.enter_context(nc.Block())

        @block.sync
        def _(sp):
            sp.dma_start(x[:], t["x"].rearrange("b (t p) d -> p (b t) d", p=P)).then_inc(s_x, 16)
            for ap, src in ((gains[:, 0:DEPTH, :], t["attn_norm_g"].rearrange("l (p c) -> p l c", c=KC)),
                            (gains[:, DEPTH:, :], t["ffn_norm_g"].rearrange("l (p c) -> p l c", c=KC)),
                            (const[:], t["consts"])):
                sp.dma_start(ap, src).then_inc(s_head, 16)

            def wait_used(l, n):
                if n < 0:
                    if l > 0:
                        s = slot_of(l, n)
                        e, k = max(e for e in range(NE) if third_of(l - 1, e % 3) == s // 3), s % 3
                        wait(sp, "down_mm" if k == 2 else "gu_mm", l - 1, e + 1)
                elif n < W_IN_LOADS:
                    wait(sp, "unit_mm", l, min(2 * n + 2, UNITS))
                elif n == W_IN_LOADS:
                    wait(sp, "ua_mm", l, 4)
                elif n == W_IN_LOADS + 1:
                    wait(sp, "uh_mm", l, 4)
                else:
                    wait(sp, "wout_mm", l, n - W_IN_LOADS - 1)

            def load(l, n, dst, src):
                wait_used(l, n - RING)
                sp.dma_start(dst, src).then_inc(landed[slot_of(l, n)], 16)

            for l in range(DEPTH):
                for i in range(W_IN_LOADS):
                    n = min(512, IN_W - 512 * i)
                    if l == 0 and i == 1:
                        sp.wait_ge(s_x, 16)
                    load(l, i, slot3(slot_of(l, i), KC, n),
                         w_in[l].rearrange("(p c) n -> p c n", c=KC)[:, :, 512 * i:512 * i + n])
                for j, w in enumerate((w_ua[l], w_uh[l], w_o[l][0:512, :], w_o[l][512:, :])):
                    i = W_IN_LOADS + j
                    load(l, i, slot3(slot_of(l, i), 4, D), w.rearrange("(c p) n -> p c n", p=P))

                first = [list(expert_loads(l, g, 3 * third_of(l, g))) for g in range(DEPTH_E)]
                for g, k in ((0, 0), (0, 1), (2, 0), (2, 1), (0, 2), (1, 0), (2, 2), (1, 1), (1, 2)):
                    _, d, src = first[g][k]
                    if g < 2:
                        load(l, MIX_LOADS + 3 * g + k, d, src)
                        continue
                    wait(sp, *(("ek_in", l, 16), ("o_mm", l, 8), ("merged_in", l, 4))[k])
                    if k == 0:
                        wait(sp, "at_mm", l, 8)
                    sp.dma_start(d, src).then_inc(landed[6 + k], 16)

                def expert_in(e, g):
                    for k, d, src in expert_loads(l, e, 3 * third_of(l, g)):
                        wait(sp, "down_mm" if k == 2 else "gu_mm", l, e - 2)
                        sp.dma_start(d, src).then_inc(landed[3 * third_of(l, g) + k], 16)

                with sp.Fori(0, (NE - 5) // 3) as i:
                    for g in range(3):
                        expert_in(i * 3 + 3 + g, g)
                for e in range(NE - 2, NE):
                    expert_in(e, e % 3)

                wait(sp, "route_in", l, 1)
                over = sp.value_load(ctl[0:1, 0:1], min_val=0, max_val=MAX_OVER)
                with sp.If(over > 0):
                    wait(sp, "down_mm", l, NE)
                    with sp.Fori(0, MAX_OVER) as j:
                        with sp.If(j < over):
                            sp.wait_ge(OV[l]["down"], j + 1)
                            e = sp.value_load(ctl[0:1, bass.ds(j + 1, 1)], min_val=0, max_val=NE - 1)
                            for k, d, src in expert_loads(l, e, 0):
                                sp.dma_start(d, src).then_inc(OV[l]["landed"], 16)
                        with sp.Else():
                            sp.nop()
                    wait(sp, "sum_last", l, 4)
                    sp.nop()
                with sp.Else():
                    sp.nop()
            for tt in range(NT):
                wait(sp, "xn_in", DEPTH, tt + 1)
                sp.dma_start(t["out"][0, P * tt:P * tt + P, :], xn[:, tt, :]).then_inc(s_out, 16)
            sp.wait_ge(s_out, NT * 16)

        @block.tensor
        def _(pe):
            def arrived(l, n):
                s = slot_of(l, n)
                pe.wait_ge(landed[s], 16 * (loads_before(l, s) + n // RING + 1))

            def turn(l, half, tt):
                for g in range(2 * tt, 2 * tt + 2):
                    q = g % 2
                    if q == 0:
                        wait(pe, "xn_in", l, 2 * half + tt + 1)
                    if g >= 2:
                        wait(pe, "h_in", l, 4 * half + g - 1)
                    for c in range(4):
                        m = pe.transpose(TB[g % 2][:, P * c:P * c + P], xn[:, tt, 4 * q + c::KC], ident)
                    inc(m, "turned")

            def unit(l, u):
                if u >= 2:
                    v = u - 2
                    if v in DVE_UNITS:
                        wait(pe, "unit_done", l, DVE_UNITS.index(v) + 1)
                    else:
                        wait(pe, "unit_seen", l, v + 1)
                if u == 0:
                    wait(pe, "h_in", l, 4)
                if u % 2 == 0:
                    arrived(l, u // 2)
                b = UB[u % 2]
                w = slot3(slot_of(l, u // 2), KC, min(512, IN_W - 512 * (u // 2)))
                c0 = 256 * (u % 2)
                for a in range(2):
                    for c in range(KC):
                        if u in TOKEN_UNITS:
                            m = pe.matmul(b[:, 256 * a:256 * a + 256], hT[:, c, P * a:P * a + P], w[:, c, c0:c0 + 256],
                                          start=(c == 0), stop=(c == KC - 1))
                        else:
                            m = pe.matmul(b[:, 256 * a:256 * a + 256], w[:, c, c0 + P * a:c0 + P * a + P], hT[:, c, :],
                                          start=(c == 0), stop=(c == KC - 1))
                inc(m, "unit_mm")

            def qk_turn(l):
                wait(pe, "roped_in", l, 1)
                for tt in range(NT):
                    for c in range(4):
                        m = pe.transpose(TB[tt][:, P * c:P * c + P], roped[:, tt, P * c:P * c + P], ident)
                    inc(m, "qk_turned")
                wait(pe, "qkT_in", l, 1)
                for tt in range(NT):
                    for kv in range(KVH):
                        n = 2 * tt + kv
                        m = pe.transpose(TB[0][:, P * n:P * n + P], roped[:, tt, 512 + P * kv:512 + P * kv + P], ident)
                inc(m, "qk_turned")

            def scores(l, g):
                b, kv = g // 2, g % 2
                if g == 0:
                    wait(pe, "qkT_in", l, 3)
                else:
                    wait(pe, "prob_exp", l, g)
                for hh in range(2):
                    for par in range(2):
                        h0 = 64 * par
                        m = pe.matmul(SB[par][:, 256 * hh:256 * hh + 256], qT[h0:h0 + 64, b, 2 * kv + hh, :],
                                      kT[h0:h0 + 64, :, kv, :], start=True, stop=True)
                inc(m, "score_mm")

            def prob_turn(l, g):
                wait(pe, "prob_in", l, g + 1)
                if g >= 1:
                    wait(pe, "prob_out", l, g)
                for j in range(NT):
                    for n in range(4):
                        m = pe.transpose(TB[j][:, P * n:P * n + P], prob[:, g % 2, n, P * j:P * j + P], ident)
                inc(m, "prob_turned")

            def pv(l, g):
                wait(pe, "prob_out", l, g + 1)
                if g >= 2:
                    wait(pe, "ya_in", l, g - 1)
                kv = g % 2
                for j in range(NT):
                    for par in range(2):
                        m = pe.matmul(OB[g % 2][64 * par:64 * par + 64, 0:256], vv[:, j, 64 * kv:64 * kv + 64],
                                      probT[:, j, 256 * par:256 * par + 256], start=(j == 0), stop=(j == NT - 1))
                inc(m, "pv_mm")

            def kend_turn(l):
                wait(pe, "kend_in", l, 1)
                wait(pe, "prob_out", l, 4)
                for r in range(2):
                    for h in range(HH):
                        m = pe.transpose(TB[r][:, P * h:P * h + P], kend[:, 4 * r + h, :], ident)
                    inc(m, "kend_turned")

            def states(l):
                wait(pe, "unit_seen", l, 11)
                for r in range(2):
                    wait(pe, "kendT_in", l, r + 1)
                    for h in range(HH):
                        m = pe.matmul(TB[r][:, P * h:P * h + P], kendT[:, 4 * r + h, :], hv[:, r, P * h:P * h + P],
                                      start=True, stop=True)
                    inc(m, "state_mm")

            def intra(l, n):
                T, h = n // HH, n % HH
                if n >= 2:
                    wait(pe, "at_in", l, n - 1)
                for r in range(2):
                    wait(pe, "ek_in", l, 2 * n + r + 1)
                    if n == 0:
                        wait(pe, "qe_in", l, r + 1)
                    for i in range(NCH):
                        lo, hi = (0, 32 * (i // 2 + 1)) if r == 0 else ((0, 0, 64, 96)[i // 2], P)
                        m = pe.matmul(SB[n % 2][lo:hi, P * r + CHUNK * i:P * r + CHUNK * i + CHUNK], ek[:, r, i, lo:hi],
                                      qe[:, r, NT * h + T, i, :], start=True, stop=True)
                inc(m, "at_mm")

            def outputs(l, n):
                T, h = n // HH, n % HH
                wait(pe, "at_in", l, n + 1)
                if n == 0:
                    wait(pe, "state_in", l, 2)
                    wait(pe, "ya_in", l, 4)
                o = OB[T][:, P * h:P * h + P]
                v = hv[:, T, P * h:P * h + P]
                pe.matmul(o, at_sb[:, n % 2, 0, :], v, start=True, stop=False)
                pe.matmul(o, at_sb[:, n % 2, 1, :], v, start=False, stop=False)
                r = 0 if T == 1 else 1
                inc(pe.matmul(o, qc[:, r, h, :], state[:, r, h, :], start=False, stop=True), "o_mm")

            def y_turn(l, T):
                wait(pe, "y_ready", l, T + 1)
                wait(pe, "state_in", l, T + 1)
                for c in range(4):
                    m = pe.transpose(TB[T][:, P * c:P * c + P], og[:, T, P * c:P * c + P], ident)
                inc(m, "y_turned")

            def up_attn(l, i):
                if i == 0:
                    arrived(l, W_IN_LOADS)
                    wait(pe, "yT_in", l, 1)
                elif i < 3:
                    wait(pe, "unit_seen", l, UNITS - 2 + i)
                w = slot3(slot_of(l, W_IN_LOADS), 4, D)
                for a in range(2):
                    f = P * (2 * i + a)
                    for c in range(4):
                        m = pe.matmul(UA[i][:, 256 * a:256 * a + 256], w[:, c, f:f + P], yaT[:, c, :],
                                      start=(c == 0), stop=(c == 3))
                inc(m, "ua_mm")

            def up_hgrn(l, i):
                if i == 0:
                    arrived(l, W_IN_LOADS + 1)
                    wait(pe, "yT_in", l, 2)
                for a in range(2):
                    f = P * (2 * i + a)
                    for c in range(4):
                        w = slot3(slot_of(l, W_IN_LOADS + 1), 4, D)
                        m = pe.matmul(UH[i][:, 256 * a:256 * a + 256], w[:, c, f:f + P], yhT[:, c, :],
                                      start=(c == 0), stop=(c == 3))
                inc(m, "uh_mm")

            def mix_out(l, tt, halves):
                if tt == 0:
                    wait(pe, "merged_in", l, 3)
                for c in range(KC):
                    n = W_IN_LOADS + 2 + c // 4
                    if tt == 0 and c % 4 == 0:
                        arrived(l, n)
                    if tt == 0 and c == 6:
                        wait(pe, "merged_in", l, 4)
                    w = slot3(slot_of(l, n), 4, D)
                    for half in halves:
                        m = pe.matmul(ACC[tt][half][:, :], merged[:, c, P * tt:P * tt + P],
                                      w[:, c % 4, 512 * half:512 * half + 512], start=(c == 0), stop=(c == KC - 1))
                    if (tt, half) == (1, 1) and c % 4 == 3:
                        inc(m, "wout_mm")
                if (tt, half) != (1, 1):
                    inc(m, "wout0_mm")

            def logits(l, tt):
                wait(pe, "h_in", l, 6 + 2 * tt)
                pe.wait_ge(s_wr, (l + 1) * 16 * 5)
                for c in range(KC):
                    m = pe.matmul(SB[0][:, 64 * tt:64 * tt + 36], hT[:, c, P * tt:P * tt + P], wr[:, c, :],
                                  start=(c == 0), stop=(c == KC - 1))
                if tt == NT - 1:
                    inc(m, "logit_mm")

            def places(l):
                wait(pe, "mask_in", l, 1)
                one, bef = C("ones"), C("before")
                pe.matmul(SB[1][:, 0:NE], bef, mh[:, 0, :], start=True, stop=True)
                pe.matmul(SB[1][:, NE:2 * NE], bef, mh[:, 1, :], start=True, stop=False)
                inc(pe.matmul(SB[1][:, NE:2 * NE], one, mh[:, 0, :], start=False, stop=True), "pos_mm")
                pe.matmul(COUNT_B, one, mh[:, 0, :], start=True, stop=False)
                inc(pe.matmul(COUNT_B, one, mh[:, 1, :], start=False, stop=True), "count_mm")

            def gather(b):
                for tt in range(NT):
                    for q in range(4):
                        m = pe.matmul(part(GB, 0)[32 * q:32 * q + 32, :], sel[:, b, tt, :],
                                      xn[:, tt, :].rearrange("p (f c) -> p c f", c=KC)[:, 2 * q:2 * q + 2, :],
                                      start=(tt == 0), stop=(tt == NT - 1))
                return m

            def rows_turn():
                for half in range(2):
                    m = pe.transpose(part(GB, 1)[:, P * half:P * half + P], hrow[:, P * half:P * half + P], ident)
                return m

            def gate_up(b, s0):
                wg, wu = slot3(s0, KC, FE), slot3(s0 + 1, KC, FE)
                for c in range(KC):
                    for q in range(4):
                        m = pe.matmul(part(HB, b)[32 * q:32 * q + 32, :], hs[:, b, c % 2, c // 2, :],
                                      (wg, wu)[q // 2][:, c, 256 * (q % 2):256 * (q % 2) + 256],
                                      start=(c == 0), stop=(c == KC - 1))
                return m

            def sel_turn(b):
                for tt in range(NT):
                    m = pe.transpose(ST_B[:, P * tt:P * tt + P], selw[:, b, tt, :, :].rearrange("p q s -> p (q s)"), ident)
                return m

            def hid_turn(b):
                for j in range(2):
                    m = pe.transpose(HT_B[:, P * j:P * j + P], hid[:, b, j::2], ident)
                return m

            def down(b, s0):
                wd = slot(s0 + 2).rearrange("p (h j d) -> p h j d", h=2, j=2)
                for k in range(4):
                    half, j = k // 2, k % 2
                    for q in range(4):
                        m = pe.matmul(part(YB, b)[32 * q:32 * q + 32, :], hidT[:, b, j, 32 * half:32 * half + 32],
                                      wd[:, half, j, 256 * q:256 * q + 256], start=(k == 0), stop=(k == 3))
                return m

            def add_up(b, first):
                for tt in range(NT):
                    for q in range(4):
                        m = add_product(b, tt, q, first and tt == 0)
                return m

            def add_product(b, tt, q, start):
                return pe.matmul(part(SUMS[q], tt), selT[32 * q:32 * q + 32, b, tt, :],
                                 ysb[32 * q:32 * q + 32, b, :], start=start, stop=True, skip_group_check=True)

            def expert(l, e, third, g, b, first=False, second=False, last=False):
                s0 = 3 * third_of(l, g)
                counts = [(third + loads_before(l, s) + mixer_loads(l, s) + 1) * 16 for s in range(s0, s0 + 3)]
                for k in range(2):
                    pe.wait_ge(landed[s0 + k], counts[k])
                wait(pe, "hs_in", l, e + 1)
                if not (first or second):
                    wait(pe, "hid_in", l, e - 1)
                inc(gate_up(b, s0), "gu_mm")
                wait(pe, "selw_in", l, e + 1)
                inc(sel_turn(b), "sel_turned")
                if not first:
                    wait(pe, "y_in", l, e)
                    inc(add_up(1 - b, second), "sum_mm")
                if not last:
                    wait(pe, "sel_in", l, e + 2)
                    if not first:
                        wait(pe, "hs_in", l, e)
                    inc(gather(1 - b), "gather_mm")
                wait(pe, "selT_in", l, e + 1)
                wait(pe, "hid_in", l, e + 1)
                inc(hid_turn(b), "hid_turned")
                if not last:
                    wait(pe, "rows_in", l, e + 2)
                    inc(rows_turn(), "rows_turned")
                wait(pe, "hidT_in", l, e + 1)
                if not (first or second):
                    wait(pe, "y_in", l, e - 1)
                pe.wait_ge(landed[s0 + 2], counts[2])
                inc(down(b, s0), "down_mm")

            pe.wait_ge(s_head, 3 * 16)
            for l in range(DEPTH):
                for tt in range(NT):
                    turn(l, 0, tt)
                for u in range(4):
                    unit(l, u)
                    if l == 0 and u == 0:
                        pe.wait_ge(s_const, 16 * 5)
                        pe.transpose(TB[0][:, 0:24], rows[:, :], ident[0:24, 0:24]).then_inc(s_lbt, 1)
                        pe.wait_ge(s_lb, 1)
                qk_turn(l)
                unit(l, 4)
                scores(l, 0)
                unit(l, 5)
                for g in range(4):
                    prob_turn(l, g)
                    if g < 3:
                        scores(l, g + 1)
                    unit(l, 6 + g)
                    pv(l, g)
                unit(l, 10)
                unit(l, 11)
                kend_turn(l)
                unit(l, 12)
                states(l)
                unit(l, 13)
                for n in range(8):
                    intra(l, n)
                    if n < 7:
                        unit(l, 14 + n)
                    else:
                        up_attn(l, 0)
                    outputs(l, n)
                    if n == 5:
                        y_turn(l, 0)
                up_attn(l, 1)
                up_attn(l, 2)
                y_turn(l, 1)
                for i in range(4):
                    if i == 3:
                        up_attn(l, 3)
                    up_hgrn(l, i)
                mix_out(l, 0, (0, 1))
                mix_out(l, 1, (0,))
                turn(l, 1, 0)
                mix_out(l, 1, (1,))
                logits(l, 0)
                turn(l, 1, 1)
                logits(l, 1)
                places(l)
                wait(pe, "sel_in", l, 1)
                inc(gather(0), "gather_mm")
                wait(pe, "rows_in", l, 1)
                inc(rows_turn(), "rows_turned")
                for e in range(FIRST_E):
                    expert(l, e, 0, e, e, first=(e == 0), second=(e == 1))
                with pe.Fori(0, LOOPS_E) as i:
                    for k in range(FIRST_E, FIRST_E + STEP_E):
                        expert(l, i * STEP_E + k, i * 2 + k // 3, k % 3, k % 2)
                for e in range(NE - LAST_E, NE):
                    expert(l, e, e // 3, e % 3, e % 2, last=(e == NE - 1))
                ov = OV[l]
                wait(pe, "route_in", l, 1)
                over = pe.value_load(ctl[0:1, 0:1], min_val=0, max_val=MAX_OVER)
                pe.sem_inc(ov["down"], 1)
                with pe.If(over > 0):
                    wait(pe, "y_in", l, NE)
                    with pe.Fori(0, MAX_OVER) as j:
                        with pe.If(j < over):
                            pe.wait_ge(ov["sel"], j + 1)
                            gather(0).then_inc(ov["gather"], 1)
                            pe.wait_ge(ov["rows"], j + 1)
                            rows_turn().then_inc(ov["rows_turned"], 1)
                            pe.wait_ge(ov["hs"], j + 1)
                            pe.wait_ge(ov["landed"], (j + 1) * 48)
                            gate_up(0, 0).then_inc(ov["gu"], 1)
                            pe.wait_ge(ov["selw"], j + 1)
                            sel_turn(0).then_inc(ov["sel_turned"], 1)
                            pe.wait_ge(ov["selT"], j + 1)
                            pe.wait_ge(ov["hid"], j + 1)
                            hid_turn(0).then_inc(ov["turned"], 1)
                            pe.wait_ge(ov["hidT"], j + 1)
                            down(0, 0).then_inc(ov["down"], 1)
                            pe.wait_ge(ov["y"], j + 1)
                            add_up(0, False).then_inc(ov["sum"], 1)
                        with pe.Else():
                            pe.nop()
                with pe.Else():
                    pe.nop()
                wait(pe, "y_in", l, NE)
                for q in range(4):
                    for tt in range(NT):
                        m = add_product(1, tt, q, False)
                    inc(m, "sum_last")

        @block.scalar
        def _(act):
            A = nc.scalar.activation
            steps = [0]
            one = C("ones")[:, 0:1]

            def link(ins):
                steps[0] += 1
                ins.then_inc(s_act, 1)
                act.wait_ge(s_act, steps[0])

            def sigmoid(ap):
                link(A(ap, ap, ACT.Ln, bias=one))
                inc(A(ap, ap, ACT.Exp, scale=-1.0), "sigmoid")

            def square(x_in, xn_out, total):
                return A(xn_out, x_in, ACT.Square, accum_out=total)

            def squares(l):
                if l == 0:
                    act.wait_ge(s_x, 16)
                for q in range(4):
                    if l > 0:
                        wait(act, "x_done", l - 1, q + 1)
                    for tt in range(NT):
                        m = square(x[:, tt, 256 * q:256 * q + 256], xn[:, tt, 256 * q:256 * q + 256], ssq[:, tt, q:q + 1])
                inc(m, "squares")

            def squares_mixed(l):
                wait(act, "x_mixed", l, 1)
                inc(square(x[:, 0, :], xn[:, 0, :], ss[:, 0:1]), "squares")
                root(l, 4, 0, 1)
                for half in range(2):
                    columns = slice(512 * half, 512 * half + 512)
                    wait(act, "x_mixed", l, 2 + half)
                    inc(square(x[:, 1, columns], xn[:, 1, columns], ssh[:, half:half + 1]), "squares")
                root(l, 5, 1, 2)

            def root(l, k, a, b):
                wait(act, "mean_in", l, k)
                inc(A(rs1[:, a:b], rs0[:, a:b], ACT.Ln), "root_log")
                wait(act, "root_log", l, k)
                inc(A(rs1[:, a:b], rs1[:, a:b], ACT.Exp, scale=-0.5), "root")

            def unit(l, u):
                wait(act, "unit_mm", l, u + 1)
                b = UB[u % 2][:, :]
                b2 = b.rearrange("p (a n) -> p a n", a=2)
                if u < 2:
                    if l > 0:
                        wait(act, "x_done", l - 1, 4)
                    m = A(raw[:, :, 256 * u:256 * u + 256], b2, ACT.Copy)
                elif u == 2:
                    A(raw[:, :, 512:640], b2[:, :, 0:P], ACT.Copy)
                    m = A(vv[:, :, :], b2[:, :, P:2 * P], ACT.Copy)
                elif u in (3, 4):
                    dst = qd[:, 2 * (u - 3):2 * (u - 3) + 2, :]
                elif u in Z_UNITS:
                    z = u - 5
                    if z >= 2:
                        wait(act, "b_in", l, z - 1)
                    dst, b2 = ft[:, z % 2, :], b
                elif u in (9, 10):
                    m = A(hv[:, :, 256 * (u - 9):256 * (u - 9) + 256], b2, ACT.Copy)
                elif u in (11, 12):
                    dst = og[:, :, 256 * (u - 11):256 * (u - 11) + 256]
                else:
                    if u == 13:
                        wait(act, "pv_mm", l, 4)
                    dst = gate[:, 2 * (u - 13):2 * (u - 13) + 2, :]
                if u not in SIGMOID_UNITS:
                    inc(m, "unit_seen")
                else:
                    inc(A(dst, b2, ACT.Exp, scale=-1.0), "unit_seen")
                    wait(act, "unit_seen", l, u + 1)
                    sigmoid(dst)

            def log_f(l, z):
                wait(act, "f_in", l, z + 1)
                if z >= 1:
                    wait(act, "b_in", l, z)
                wait(act, "cleared", l, 1)
                inc(A(logf, ft[:, z % 2, :], ACT.Ln), "f_log")

            def probs(l, g):
                wait(act, "sunk", l, g + 1)
                if g >= 2:
                    wait(act, "prob_turned", l, g - 1)
                for n in range(4):
                    par, hh = n // 2, n % 2
                    A(prob[:, g % 2, n, :], SB[par][:, 256 * hh:256 * hh + 256], ACT.Exp, scale=1.0,
                      bias=anm[:, g % 2, n:n + 1], accum_out=asum[:, g % 2, n:n + 1])
                inc(A(aexp[:, g % 2, :], adif[:, g % 2, :], ACT.Exp), "prob_exp")

            def prob_out(l, g):
                wait(act, "prob_turned", l, g + 1)
                if g >= 1:
                    wait(act, "pv_mm", l, g)
                for j in range(NT):
                    m = A(probT[:, j, :], TB[j][:, :], ACT.Copy)
                inc(m, "prob_out")

            def kend_exp(l):
                wait(act, "b_in", l, 4)
                for r in range(2):
                    for h in range(HH):
                        hT_ = NT * h + r
                        b, edge = ((bd[:, 0, hT_, 1:P + 1], bd[:, 0, hT_, P:P + 1]) if r == 0 else
                                   (bd[:, 1, hT_, 0:P], bd[:, 1, hT_, 0:1]))
                        m = A(kend[:, 4 * r + h, :], b, ACT.Exp, scale=-1.0, bias=edge)
                inc(m, "kend_exp")

            def q_exp(l):
                for r in range(2):
                    wait(act, "qe_sub", l, r + 1)
                    inc(A(xn[:, r, :], xn[:, r, :], ACT.Exp), "qe_exp")
                    b = bd[:, r, 1 - r::NT, :]
                    inc(A(qc[:, r, :, :], b[:, :, 1 - r:P + 1 - r], ACT.Exp), "qc_exp")

            def kendT(l):
                for r in range(2):
                    wait(act, "kend_turned", l, r + 1)
                    inc(A(ek[:, 1, 4 * r:4 * r + 4, :], TB[r][:, :].rearrange("p (h s) -> p h s", h=HH), ACT.Copy), "kendT_in")

            def state_in(l):
                for r in range(2):
                    wait(act, "state_mm", l, r + 1)
                    inc(A(ft[:, r, :], TB[r][:, :], ACT.Copy), "state_in")

            def ek_exp(l, n):
                T, h = n // HH, n % HH
                for r in range(2):
                    if n == 0:
                        wait(act, "state_mm", l, 2)
                    else:
                        wait(act, "at_mm", l, n)
                    b = bd[:, r, NT * h + T, :]
                    for i in range(NCH):
                        if r == 0:
                            m = A(ek[:, 0, i, 0:CHUNK * (i + 1)], b[:, 1:CHUNK * (i + 1) + 1], ACT.Exp, scale=-1.0,
                                  bias=b[:, CHUNK * i:CHUNK * i + 1])
                        else:
                            m = A(ek[:, 1, i, CHUNK * i:P], b[:, CHUNK * i:P], ACT.Exp, scale=-1.0,
                                  bias=b[:, CHUNK * (i + 1):CHUNK * (i + 1) + 1])
                    inc(m, "ek_exp")

            def o_square(l, T):
                wait(act, "o_mm", l, 4 * T + 4)
                inc(A(junk[:, :], OB[T][:, :], ACT.Square, accum_out=ss[:, T:T + 1]), "osq")
                root(l, 2 + T, T, T + 1)

            def gate_out(b):
                A(eg[0:64, b, :], part(HB, b)[0:64, :], ACT.Exp, scale=-1.0)
                return A(up[0:64, b, :], part(HB, b)[64:128, :], ACT.Copy)

            def selT_out(b):
                return A(selT[:, b, :, :], ST_B.rearrange("p (t s) -> p t s", t=NT), ACT.Copy)

            def rows_out():
                return A(hrow, part(GB, 0), ACT.Copy)

            def hidT_out(b):
                return A(hidT[:, b, :, :], HT_B.rearrange("p (j s) -> p j s", j=2)[:, :, 0:64], ACT.Copy)

            def expert(l, e, b, early=False, last=False):
                wait(act, "gu_mm", l, e + 1)
                if not early:
                    wait(act, "hid_in", l, e - 1)
                inc(gate_out(b), "gu_seen")
                wait(act, "sel_turned", l, e + 1)
                if not early:
                    wait(act, "sum_mm", l, e - 1)
                inc(selT_out(b), "selT_in")
                if not last:
                    wait(act, "gather_mm", l, e + 2)
                    inc(rows_out(), "rows_in")
                wait(act, "hid_turned", l, e + 1)
                inc(hidT_out(b), "hidT_in")
                wait(act, "down_mm", l, e + 1)
                inc(A(ysb[:, b, :], part(YB, b), ACT.Copy), "y_in")

            nc.scalar.preload_act_table_set("natural_log_exp_and_others")
            for ap, src in ((rows[0:16, :], t["hgrn_lb_table"].rearrange("l r (h p) -> (l r h) p", p=HK)),
                            (rows[16:24, :], t["hgrn_norm_g"].rearrange("l (h p) -> (l h) p", p=HK)),
                            (sink[:], spread(t["sink_logits"])),
                            (bias[:, :, 0:GROUPS], spread(t["b_router_group"])),
                            (bias[:, :, GROUPS:], spread(t["b_router_expert"].rearrange("l g e -> l (g e)")))):
                act.dma_start(ap, src).then_inc(s_const, 16)
            for l in range(DEPTH):
                squares(l)
                root(l, 1, 0, NT)
                if l == 0:
                    act.wait_ge(s_head, 3 * 16)
                for u in range(5):
                    unit(l, u)
                    if l == 0 and u == 0:
                        act.wait_ge(s_lb, 2)
                        A(cols[:, 0:16], cols[:, 0:16], ACT.Exp).then_inc(s_lbe, 1)
                probs(l, 0)
                unit(l, 5)
                for g in range(4):
                    prob_out(l, g)
                    log_f(l, g)
                    if g < 3:
                        probs(l, g + 1)
                    unit(l, 6 + g)
                unit(l, 10)
                kend_exp(l)
                q_exp(l)
                unit(l, 11)
                kendT(l)
                unit(l, 12)
                state_in(l)
                ek_exp(l, 0)
                unit(l, 13)
                for n in range(8):
                    if n < 7:
                        ek_exp(l, n + 1)
                        unit(l, 14 + n)
                    if n == 4:
                        o_square(l, 0)
                o_square(l, 1)
                squares_mixed(l)
                wait(act, "gsub", l, 1)
                inc(A(gexp, gexp, ACT.Exp), "gexp")
                wait(act, "e2sub", l, 1)
                inc(A(e2, e2, ACT.Exp), "e2exp")
                wait(act, "gather_mm", l, 1)
                inc(rows_out(), "rows_in")
                for e in range(2):
                    expert(l, e, e, early=True)
                with act.Fori(1, NE // 2 - 1) as i:
                    for b in range(2):
                        expert(l, i * 2 + b, b)
                for e in range(NE - 2, NE):
                    expert(l, e, e % 2, last=(e == NE - 1))
                ov = OV[l]
                wait(act, "route_in", l, 1)
                over = act.value_load(ctl[0:1, 0:1], min_val=0, max_val=MAX_OVER)
                wait(act, "sum_mm", l, NE - 1)
                with act.If(over > 0):
                    with act.Fori(0, MAX_OVER) as j:
                        with act.If(j < over):
                            act.wait_ge(ov["gather"], j + 1)
                            rows_out().then_inc(ov["rows"], 1)
                            act.wait_ge(ov["gu"], j + 1)
                            gate_out(0).then_inc(ov["seen"], 1)
                            act.wait_ge(ov["sel_turned"], j + 1)
                            selT_out(0).then_inc(ov["selT"], 1)
                            act.wait_ge(ov["turned"], j + 1)
                            hidT_out(0).then_inc(ov["hidT"], 1)
                            act.wait_ge(ov["down"], j + 2)
                            A(ysb[:, 0, :], part(YB, 0), ACT.Copy).then_inc(ov["y"], 1)
                        with act.Else():
                            act.nop()
                with act.Else():
                    act.nop()
            squares(DEPTH)
            root(DEPTH, 1, 0, NT)

        @block.vector
        def _(dve):
            V = nc.vector
            step = [0]

            def link(ins):
                step[0] += 1
                ins.then_inc(s_dve, 1)
                dve.wait_ge(s_dve, step[0])

            def bc(ap, n):
                return ap.unsqueeze(len(ap.shape)).broadcast_to([*ap.shape, n])

            def inverse_root(l, k, a, b, n):
                v, y, u = rs0[:, a:b], rs1[:, a:b], rs2[:, a:b]
                if k == 5:
                    wait(dve, "squares", l, 3)
                    link(V.tensor_scalar(v, ssh[:, 0:1], 1.0 / n, EPS, ALU.mult, ALU.add))
                    wait(dve, "squares", l, 4)
                    inc(V.scalar_tensor_tensor(out=v, in0=ssh[:, 1:2], scalar=1.0 / n, in1=v, op0=ALU.mult,
                                               op1=ALU.add), "mean_in")
                else:
                    if k in (2, 3):
                        wait(dve, "osq", l, k - 1)
                    else:
                        wait(dve, "squares", l, 1 if k == 1 else 2)
                        if k == 1:
                            link(V.tensor_reduce(ss, ssq, AX_X, ALU.add))
                    inc(V.tensor_scalar(v, ss[:, a:b], 1.0 / n, EPS, ALU.mult, ALU.add), "mean_in")
                wait(dve, "root", l, k)
                link(V.tensor_tensor(u, y, y, ALU.mult))
                link(V.tensor_tensor(u, u, v, ALU.mult))
                link(V.tensor_scalar(u, u, -0.5, 1.5, ALU.mult, ALU.add))
                link(V.tensor_tensor(rstd[:, a:b], y, u, ALU.mult))

            def scale_tile(tt):
                return V.tensor_scalar(xn[:, tt, :], x[:, tt, :], rstd[:, tt:tt + 1], None, ALU.mult)

            def normalise(l):
                inverse_root(l, 1, 0, NT, D)
                for tt in range(NT):
                    inc(scale_tile(tt), "xn_in")

            def mixed(l, tt, halves, k):
                for half in halves:
                    xs = x[:, tt, 512 * half:512 * half + 512]
                    m = V.tensor_tensor(xs, xs, ACC[tt][half][:, :], ALU.add)
                inc(m, "x_mixed")
                wait(dve, "x_mixed", l, k)

            def mix_and_normalise(l):
                wait(dve, "wout0_mm", l, 1)
                mixed(l, 0, (0, 1), 1)
                inverse_root(l, 4, 0, 1, D)
                inc(scale_tile(0), "xn_in")
                wait(dve, "wout0_mm", l, 2)
                mixed(l, 1, (0,), 2)
                turned(l, 1, 0)
                wait(dve, "wout_mm", l, WO_PARTS)
                mixed(l, 1, (1,), 3)
                inverse_root(l, 5, 1, 2, D)
                inc(scale_tile(1), "xn_in")
                turned(l, 1, 1)

            def turned(l, half, tt):
                for g in range(2 * tt, 2 * tt + 2):
                    q = g % 2
                    wait(dve, "turned", l, 4 * half + g + 1)
                    inc(V.tensor_tensor(hT[:, 4 * q:4 * q + 4, P * tt:P * tt + P],
                                        TB[g % 2][:, :].rearrange("p (c s) -> p c s", c=4),
                                        bc(gains[:, DEPTH * half + l, 4 * q:4 * q + 4], P), ALU.mult), "h_in")

            def rope(l):
                for h0, h1 in ((0, HEADS), (HEADS, HEADS + KVH)):
                    wait(dve, "unit_seen", l, 2 if h0 == 0 else 3)
                    n = h1 - h0
                    c = cos.unsqueeze(2).broadcast_to([P, NT, n, 32])
                    s = sin.unsqueeze(2).broadcast_to([P, NT, n, 32])
                    src = raw.rearrange("p t (h a f) -> p t h a f", a=2, f=32)[:, :, h0:h1]
                    t1, t2 = src[:, :, :, 0, :], src[:, :, :, 1, :]
                    r0, r1 = (rot[:, i, 0:64 * n].rearrange("p (t h f) -> p t h f", t=NT, f=32) for i in range(2))
                    for a, (u, w, op) in enumerate(((t1, t2, ALU.subtract), (t2, t1, ALU.add))):
                        for tt in range(NT):
                            V.tensor_tensor(r0[:, tt], u[:, tt], c[:, tt], ALU.mult)
                            m = V.tensor_tensor(r1[:, tt], w[:, tt], s[:, tt], ALU.mult)
                        link(m)
                        for tt in range(NT):
                            if h0 == 0:
                                dq = roped[:, tt, 0:512].rearrange("p (h a f) -> p h a f", a=2, f=32)
                                m = V.tensor_tensor(dq[:, :, a, :], r0[:, tt], r1[:, tt], op)
                            else:
                                dk = roped[:, tt, 512:768].rearrange("p (v d a f) -> p v d a f", v=2, d=2, f=32)
                                for d in range(2):
                                    m = V.tensor_tensor(dk[:, :, d, a, :], r0[:, tt], r1[:, tt], op)
                        if h0 > 0 and a == 1:
                            inc(m, "roped_in")
                        else:
                            link(m)

            def qk_in(l):
                for tt in range(NT):
                    wait(dve, "qk_turned", l, tt + 1)
                    inc(V.tensor_scalar(qT[:, tt, :, :], TB[tt][:, :].rearrange("p (c s) -> p c s", c=4), HD ** -0.5, None,
                                        ALU.mult), "qkT_in")
                wait(dve, "qk_turned", l, 3)
                inc(V.tensor_copy(kT[:, :, :, :], TB[0][:, :].rearrange("p (t k s) -> p t k s", t=NT, k=KVH)), "qkT_in")

            def sink_max(l, g):
                b, kv = g // 2, g % 2
                wait(dve, "score_mm", l, g + 1)
                for par in range(2):
                    sc = SB[par][:, :].rearrange("p (h s) -> p h s", h=2)
                    part = sc[:, :, P:2 * P] if b == 0 else sc[:, :, 0:P]
                    mask = C("win0" if b == 0 else "win1").unsqueeze(1).broadcast_to([P, 2, P])
                    link(V.tensor_tensor(part, part, mask, ALU.add))
                for par in range(2):
                    sc = SB[par][:, :].rearrange("p (h s) -> p h s", h=2)
                    link(V.tensor_reduce(amax[:, g % 2, 2 * par:2 * par + 2], sc, AX_X, ALU.max))
                sk = sink[:, l, 4 * kv:4 * kv + 4].rearrange("p (h a) -> p a h", a=2)
                mx, m4 = amax[:, g % 2, :], am[:, g % 2, :]
                link(V.tensor_tensor(m4.rearrange("p (a h) -> p a h", a=2), mx.rearrange("p (a h) -> p a h", a=2), sk, ALU.max))
                link(V.tensor_scalar(anm[:, g % 2, :], m4, -1.0, None, ALU.mult))
                inc(V.tensor_tensor(adif[:, g % 2, :].rearrange("p (a h) -> p a h", a=2), sk,
                                    m4.rearrange("p (a h) -> p a h", a=2), ALU.subtract), "sunk")

            def prob_in(l, g):
                wait(dve, "prob_exp", l, g + 1)
                ad = aden[:, g % 2, :]
                link(V.tensor_tensor(ad, asum[:, g % 2, :], aexp[:, g % 2, :], ALU.add))
                link(V.reciprocal(ad, ad))
                for n in range(4):
                    m = V.tensor_scalar(prob[:, g % 2, n, :], prob[:, g % 2, n, :], ad[:, n:n + 1], None, ALU.mult)
                inc(m, "prob_in")

            def ya_in(l, g):
                b, kv = g // 2, g % 2
                wait(dve, "pv_mm", l, g + 1)
                inc(V.tensor_copy(yaT[:, 2 * kv:2 * kv + 2, P * b:P * b + P],
                                  OB[g % 2][:, 0:256].rearrange("p (c s) -> p c s", c=2)), "ya_in")

            def silu_unit(l, u):
                wait(dve, "sigmoid", l, SIGMOID_UNITS.index(u) + 1)
                b2 = UB[u % 2][:, :].rearrange("p (a n) -> p a n", a=2)
                dst = qd[:, 2 * (u - 3):2 * (u - 3) + 2, :] if u < 5 else og[:, :, 256 * (u - 11):256 * (u - 11) + 256]
                inc(V.tensor_tensor(dst, dst, b2, ALU.mult), "unit_done")

            def forget(l, z):
                r, hh = z // 2, z % 2
                wait(dve, "sigmoid", l, SIGMOID_UNITS.index(5 + z) + 1)
                f = ft[:, z % 2, :]
                for a in range(2):
                    h = 4 * r + 2 * hh + a
                    link(V.tensor_scalar(f[:, 256 * a:256 * a + 256], f[:, 256 * a:256 * a + 256], lbs[:, 0, l, h:h + 1],
                                         lbs[:, 1, l, h:h + 1], ALU.mult, ALU.add))
                V.tensor_scalar(f, f, float(np.exp(LOGF_MIN)), None, ALU.max).then_inc(PEV["f_in"][0], 1)
                wait(dve, "f_in", l, z + 1)
                link(V.tensor_scalar(kd[:, r, 2 * hh:2 * hh + 2, :].rearrange("p a s -> p (a s)"), f, -1.0, 1.0,
                                     ALU.mult, ALU.add))

            def cumulate(l, z):
                r, hh = z // 2, z % 2
                wait(dve, "f_log", l, z + 1)
                wait(dve, "cleared", l, 1)
                for a in range(2):
                    for T in range(NT):
                        lf = logf[:, 256 * a + P * T:256 * a + P * T + P]
                        b = bd[:, r, NT * (2 * hh + a) + T, :]
                        if r == 0:
                            m = V.tensor_tensor_scan(b[:, 1:P + 1], C("ones"), lf, 0.0, ALU.mult, ALU.add)
                        else:
                            m = V.tensor_tensor_scan(b[:, 0:P][:, ::-1], C("ones"), lf[:, ::-1], 0.0, ALU.mult, ALU.add)
                inc(m, "b_in")

            def q_sub(l):
                wait(dve, "b_in", l, 4)
                for r in range(2):
                    b = bd[:, r, :, 1 - r:P + 1 - r].rearrange("p h (c u) -> p h c u", u=CHUNK)
                    edge = bd[:, r, :, CHUNK * r:P + CHUNK * r - (CHUNK - 1):CHUNK] if r == 0 else \
                        bd[:, r, :, CHUNK:P + 1:CHUNK]
                    inc(V.tensor_tensor(qe[:, r, :, :, :], b, bc(edge, CHUNK), ALU.subtract), "qe_sub")

            def q_in(l):
                for r in range(2):
                    wait(dve, "qc_exp", l, r + 1)
                    V.tensor_tensor(qc[:, r, :, :], qc[:, r, :, :], qd[:, :, P * (1 - r):P * (1 - r) + P], ALU.mult)
                    e = xn[:, r, :]
                    inc(V.tensor_tensor(e, e, qd[:, :, :].rearrange("p h s -> p (h s)"), ALU.mult), "qe_in")

            def kend_in(l):
                wait(dve, "kend_exp", l, 1)
                for r in range(2):
                    e = kend[:, 4 * r:4 * r + 4, :]
                    m = V.tensor_tensor(e, e, kd[:, r, :, P * r:P * r + P], ALU.mult)
                inc(m, "kend_in")

            def ek_in(l, n):
                T, h = n // HH, n % HH
                for r in range(2):
                    wait(dve, "ek_exp", l, 2 * n + r + 1)
                    k = kd[:, r, h, P * T:P * T + P].unsqueeze(1).broadcast_to([P, NCH, P])
                    inc(V.tensor_tensor(ek[:, r, :, :], ek[:, r, :, :], k, ALU.mult), "ek_in")

            def at_in(l, n):
                wait(dve, "at_mm", l, n + 1)
                if n >= 2:
                    wait(dve, "o_mm", l, n - 1)
                for r, name in ((0, "tri_f"), (1, "tri_b")):
                    m = V.tensor_tensor(at_sb[:, n % 2, r, :], SB[n % 2][:, P * r:P * r + P], C(name), ALU.mult)
                inc(m, "at_in")

            def y_ready(l, T):
                inverse_root(l, 2 + T, T, T + 1, HW)
                inc(V.scalar_tensor_tensor(out=og[:, T, :], in0=OB[T][:, :], scalar=rstd[:, T:T + 1], in1=og[:, T, :],
                                           op0=ALU.mult, op1=ALU.mult), "y_ready")

            def yT_in(l, T):
                wait(dve, "y_turned", l, T + 1)
                inc(V.tensor_tensor(yhT[:, :, P * T:P * T + P], TB[T][:, :].rearrange("p (c s) -> p c s", c=4),
                                    bc(cols[:, 16 + 4 * l:20 + 4 * l], P), ALU.mult), "yT_in")

            def merge(l, i):
                wait(dve, "sigmoid", l, 16)
                wait(dve, "ua_mm", l, i + 1)
                wait(dve, "uh_mm", l, i + 1)
                ga, gb = gate[:, 2 * i:2 * i + 2, :], gate[:, 8 + 2 * i:8 + 2 * i + 2, :]
                V.tensor_tensor(ga, ga, UA[i][:, :].rearrange("p (a s) -> p a s", a=2), ALU.mult)
                link(V.tensor_tensor(gb, gb, UH[i][:, :].rearrange("p (a s) -> p a s", a=2), ALU.mult))
                inc(V.tensor_tensor(merged[:, 2 * i:2 * i + 2, :], ga, gb, ALU.add), "merged_in")

            def first_of(out, values, best, n):
                tv = tie[:, :, 0:n]
                for tt in range(NT):
                    m = V.scalar_tensor_tensor(out=tv[:, tt, :], in0=values[:, tt, :], scalar=best[:, tt:tt + 1],
                                               in1=C("falling")[:, NE - n:NE], op0=ALU.is_equal, op1=ALU.mult)
                link(m)
                link(V.tensor_reduce(cmax, tv, AX_X, ALU.max))
                link(V.tensor_tensor(out, tv, bc(cmax, n), ALU.is_equal))

            def route(l):
                wait(dve, "logit_mm", l, 1)
                b2 = SB[0][:, 0:128].rearrange("p (t n) -> p t n", t=NT)[:, :, 0:GROUPS + NE]
                link(V.tensor_tensor(lg, b2, bias[:, l, :].unsqueeze(1).broadcast_to([P, NT, GROUPS + NE]), ALU.add))
                g4 = lg[:, :, 0:GROUPS]
                link(V.tensor_reduce(gmax, g4, AX_X, ALU.max))
                inc(V.tensor_tensor(gexp, g4, bc(gmax, GROUPS), ALU.subtract), "gsub")
                first_of(ohg, g4, gmax, GROUPS)
                link(V.tensor_scalar(ohg, ohg, -1.0, -NEG, ALU.add, ALU.mult))
                link(V.tensor_tensor(masked.rearrange("p t (g e) -> p t g e", g=GROUPS),
                                     lg[:, :, GROUPS:].rearrange("p t (g e) -> p t g e", g=GROUPS), bc(ohg, EPG), ALU.add))
                link(V.tensor_reduce(m1, masked, AX_X, ALU.max))
                first_of(m1h, masked, m1, NE)
                link(V.scalar_tensor_tensor(out=masked, in0=m1h, scalar=NEG, in1=masked, op0=ALU.mult, op1=ALU.add))
                link(V.tensor_reduce(m2, masked, AX_X, ALU.max))
                inc(V.tensor_tensor(e2, m2, m1, ALU.subtract), "e2sub")
                first_of(m2h, masked, m2, NE)
                inc(V.tensor_tensor(mh, m1h, m2h, ALU.add), "mask_in")
                wait(dve, "gexp", l, 1)
                link(V.tensor_reduce(psum_g, gexp, AX_X, ALU.add))
                link(V.reciprocal(ptop, psum_g))
                wait(dve, "e2exp", l, 1)
                link(V.tensor_scalar(den2, e2, 1.0, None, ALU.add))
                link(V.reciprocal(den2, den2))
                link(V.tensor_tensor(w1, den2, ptop, ALU.mult))
                link(V.tensor_tensor(w2, w1, e2, ALU.mult))
                wait(dve, "pos_mm", l, 1)
                link(V.scalar_tensor_tensor(out=posm.rearrange("p t e -> p (t e)"), in0=SB[1][:, 0:2 * NE], scalar=1.0,
                                            in1=mh.rearrange("p t e -> p (t e)"), op0=ALU.add, op1=ALU.mult))

            def weights(l):
                for tt in range(NT):
                    V.tensor_scalar(wsel[:, tt, :], m1h[:, tt, :], w1[:, tt:tt + 1], None, ALU.mult)
                wait(dve, "count_mm", l, 1)
                link(V.tensor_copy(count, COUNT_B))
                for tt in range(NT):
                    m = V.scalar_tensor_tensor(out=wsel[:, tt, :], in0=m2h[:, tt, :], scalar=w2[:, tt:tt + 1],
                                               in1=wsel[:, tt, :], op0=ALU.mult, op1=ALU.add)
                link(m)

            def over_table(l):
                link(V.tensor_tensor(grid2, bc(count, 7), C("limits").unsqueeze(1).broadcast_to([P, NE, 7]), ALU.is_gt))
                link(V.tensor_reduce(novb, grid2, AX_X, ALU.add))
                link(V.tensor_tensor_scan(oend, C("ones")[:, 0:NE], novb, 0.0, ALU.mult, ALU.add))
                link(V.tensor_copy(ctlf[:, 0:1], oend[:, NE - 1:NE]))
                link(V.tensor_tensor(grid, oend.unsqueeze(1).broadcast_to([P, MAX_OVER, NE]), bc(C("over_at"), NE), ALU.is_le))
                link(V.tensor_reduce(ctlf[:, 1:], grid, AX_X, ALU.add))
                link(V.tensor_scalar(ctlf[:, 1:], ctlf[:, 1:], float(NE - 1), None, ALU.min))
                link(V.tensor_tensor(grid, grid, novb.unsqueeze(1).broadcast_to([P, MAX_OVER, NE]), ALU.mult))
                link(V.tensor_reduce(ooff, grid, AX_X, ALU.add))
                link(V.tensor_tensor(ooff, C("over_at"), ooff, ALU.subtract))
                link(V.tensor_scalar(ooff, ooff, 1.0, float(SLOTS), ALU.add, ALU.mult))
                inc(V.tensor_copy(ctl[0:1, :], ctlf[0:1, :]), "route_in")

            def select(b, column, offset=None):
                for tt in range(NT):
                    if offset is None:
                        m = V.tensor_scalar(sel[:, b, tt, :], C("iota"), posm[:, tt, bass.ds(column, 1)], None, ALU.is_equal)
                    else:
                        m = V.tensor_scalar(sel[:, b, tt, :], C("iota"), offset, posm[:, tt, bass.ds(column, 1)],
                                            ALU.add, ALU.is_equal)
                return m

            def weigh(b, column):
                for tt in range(NT):
                    m = V.tensor_scalar(selw[:, b, tt, :, :], sel[:, b, tt, :].unsqueeze(1).broadcast_to([P, 4, SLOTS]),
                                        wsel[:, tt, bass.ds(column, 1)], None, ALU.mult)
                return m

            def tokens_in(l, b):
                return V.tensor_tensor(hs[:, b, :, :, :].rearrange("p h q s -> p (h q) s"),
                                       part(GB, 1).rearrange("p (c s) -> p c s", c=KC),
                                       bc(gains2[:, l, :], SLOTS), ALU.mult)

            def hidden(b, own):
                g = eg[0:64, b, :]
                own(V.tensor_scalar(g, g, 1.0, None, ALU.add))
                own(V.reciprocal(g, g))
                own(V.tensor_tensor(g, g, part(HB, b)[0:64, :], ALU.mult))
                return V.tensor_tensor(hid[0:64, b, :], g, up[0:64, b, :], ALU.mult)

            def expert(l, e, b, own, first=False, second=False, last=False):
                early = first or second
                if not early:
                    wait(dve, "sel_turned", l, e - 1)
                inc(weigh(b, e), "selw_in")
                if not last:
                    if not first:
                        wait(dve, "gather_mm", l, e)
                    inc(select(1 - b, e + 1), "sel_in")
                wait(dve, "gu_seen", l, e + 1)
                if not early:
                    wait(dve, "hid_turned", l, e - 1)
                inc(hidden(b, own), "hid_in")
                if not last:
                    wait(dve, "rows_turned", l, e + 2)
                    if not first:
                        wait(dve, "gu_mm", l, e)
                    inc(tokens_in(l, 1 - b), "hs_in")

            def lower_bounds():
                dve.wait_ge(s_lbt, 1)
                V.tensor_copy(cols[:, :], TB[0][:, 0:24]).then_inc(s_lb, 1)
                dve.wait_ge(s_lb, 1)
                link(V.tensor_tensor(small[:, 128:136], cols[:, 0:8], cols[:, 8:16], ALU.max))
                V.tensor_tensor(cols[:, 0:8], cols[:, 0:8], small[:, 128:136], ALU.subtract)
                V.tensor_tensor(cols[:, 8:16], cols[:, 8:16], small[:, 128:136], ALU.subtract).then_inc(s_lb, 1)
                dve.wait_ge(s_lbe, 1)
                link(V.tensor_tensor(small[:, 128:136], cols[:, 0:8], cols[:, 8:16], ALU.add))
                link(V.reciprocal(small[:, 128:136], small[:, 128:136]))
                link(V.tensor_tensor(cols[:, 0:8], cols[:, 0:8], small[:, 128:136], ALU.mult))
                link(V.tensor_tensor(cols[:, 8:16], cols[:, 8:16], small[:, 128:136], ALU.mult))
                link(V.tensor_tensor(small[:, 136:144], cols[:, 0:8], cols[:, 8:16], ALU.add))
                link(V.tensor_tensor(small[:, 144:152], cols[:, 0:8], cols[:, 0:8], ALU.subtract))
                link(V.tensor_tensor(small[:, 152:160], small[:, 136:144], cols[:, 0:8], ALU.subtract))
                for l in range(DEPTH):
                    lb = small[:, 144 + 8 * l:152 + 8 * l]
                    link(V.tensor_scalar(lbs[:, 0, l, :], lb, -1.0, 1.0, ALU.mult, ALU.add))
                    link(V.tensor_scalar(lbs[:, 1, l, :], lb, 1e-30, None, ALU.max))

            for l in range(DEPTH):
                normalise(l)
                if l == 0:
                    dve.wait_ge(s_head, 3 * 16)
                for tt in range(NT):
                    turned(l, 0, tt)
                if l == 0:
                    dve.wait_ge(s_const, 16 * 5)
                    for half in range(2):
                        m = V.tensor_copy(gains2[:, :, 4 * half:4 * half + 4], gains[:, DEPTH:, half::2])
                    link(m)
                    lower_bounds()
                rope(l)
                qk_in(l)
                silu_unit(l, 3)
                silu_unit(l, 4)
                sink_max(l, 0)
                prob_in(l, 0)
                forget(l, 0)
                for g in range(4):
                    if g < 3:
                        sink_max(l, g + 1)
                    cumulate(l, g)
                    if g < 3:
                        prob_in(l, g + 1)
                    ya_in(l, g)
                    if g < 3:
                        forget(l, g + 1)
                q_sub(l)
                kend_in(l)
                q_in(l)
                silu_unit(l, 11)
                silu_unit(l, 12)
                ek_in(l, 0)
                for n in range(8):
                    at_in(l, n)
                    if n < 7:
                        ek_in(l, n + 1)
                    if n == 4:
                        y_ready(l, 0)
                    if n == 5:
                        yT_in(l, 0)
                y_ready(l, 1)
                yT_in(l, 1)
                for i in range(4):
                    merge(l, i)
                mix_and_normalise(l)
                route(l)
                inc(select(0, 0), "sel_in")
                weights(l)
                wait(dve, "rows_turned", l, 1)
                inc(tokens_in(l, 0), "hs_in")
                for e in range(2):
                    expert(l, e, e, link, first=(e == 0), second=(e == 1))
                over_table(l)
                per = 6
                base = step[0]
                with dve.Fori(1, NE // 2 - 1) as i:
                    done = [0]

                    def own(ins):
                        done[0] += 1
                        ins.then_inc(s_dve, 1)
                        dve.wait_ge(s_dve, i * per + (base - per + done[0]))

                    for b in range(2):
                        expert(l, i * 2 + b, b, own)
                    assert done[0] == per
                step[0] += per * (NE // 2 - 2)
                for e in range(NE - 2, NE):
                    expert(l, e, e % 2, link, last=(e == NE - 1))

                ov = OV[l]
                over = dve.value_load(ctl[0:1, 0:1], min_val=0, max_val=MAX_OVER)
                wait(dve, "sum_mm", l, NE - 1)
                s_own = s_ov[l]
                with dve.If(over > 0):
                    with dve.Fori(0, MAX_OVER) as j:
                        with dve.If(j < over):
                            e = dve.value_load(ctl[0:1, bass.ds(j + 1, 1)], min_val=0, max_val=NE - 1)
                            done = [0]

                            def own(ins):
                                done[0] += 1
                                ins.then_inc(s_own, 1)
                                dve.wait_ge(s_own, j * 4 + done[0])

                            own(select(0, e, ooff[:, bass.ds(j, 1)]))
                            weigh(0, e).then_inc(ov["selw"], 1)
                            dve.sem_inc(ov["sel"], 1)
                            dve.wait_ge(ov["rows_turned"], j + 1)
                            tokens_in(l, 0).then_inc(ov["hs"], 1)
                            dve.wait_ge(ov["seen"], j + 1)
                            dve.wait_ge(ov["sel_turned"], j + 1)
                            hidden(0, own).then_inc(ov["hid"], 1)
                        with dve.Else():
                            dve.nop()
                with dve.Else():
                    dve.nop()

                for q in range(4):
                    wait(dve, "sum_last", l, q + 1)
                    xs = x[:, :, 256 * q:256 * q + 256]
                    inc(V.tensor_tensor(xs, xs, SUMS[q][:, :].rearrange("p (t n) -> p t n", t=NT), ALU.add), "x_done")
            inverse_root(DEPTH, 1, 0, NT, D)
            dve.wait_ge(s_fin, 16)
            for tt in range(NT):
                inc(V.scalar_tensor_tensor(out=xn[:, tt, :], in0=x[:, tt, :], scalar=rstd[:, tt:tt + 1], in1=fin_g,
                                           op0=ALU.mult, op1=ALU.mult), "xn_in")

        @block.gpsimd
        def _(pool):
            for l in range(DEPTH):
                if l > 0:
                    wait(pool, "x_done", l - 1, 4)
                for ap in (bd[:, 0, :, 0:1], bd[:, 1, :, P:P + 1], ek[:, :, :, :]):
                    m = pool.memset(ap, 0.0)
                inc(m, "cleared")
                wait(pool, "unit_mm", l, 1)
                for i, src in enumerate([t["w_router_group"][l].rearrange("(p c) g -> p c g", c=KC)] +
                                        [t["w_router_expert"][l, g].rearrange("(p c) e -> p c e", c=KC)
                                         for g in range(GROUPS)]):
                    a = 0 if i == 0 else GROUPS + EPG * (i - 1)
                    n = GROUPS if i == 0 else EPG
                    pool.dma_start(wr[:, :, a:a + n], src).then_inc(s_wr, 16)
            wait(pool, "logit_mm", DEPTH - 1, 1)
            pool.dma_start(fin_g, t["final_norm_g"].rearrange("(o n) -> o n", o=1).broadcast_to([P, D])).then_inc(s_fin, 16)


TOKEN_UNITS = (0, 1, 2, 9, 10, 11, 12)
SIGMOID_UNITS = (3, 4, 5, 6, 7, 8, 11, 12, 13, 14, 15, 16, 17, 18, 19, 20)
Z_UNITS = (5, 6, 7, 8)
DVE_UNITS = (3, 4, 11, 12)

_INS = ["x", "attn_norm_g", "w_in", "sink_logits", "hgrn_lb_table", "hgrn_norm_g", "w_up_attn", "w_up_hgrn",
        "w_out", "ffn_norm_g", "w_router_group", "b_router_group", "w_router_expert", "b_router_expert",
        "w_expert_gate", "w_expert_up", "w_expert_down", "final_norm_g"]


def kernel(**inputs):
    import concourse.bacc as _bacc
    from concourse.bass_utils import run_bass_kernel_spmd as _run

    nc = _bacc.Bacc("TRN2", target_bir_lowering=False, num_devices=1)
    arrays = {f"in_{n}": np.ascontiguousarray(inputs[n]) for n in _INS}
    arrays["in_consts"] = constants()
    t = {}
    for n, a in arrays.items():
        t[n[3:]] = nc.dram_tensor(n, a.shape, mybir.dt.from_np(a.dtype), kind="ExternalInput").ap()
    t["out"] = nc.dram_tensor("result", (1, S, D), F32, kind="ExternalOutput").ap()
    layers_program(nc, t)
    r = _run(nc, [arrays], core_ids=[0])
    return r.results[0]["result"]
```
